# Optimizing a Trainium2 kernel written in Bass

```python
import math
import jax, jax.numpy as jnp
from jax import lax
import numpy as np

D_MODEL = 1024
BATCH = 1
SEQ = 256
DEPTH = 2

N_A_LAYERS = DEPTH // 2
N_B_LAYERS = DEPTH - N_A_LAYERS
N_EVEN = (DEPTH + 1) // 2
N_ODD = DEPTH // 2
CONV_WIDTH = 31
N_HEADS = 16
HEAD_DIM = D_MODEL // N_HEADS
DILATED_GROUPS = ((128, 1), (512, 4), (2048, 16))
N_GROUPS = len(DILATED_GROUPS)
Q_WIDTH = N_GROUPS * N_HEADS * HEAD_DIM
BLK = 128
N_BUCKETS = 32
MAX_DISTANCE = 2048
D_FF = 2752
N_EXPERTS = 8
TOP_K = 2
D_FF_EXPERT = 3584
EPS = 1e-6
NEG = -1e30

kernel_name = "yoco_conformer_dilated_moe_trunk"

def rmsnorm(x, g):
    xf = x.astype(jnp.float32)
    y = xf * lax.rsqrt(jnp.mean(xf * xf, axis=-1, keepdims=True) + EPS)
    return (y * g.astype(jnp.float32)).astype(x.dtype)

def layernorm(x, g, b):
    xf = x.astype(jnp.float32)
    mu = jnp.mean(xf, axis=-1, keepdims=True)
    var = jnp.mean(jnp.square(xf - mu), axis=-1, keepdims=True)
    y = (xf - mu) * lax.rsqrt(var + EPS)
    return (y * g.astype(jnp.float32) + b.astype(jnp.float32)).astype(x.dtype)

def swiglu(h, w_gate, w_up, w_down):
    return (jax.nn.silu(h @ w_gate) * (h @ w_up)) @ w_down

def t5_bucket(dist):
    n = np.asarray(dist)
    max_exact = N_BUCKETS // 2
    large = max_exact + (np.log(np.maximum(n, 1) / max_exact)
                         / np.log(MAX_DISTANCE / max_exact)
                         * (N_BUCKETS - max_exact)).astype(np.int32)
    large = np.minimum(large, N_BUCKETS - 1)
    return np.where(n < max_exact, n, large).astype(np.int32)

def make_band_bias(rel_bias, g):
    window, d = DILATED_GROUPS[g]
    span = window // d
    sub = BLK + np.arange(BLK)[:, None] - np.arange(2 * BLK)[None, :]
    in_band = (sub >= 0) & (sub <= span)
    bucket = t5_bucket(np.clip(sub, 0, span) * d)
    table_g = rel_bias[:, g * N_HEADS:(g + 1) * N_HEADS]
    bias = jnp.transpose(table_g[bucket], (2, 0, 1)).astype(jnp.float32)
    return jnp.where(jnp.asarray(in_band), bias, NEG)

def to_residue_layout(t, d):
    b, s = t.shape[0], t.shape[1]
    p = -(-s // (d * BLK)) * d * BLK
    t = jnp.pad(t, ((0, 0), (0, p - s)) + ((0, 0),) * (t.ndim - 2))
    t = t.reshape((b, p // d, d) + t.shape[2:])
    return jnp.swapaxes(t, 1, 2)

def from_residue_layout(t, s):
    b, d, l = t.shape[0], t.shape[1], t.shape[2]
    t = jnp.swapaxes(t, 1, 2)
    return t.reshape((b, l * d) + t.shape[3:])[:, :s]

def conv_module(x, norm_g, w_in, b_in, dw_w, dw_b, ln_g, ln_b, w_out, b_out):
    h = rmsnorm(x, norm_g)
    u = h @ w_in + b_in
    a, gate = jnp.split(u, 2, axis=-1)
    u = a * jax.nn.sigmoid(gate)
    u = lax.conv_general_dilated(u, dw_w[:, None, :], window_strides=(1,),
                                 padding=[(CONV_WIDTH - 1, 0)],
                                 dimension_numbers=('NWC', 'WIO', 'NWC'),
                                 feature_group_count=D_MODEL) + dw_b
    u = jax.nn.silu(layernorm(u, ln_g, ln_b))
    return u @ w_out + b_out

def shared_kv(x, kv_norm, w_kv, k_norm):
    b, s, _ = x.shape
    h = rmsnorm(x, kv_norm)
    kv = (h @ w_kv).reshape(b, s, 2, N_GROUPS, N_HEADS, HEAD_DIM)
    k = rmsnorm(kv[:, :, 0], k_norm[:, None, :])
    v = kv[:, :, 1]
    ks, vs = [], []
    for g, (_, d) in enumerate(DILATED_GROUPS):
        pad = ((0, 0), (0, 0), (BLK, 0), (0, 0), (0, 0))
        ks.append(jnp.pad(to_residue_layout(k[:, :, g], d), pad))
        vs.append(jnp.pad(to_residue_layout(v[:, :, g], d), pad))
    return ks, vs

def dilated_branch(q, k_res, v_res, band_bias, d):
    s = q.shape[1]
    q_res = to_residue_layout(q, d)
    b, _, l = q_res.shape[0], q_res.shape[1], q_res.shape[2]
    nb = l // BLK
    scale = HEAD_DIM ** -0.5

    def block(i):
        qb = lax.dynamic_slice_in_dim(q_res, i * BLK, BLK, axis=2).astype(jnp.float32)
        kb = lax.dynamic_slice_in_dim(k_res, i * BLK, 2 * BLK, axis=2).astype(jnp.float32)
        vb = lax.dynamic_slice_in_dim(v_res, i * BLK, 2 * BLK, axis=2).astype(jnp.float32)
        sc = jnp.einsum('brqhd,brkhd->brhqk', qb, kb) * scale + band_bias
        key_ok = (i * BLK - BLK + jnp.arange(2 * BLK)) >= 0
        sc = jnp.where(key_ok, sc, NEG)
        m = jnp.max(sc, axis=-1, keepdims=True)
        p = jnp.exp(sc - m)
        den = jnp.sum(p, axis=-1, keepdims=True)
        o = jnp.einsum('brhqk,brkhd->brqhd', p, vb) / jnp.swapaxes(den, 2, 3)
        lse = jnp.swapaxes((m + jnp.log(den))[..., 0], 2, 3)
        return o, lse

    o, lse = lax.map(block, jnp.arange(nb))
    o = jnp.moveaxis(o, 0, 2).reshape(b, d, l, N_HEADS, HEAD_DIM)
    lse = jnp.moveaxis(lse, 0, 2).reshape(b, d, l, N_HEADS)
    return from_residue_layout(o, s), from_residue_layout(lse, s)

def dilated_attention(x, norm_g, w_q, q_norm, w_o, ks, vs, band_biases):
    b, s, _ = x.shape
    h = rmsnorm(x, norm_g)
    q = (h @ w_q).reshape(b, s, N_GROUPS, N_HEADS, HEAD_DIM)
    q = rmsnorm(q, q_norm[:, None, :])
    outs, lses = [], []
    for g, (_, d) in enumerate(DILATED_GROUPS):
        o_g, lse_g = dilated_branch(q[:, :, g], ks[g], vs[g], band_biases[g], d)
        outs.append(o_g)
        lses.append(lse_g)
    wgt = jax.nn.softmax(jnp.stack(lses, axis=-1), axis=-1)
    o = jnp.einsum('bshg,bshgd->bshd', wgt, jnp.stack(outs, axis=3))
    return o.reshape(b, s, N_HEADS * HEAD_DIM).astype(x.dtype) @ w_o

def moe_ffn(x, norm_g, w_router, w_gate, w_up, w_down):
    h = rmsnorm(x, norm_g).reshape(-1, D_MODEL)
    logits = (h @ w_router).astype(jnp.float32)
    top_val, top_idx = lax.top_k(logits, TOP_K)
    gates = jax.nn.softmax(top_val, axis=-1)
    combine = jnp.sum(jax.nn.one_hot(top_idx, N_EXPERTS, dtype=jnp.float32)
                      * gates[..., None], axis=1)
    y = jnp.zeros(h.shape, jnp.float32)
    for e in range(N_EXPERTS):
        y = y + combine[:, e:e + 1] * swiglu(h, w_gate[e], w_up[e], w_down[e]).astype(jnp.float32)
    return y.astype(x.dtype).reshape(x.shape)

def setup_inputs(seed: int = 0) -> dict:
    key = jax.random.key(seed)
    ks = jax.random.split(key, 32)

    def nrm(k, shape, scale):
        return jax.random.normal(k, shape, jnp.float32) * scale

    def gain(k, shape):
        return 1.0 + 0.02 * jax.random.normal(k, shape, jnp.float32)

    D = D_MODEL
    return {
        "x": nrm(ks[0], (BATCH, SEQ, D), 1.0),
        "rel_bias": nrm(ks[1], (N_BUCKETS, N_GROUPS * N_HEADS), 0.5),
        "conv_norm": gain(ks[2], (N_A_LAYERS, D)),
        "conv_w_in": nrm(ks[3], (N_A_LAYERS, D, 2 * D), D ** -0.5),
        "conv_b_in": nrm(ks[4], (N_A_LAYERS, 2 * D), 0.02),
        "conv_dw_w": nrm(ks[5], (N_A_LAYERS, CONV_WIDTH, D), CONV_WIDTH ** -0.5),
        "conv_dw_b": nrm(ks[6], (N_A_LAYERS, D), 0.02),
        "conv_ln_g": gain(ks[7], (N_A_LAYERS, D)),
        "conv_ln_b": nrm(ks[8], (N_A_LAYERS, D), 0.02),
        "conv_w_out": nrm(ks[9], (N_A_LAYERS, D, D), D ** -0.5),
        "conv_b_out": nrm(ks[10], (N_A_LAYERS, D), 0.02),
        "kv_norm": gain(ks[11], (D,)),
        "w_kv": nrm(ks[12], (D, 2 * Q_WIDTH), D ** -0.5),
        "k_norm": gain(ks[13], (N_GROUPS, HEAD_DIM)),
        "attn_norm": gain(ks[14], (N_B_LAYERS, D)),
        "w_q": nrm(ks[15], (N_B_LAYERS, D, Q_WIDTH), D ** -0.5),
        "q_norm": gain(ks[16], (N_B_LAYERS, N_GROUPS, HEAD_DIM)),
        "w_o": nrm(ks[17], (N_B_LAYERS, N_HEADS * HEAD_DIM, D), (N_HEADS * HEAD_DIM) ** -0.5),
        "ffn_norm": gain(ks[18], (DEPTH, D)),
        "ffn_w_gate": nrm(ks[19], (N_EVEN, D, D_FF), D ** -0.5),
        "ffn_w_up": nrm(ks[20], (N_EVEN, D, D_FF), D ** -0.5),
        "ffn_w_down": nrm(ks[21], (N_EVEN, D_FF, D), D_FF ** -0.5),
        "moe_router": nrm(ks[22], (N_ODD, D, N_EXPERTS), D ** -0.5),
        "moe_w_gate": nrm(ks[23], (N_ODD, N_EXPERTS, D, D_FF_EXPERT), D ** -0.5),
        "moe_w_up": nrm(ks[24], (N_ODD, N_EXPERTS, D, D_FF_EXPERT), D ** -0.5),
        "moe_w_down": nrm(ks[25], (N_ODD, N_EXPERTS, D_FF_EXPERT, D), D_FF_EXPERT ** -0.5),
    }

def reference(x, rel_bias, conv_norm, conv_w_in, conv_b_in, conv_dw_w, conv_dw_b,
              conv_ln_g, conv_ln_b, conv_w_out, conv_b_out, kv_norm, w_kv, k_norm,
              attn_norm, w_q, q_norm, w_o, ffn_norm, ffn_w_gate, ffn_w_up, ffn_w_down,
              moe_router, moe_w_gate, moe_w_up, moe_w_down):
    band_biases = [make_band_bias(rel_bias, g) for g in range(N_GROUPS)]
    ks, vs = None, None
    for l in range(DEPTH):
        if l == N_A_LAYERS:
            ks, vs = shared_kv(x, kv_norm, w_kv, k_norm)
        if l < N_A_LAYERS:
            x = x + conv_module(x, conv_norm[l], conv_w_in[l], conv_b_in[l], conv_dw_w[l],
                                conv_dw_b[l], conv_ln_g[l], conv_ln_b[l], conv_w_out[l],
                                conv_b_out[l])
        else:
            j = l - N_A_LAYERS
            x = x + dilated_attention(x, attn_norm[j], w_q[j], q_norm[j], w_o[j],
                                      ks, vs, band_biases)
        if l % 2 == 0:
            e = l // 2
            x = x + swiglu(rmsnorm(x, ffn_norm[l]), ffn_w_gate[e], ffn_w_up[e], ffn_w_down[e])
        else:
            e = l // 2
            x = x + moe_ffn(x, ffn_norm[l], moe_router[e], moe_w_gate[e], moe_w_up[e],
                            moe_w_down[e])
    return x


_drawn_inputs = setup_inputs


def setup_inputs(seed=0):
    import zlib

    import numpy as np

    out = dict(_drawn_inputs(seed))
    spreads = {}
    factors = {'kv_norm': 3.489, 'k_norm': 5.801, 'attn_norm': 4.078, 'q_norm': 4.17}
    for name, (base, spread) in spreads.items():
        noise = np.random.default_rng([zlib.crc32(name.encode()), seed]).standard_normal(out[name].shape)
        drawn = base * np.exp(spread * noise) if base else spread * noise
        out[name] = __import__('jax').numpy.asarray(drawn.astype(out[name].dtype))
    for name, factor in factors.items():
        out[name] = (out[name] * factor).astype(out[name].dtype)
    return out
```

```python
from contextlib import ExitStack
import math

import numpy as np
import concourse.bass as bass
from concourse import mybir

P = 128
D = 1024
SEQ = 256
NB = SEQ // P
KC = D // P
CONV = 31
HEADS = 16
DH = 64
GROUPS = ((128, 1), (512, 4), (2048, 16))
NG = len(GROUPS)
QW = NG * HEADS * DH
BUCKETS = 32
MAX_DISTANCE = 2048
FF = 2752
FF_COLS = 344
FF_CHUNKS = FF // FF_COLS
FF_KC = -(-FF // P)
FF_TAIL = FF - (FF_KC - 1) * P
NE = 8
FE = 3584
FE_CHUNKS = FE // 512
FE_KC = FE // P
EPS = 1e-6
NEG = -1e30
CONV_DVE = 4
DIAGS = 8
RING = 4
SLAB = 2048
BW = 384
COPIES = 64

S_WIN = 0
S_WOUT = S_WIN + 8
S_FFN = S_WOUT + 4
S_DOWN = S_FFN + 4 * FF_CHUNKS
S_KVQ = S_DOWN + FF_KC // 2
S_WO = S_KVQ + 2 * 18
S_END = S_WO + 4
BASE = [(S_END - s + RING - 1) // RING for s in range(RING)]
PER_JOB = [11, 11, 10, 10]
MAX_JOBS = NE + 4


def host_constants():
    ident = np.eye(P, dtype=np.float32)
    before = np.triu(np.ones((P, P), np.float32), 1)
    iota = np.tile(np.arange(P, dtype=np.float32), (P, 1))
    dist = 255 - np.arange(BW)
    exact = BUCKETS // 2
    n = np.clip(dist, 0, None)
    large = exact + (np.log(np.maximum(n, 1) / exact) / np.log(MAX_DISTANCE / exact)
                     * (BUCKETS - exact)).astype(np.int32)
    bucket = np.where(n < exact, n, np.minimum(large, BUCKETS - 1))
    hot = (bucket[None, :] == np.arange(BUCKETS)[:, None])
    ok = np.zeros((NG, BW), bool)
    for g, (window, d) in enumerate(GROUPS):
        ok[g] = (dist >= 0) & (dist <= window) & (dist % d == 0) & (dist // d <= P)
    hots = np.zeros((BUCKETS, NG, BW), np.float32)
    mask = np.zeros((HEADS, NG, BW), np.float32)
    for g in range(NG):
        hots[:, g] = hot & ok[g][None, :]
        mask[:, g] = np.where(ok[g], 0.0, NEG)[None, :]
    return {"c_ident": ident, "c_before": before, "c_iota": iota,
            "c_hot": hots, "c_mask": mask}


def build(nc, a, out):
    f32, f32r, u32 = mybir.dt.float32, mybir.dt.float32r, mybir.dt.uint32
    i32 = mybir.dt.int32
    ALU, ACT, AX = mybir.AluOpType, mybir.ActivationFunctionType, mybir.AxisListType

    scratch_bias = nc.dram_tensor("bias_rows", (COPIES, HEADS, NG, BW), f32).ap()

    with ExitStack() as ctx:
        def sb(name, shape, dt=f32, where=ctx):
            return where.enter_context(nc.sbuf_tensor("sb_" + name, shape, dt))

        def sem(name):
            return ctx.enter_context(nc.semaphore(name))

        raw = sb("raw", [P, RING, SLAB])
        w_hi = sb("w_hi", [P, RING, SLAB], f32r)
        w_lo = sb("w_lo", [P, RING, SLAB], f32r)
        x = sb("x", [P, NB, D])
        xt_hi = sb("xt_hi", [P, KC, SEQ], f32r)
        xt_lo = sb("xt_lo", [P, KC, SEQ], f32r)
        ident = sb("ident", [P, P])
        small = sb("small", [P, 64])
        ss, ms, sd, rr = (small[:, 2 * i:2 * i + 2] for i in range(4))
        cols = sb("cols", [P, KC, 40])
        qk_gain = sb("qk_gain", [P, 8])
        ss16, ms16, sd16, rr16 = (sb(f"h16_{i}", [P, 2, 16]) for i in range(4))
        def phase():
            return ExitStack()

        with phase() as ph:
            z = sb("z", [P, NB, D], where=ph)
            vec_rows = sb("vec_rows", [40, D], where=ph)
            kq_rows = sb("kq_rows", [8, P], where=ph)
            bin_row = sb("bin_row", [1, 2 * D], where=ph)
            bout_row = sb("bout_row", [1, D], where=ph)
            ones_row = sb("ones_row", [1, P], where=ph)
            sig = sb("sig", [P, NB, 512], where=ph)
            u_tok = sb("u_tok", [P, NB, D], where=ph)
            u_t = sb("u_t", [P, KC, CONV - 1 + SEQ], where=ph)
            diag = sb("diag", [P, DIAGS, P], where=ph)
            conv_t = sb("conv_t", [P, KC, SEQ], where=ph)
            act_tmp = sb("act_tmp", [P, KC, SEQ], where=ph)
            bn = sb("bn", [P, NB, 2, 6], where=ph)
            hot_sb = sb("hot_sb", [BUCKETS, NG, BW], where=ph)
            rel_sb = sb("rel_sb", [BUCKETS, NG * HEADS], where=ph)
            mask_sb = sb("mask_sb", [HEADS, NG, BW], where=ph)
            bias_sb = sb("bias_sb", [HEADS, NG, BW], where=ph)
        with phase() as ph:
            z_b = sb("z_b", [P, NB, D], where=ph)
            silu_ff = sb("silu_ff", [P, NB, FF_COLS], where=ph)
            act_ff = sb("act_ff", [P, NB, FF], where=ph)
            actt_hi = sb("actt_hi", [P, FF_KC, SEQ], f32r, where=ph)
            actt_lo = sb("actt_lo", [P, FF_KC, SEQ], f32r, where=ph)
        with phase() as ph:
            z_c = sb("z_c", [P, NB, D], where=ph)
            k_t = sb("k_t", [P, NG * 4, SEQ], where=ph)
            q_t = sb("q_t", [P, NG * 4, SEQ], where=ph)
            v_tok = sb("v_tok", [P, NB, QW // 2], where=ph)
            kn = sb("kn", [P, NB, 512], where=ph)
            sq = sb("sq", [P, NB, 512], where=ph)
            bias_t = sb("bias_t", [P, 2, NG, SEQ], where=ph)
            scores = sb("scores", [P, 2, NG * SEQ], where=ph)
            probs_t = sb("probs_t", [P, 2, 2 * NG * P], where=ph)
            o_tok = sb("o_tok", [P, NB, D], where=ph)
        probs = [kn[:, :, :].rearrange("p b d -> p (b d)")[:, 0:NG * SEQ],
                 sq[:, :, :].rearrange("p b d -> p (b d)")[:, 0:NG * SEQ]]
        with phase() as ph:
            h_tok = sb("h_tok", [P, NB, D], where=ph)
            h_t = sb("h_t", [P, KC, SEQ], where=ph)
            gain_row = sb("gain_row", [P, D], where=ph)
            router = sb("router", [P, KC, NE], where=ph)
            xs_hi = sb("xs_hi", [P, KC, P], f32r, where=ph)
            xs_lo = sb("xs_lo", [P, KC, P], f32r, where=ph)
            silu_e = sb("silu_e", [P, 512], where=ph)
            act_e = sb("act_e", [P, 512], where=ph)
            aet_hi = sb("aet_hi", [P, FE_KC, P], f32r, where=ph)
            aet_lo = sb("aet_lo", [P, FE_KC, P], f32r, where=ph)
            y_e = sb("y_e", [P, D], where=ph)
            pick = sb("pick", [P, NB, P], where=ph)
            put = sb("put", [P, NB, P], where=ph)
            put_t = sb("put_t", [P, NB, P], where=ph)
            iota = sb("iota", [P, P], where=ph)
            before = sb("before", [P, P], where=ph)
            ones = sb("ones", [P, P], where=ph)
            logits = sb("logits", [P, NB, NE], where=ph)
            top = sb("top", [P, NB, 8], where=ph)
            top_i = sb("top_i", [P, NB, 8], u32, where=ph)
            top_f = sb("top_f", [P, NB, 8], where=ph)
            gate2 = sb("gate2", [P, NB, 8], where=ph)
            hot1 = sb("hot1", [P, NB, NE], where=ph)
            hot2 = sb("hot2", [P, NB, NE], where=ph)
            chosen = sb("chosen", [P, NB, NE], where=ph)
            rank = sb("rank", [P, NB, MAX_JOBS], where=ph)
            share = sb("share", [P, NB, MAX_JOBS], where=ph)
            over = sb("over", [P, 8, NE], where=ph)
            over_i = sb("over_i", [P, 8], i32, where=ph)
            rk_now = sb("rk_now", [P, NB], where=ph)
            sh_now = sb("sh_now", [P, NB], where=ph)

        acc = ctx.enter_context(nc.psum_tensor("acc", [P, 4, 512], f32))
        tb = ctx.enter_context(nc.psum_tensor("tb", [P, 4, 512], f32))

        raw_in = [sem(f"raw_in{s}") for s in range(RING)]
        hi_done = [sem(f"hi_done{s}") for s in range(RING)]
        lo_done = [sem(f"lo_done{s}") for s in range(RING)]
        slab_used = [sem(f"slab_used{s}") for s in range(RING)]
        x_in, consts_in, rows_in = sem("x_in"), sem("consts_in"), sem("rows_in")
        bias_in = sem("bias_in")
        tables_in = sem("tables_in")
        cols_tr, cols_done, gains_done = sem("cols_tr"), sem("cols_done"), sem("gains_done")
        bias_mm, bias_rows, bias_out = sem("bias_mm"), sem("bias_rows"), sem("bias_out")
        sq_done, ms_done, sd_done, z_done = sem("sq_done"), sem("ms_done"), sem("sd_done"), sem("z_done")
        xt_tr, xt_hi_done, xt_lo_done = sem("xt_tr"), sem("xt_hi_done"), sem("xt_lo_done")
        act_step, dve_step = sem("act_step"), sem("dve_step")
        pad_done = sem("pad_done")
        glu_sig, glu_u, glu_tr, glu_t = sem("glu_sig"), sem("glu_u"), sem("glu_tr"), sem("glu_t")
        diag_a, diag_p, diag_used, conv_mm, conv_out = (sem(n) for n in ("diag_a", "diag_p", "diag_used", "conv_mm", "conv_out"))
        conv_done, conv_tr, var_done, lnsd_done = sem("conv_done"), sem("conv_tr"), sem("var_done"), sem("lnsd_done")
        res_done = sem("res_done")
        ff_silu, ff_act = sem("ff_silu"), sem("ff_act")
        fft_tr, fft_hi, fft_lo = sem("fft_tr"), sem("fft_hi"), sem("fft_lo")
        pr_sq, pr_ms, pr_sd, pr_kn, pr_tr, pr_t = (sem(n) for n in
            ("pr_sq", "pr_ms", "pr_sd", "pr_kn", "pr_tr", "pr_t"))
        bias_t_in = [sem("bias_t_in0"), sem("bias_t_in1")]
        at_qk, at_max, at_exp, at_tr, at_ta, at_tv, at_pv, at_o = (sem(n) for n in
            ("at_qk", "at_max", "at_exp", "at_tr", "at_ta", "at_tv", "at_pv", "at_o"))
        rt_mm, rt_v, rt_e, rt_rank_in, rt_rank, rt_done = (sem(n) for n in
            ("rt_mm", "rt_v", "rt_e", "rt_rank_in", "rt_rank", "rt_done"))
        ht_done = sem("ht_done")
        pick_done, put_done, rk_sem, sh_sem = sem("pick_done"), sem("put_done"), sem("rank_taken"), sem("share_taken")
        gather_mm, xs_hi_done, xs_lo_done = sem("gather_mm"), sem("xs_hi_done"), sem("xs_lo_done")
        e_silu, e_act = sem("e_silu"), sem("e_act")
        et_tr, et_hi, et_lo = sem("et_tr"), sem("et_hi"), sem("et_lo")
        put_tr, put_t_done = sem("put_tr"), sem("put_t_done")
        y_done, sc_mm, sum_done = sem("y_done"), sem("sc_mm"), sem("sum_done")
        out_done = sem("out_done")

        C_DWB, C_CN, C_LG, C_LB, C_KVN, C_AN, C_F0 = range(CONV, CONV + 7)
        NCOL = CONV + 7


        def wait_slab(eng, i):
            eng.wait_ge(slab_used[i % RING], i // RING + 1)

        def wait_expert_slab(eng, s, j, n):
            eng.wait_ge(slab_used[s], BASE[s] + j * PER_JOB[s] + n)

        PE_TAPS = [(k, t) for k in range(CONV_DVE, KC) for t in range(CONV)]

        def slab_view(t, s, k, n):
            return t[:, s, 0:k * n].rearrange("p (k n) -> p k n", k=k)

        def w_src(w, k0, k, c0, n):
            return w[k0 * P:(k0 + k) * P, c0:c0 + n].rearrange("(k p) n -> p k n", p=P)

        def fixed_slabs():
            w_in, w_out = a["conv_w_in"][0], a["conv_w_out"][0]
            for c in range(2):
                for half in range(2):
                    for kh in range(2):
                        yield w_src(w_in, 4 * kh, 4, D * half + 512 * c, 512), 4, 512
            for c in range(2):
                for kh in range(2):
                    yield w_src(w_out, 4 * kh, 4, 512 * c, 512), 4, 512
            for c in range(FF_CHUNKS):
                for w in (a["ffn_w_gate"][0], a["ffn_w_up"][0]):
                    for kh in range(2):
                        yield w_src(w, 4 * kh, 4, FF_COLS * c, FF_COLS), 4, FF_COLS
            for d in range(FF_KC // 2):
                yield (w_src(a["ffn_w_down"][0], 2 * d, 2, 0, D) if d < FF_KC // 2 - 1 else None), 2, D
            for half in range(2):
                for w, c0 in ((a["w_kv"], 0), (a["w_kv"], QW), (a["w_q"][0], 0)):
                    for g in range(NG):
                        for kh in range(2):
                            yield w_src(w, 4 * kh, 4, c0 + g * D + 512 * half, 512), 4, 512
            for c in range(2):
                for kh in range(2):
                    yield w_src(a["w_o"][0], 4 * kh, 4, 512 * c, 512), 4, 512

        n_over_ap = over_i[0:1, 4:5]

        def job_loops(eng, body, after_routing):
            with eng.Fori(0, NE) as j:
                body(j, j)
            eng.wait_ge(rt_done, 1)
            n_over = eng.value_load(n_over_ap, min_val=0, max_val=3)
            with eng.If(n_over > 0):
                with eng.Fori(0, n_over) as k:
                    body(k + NE, k)
            return n_over + NE

        block = ctx.enter_context(nc.Block())

        def use_bytes(s, use):
            i = S_DOWN + FF_KC // 2 - 1
            if isinstance(use, int):
                extra = 16 if (s == i % RING and use >= i // RING) else 0
                return 16 * (use + 1) + extra
            return use * 16 + (16 + (16 if s == i % RING else 0))

        @block.sync
        def _(sp):
            sp.dma_start(x[:, :, :], a["x"][0].rearrange("(b p) d -> p b d", p=P)).then_inc(x_in, 16)
            slabs = list(fixed_slabs())
            assert len(slabs) == S_END

            def load(i):
                s, use = i % RING, i // RING
                src, k, n = slabs[i]
                if use:
                    sp.wait_ge(lo_done[s], use)
                if src is None:
                    w = a["ffn_w_down"][0]
                    k0 = FF_KC - 2
                    sp.dma_start(raw[:, s, 0:D], w[k0 * P:(k0 + 1) * P, :]).then_inc(raw_in[s], 16)
                    sp.dma_start(raw[0:FF_TAIL, s, D:2 * D], w[(k0 + 1) * P:FF, :]).then_inc(raw_in[s], 16)
                else:
                    sp.dma_start(slab_view(raw, s, k, n), src).then_inc(raw_in[s], 16)

            for i in range(4):
                load(i)
            for i in range(4, S_FFN):
                load(i)
            sp.wait_ge(bias_rows, 1)
            sp.dma_start(scratch_bias.rearrange("c h g w -> h c (g w)"),
                         bias_sb[:, :, :].rearrange("h g w -> h (g w)").unsqueeze(1).to_broadcast([HEADS, COPIES, NG * BW])).then_inc(bias_out, 16)
            for i in range(S_FFN, S_KVQ + 18):
                load(i)
            sp.wait_ge(bias_out, 16)

            def load_bias(h):
                if h >= 2:
                    sp.wait_ge(at_max, 2 * (h - 1))
                for top_row in range(0, P, COPIES):
                    src = bass.AP(scratch_bias.tensor, h * NG * BW + P - 1 - top_row,
                                  [[HEADS * NG * BW - 1, COPIES], [BW, NG], [1, SEQ]])
                    sp.dma_start(bias_t[top_row:top_row + COPIES, h % 2, :, :], src).then_inc(bias_t_in[h % 2], 16)

            sp.wait_ge(res_done, 5 + 0)
            load_bias(0)
            load_bias(1)
            for i in range(S_KVQ + 18, S_KVQ + 26):
                load(i)
            for h in range(2, 8):
                load_bias(h)
            for i in range(S_KVQ + 26, S_WO):
                load(i)
            load_bias(8)
            load_bias(9)
            for i in range(S_WO, S_END):
                load(i)

            def load_expert_slab(s, use, src, k, n):
                sp.wait_ge(lo_done[s], use)
                sp.dma_start(slab_view(raw, s, k, n), src).then_inc(raw_in[s], 16)

            for h in range(10, HEADS):
                load_bias(h)
            sp.wait_ge(res_done, 7)
            sp.dma_start(gain_row[:, :], a["ffn_norm"][1:2].to_broadcast([P, D])).then_inc(tables_in, 16)
            sp.dma_start(router[:, :, :], a["moe_router"][0].rearrange("(k p) e -> p k e", p=P)).then_inc(tables_in, 16)
            sp.dma_start(iota[:, :], a["c_iota"]).then_inc(tables_in, 16)
            sp.dma_start(before[:, :], a["c_before"]).then_inc(tables_in, 16)

            def job(j, expert):
                wg, wu, wd = (a[n][0, bass.ds(expert, 1)].rearrange("o k n -> (o k) n") for n in ("moe_w_gate", "moe_w_up", "moe_w_down"))
                with sp.Fori(0, FE_CHUNKS) as c:
                    for q, (w, kh) in enumerate(((wg, 0), (wg, 1), (wu, 0), (wu, 1))):
                        s = q
                        load_expert_slab(s, BASE[s] + j * PER_JOB[s] + c,
                                         w[kh * 512:(kh + 1) * 512, bass.ds(c * 512, 512)].rearrange("(k p) n -> p k n", p=P), 4, 512)
                for d in range(FE_KC // 2):
                    s = d % RING
                    load_expert_slab(s, j * PER_JOB[s] + (BASE[s] + FE_CHUNKS + d // RING), wd[2 * d * P:(2 * d + 2) * P, :].rearrange("(k p) n -> p k n", p=P), 2, D)

            with sp.Fori(0, NE) as j:
                job(j, j)
            sp.wait_ge(rt_done, 1)
            n_over = sp.value_load(over_i[0:1, 4:5], min_val=0, max_val=3)
            with sp.If(n_over > 0):
                with sp.Fori(0, n_over) as k:
                    expert = sp.value_load(over_i[0:1, bass.ds(k, 1)], min_val=0, max_val=NE - 1)
                    job(k + NE, expert)
            sp.wait_ge(sum_done, n_over + (NE + 2))
            sp.dma_start(out[0].rearrange("(b p) d -> p b d", p=P), x[:, :, :]).then_inc(out_done, 16)
            sp.wait_ge(out_done, 16)

        E_CONV_IN, E_CONV_OUT, E_FFN, E_KV, E_Q, E_KV2, E_Q2, E_O = range(8)
        nu = HEADS

        @block.tensor
        def _(pe):
            def transpose(o, i):
                n = i.shape[0]
                return nc.tensor.transpose(o, i, ident[0:n, 0:n])

            def three(o, hi_x, lo_x, hi_w, lo_w, start, stop):
                nc.tensor.matmul(o, hi_x, hi_w, start=start, stop=False)
                nc.tensor.matmul(o, hi_x, lo_w, start=False, stop=False)
                return nc.tensor.matmul(o, lo_x, hi_w, start=False, stop=stop)

            def slab_mm(i, k0, k, n, first, last, outs, xh=xt_hi, xl=xt_lo, rows=None):
                s, use = i % RING, i // RING
                pe.wait_ge(lo_done[s], use + 1)
                wh, wl = slab_view(w_hi, s, k, n), slab_view(w_lo, s, k, n)
                for kk in range(k):
                    r = slice(0, P if rows is None else rows[kk])
                    for tok, col, o in outs:
                        ins = three(o, xh[r, k0 + kk, tok], xl[r, k0 + kk, tok], wh[r, kk, col], wl[r, kk, col],
                                    first and kk == 0, last and kk == k - 1)
                ins.then_inc(slab_used[s], 1)
                return ins

            def blocks(bank, n):
                return [(slice(P * b, P * b + P), slice(0, n), acc[:, bank + b, 0:n]) for b in range(NB)]

            def to_xt(event, src):
                if event:
                    pe.wait_ge(xt_lo_done, 4 * event)
                pe.wait_ge(z_done, event + 1)
                for pair in range(4):
                    for kk in range(2):
                        for b in range(NB):
                            k = 2 * pair + kk
                            ins = transpose(tb[:, pair, kk * SEQ + b * P:kk * SEQ + b * P + P], src[:, b, k * P:k * P + P])
                    ins.then_inc(xt_tr, 1)

            pe.sem_inc(et_tr, 1)
            pe.wait_ge(consts_in, 16)
            pe.wait_ge(rows_in, 16 * 12)
            for k in range(KC):
                transpose(acc[:, 0, k * 40:k * 40 + NCOL], vec_rows[0:NCOL, k * P:k * P + P])
            transpose(acc[:, 1, 0:2 * NG], kq_rows[0:2 * NG, :]).then_inc(cols_tr, 1)

            to_xt(E_CONV_IN, z)
            pe.wait_ge(cols_done, 1)
            pe.wait_ge(gains_done, 1)
            pe.wait_ge(bias_in, 32)
            pe.wait_ge(pad_done, 2)
            for c in range(2):
                if c:
                    pe.wait_ge(glu_u, c)
                for half in range(2):
                    for b in range(NB):
                        nc.tensor.matmul(acc[:, 2 * half + b, :], ones_row[0:1, :],
                                         bin_row[0:1, half * D + c * 512:half * D + c * 512 + 512], start=True, stop=False)
                    for kh in range(2):
                        if c == 0 and half == 0:
                            pe.wait_ge(xt_lo_done, 4 * E_CONV_IN + 2 * kh + 2)
                        ins = slab_mm(S_WIN + 4 * c + 2 * half + kh, 4 * kh, 4, 512, False, kh == 1, blocks(2 * half, 512))
                pe.wait_ge(glu_u, c + 1)
                for pair in range(2):
                    for kk in range(2):
                        for b in range(NB):
                            k = 4 * c + 2 * pair + kk
                            ins = transpose(tb[:, 2 * c + pair, kk * SEQ + b * P:kk * SEQ + b * P + P], u_tok[:, b, k * P:k * P + P])
                    ins.then_inc(glu_tr, 1)
            pe.wait_ge(glu_t, 4)
            for n, (k, t) in enumerate(PE_TAPS):
                pe.wait_ge(diag_p if n % 2 else diag_a, n // 2 + 1)
                ins = nc.tensor.matmul(acc[:, k - CONV_DVE, 0:SEQ], diag[:, n % DIAGS, :], u_t[:, k, t:t + SEQ],
                                       start=t == 0, stop=t == CONV - 1)
                ins.then_inc(diag_used, 1)
                if t == CONV - 1:
                    pe.wait_ge(diag_used, n + 1)
                    pe.sem_inc(conv_mm, 1)
            pe.wait_ge(conv_out, KC - CONV_DVE)
            pe.wait_ge(tables_in, 48)
            for g in range(NG):
                ins = nc.tensor.matmul(acc[0:HEADS, g, 0:BW], rel_sb[:, g * HEADS:(g + 1) * HEADS], hot_sb[:, g, :],
                                       start=True, stop=True)
            ins.then_inc(bias_mm, 1)
            pe.wait_ge(conv_done, CONV * CONV_DVE)
            for b in range(NB):
                for k in range(KC):
                    ins = transpose(tb[:, 2 * b + k // 4, (k % 4) * P:(k % 4) * P + P], conv_t[:, k, b * P:b * P + P])
            ins.then_inc(conv_tr, 1)
            to_xt(E_CONV_OUT, z)
            pe.wait_ge(bias_rows, 1)

            def residual_product(s0, event, n0, bias_row=None):
                pe.wait_ge(xt_lo_done, 4 * event + 2)
                for c in range(2):
                    if bias_row is not None:
                        for b in range(NB):
                            nc.tensor.matmul(acc[:, 2 * c + b, :], ones_row[0:1, :], bias_row[0:1, c * 512:c * 512 + 512],
                                             start=True, stop=False)
                    for kh in range(2):
                        if c == 0 and kh:
                            pe.wait_ge(xt_lo_done, 4 * (event + 1))
                        ins = slab_mm(s0 + 2 * c + kh, 4 * kh, 4, 512, bias_row is None and kh == 0, kh == 1, blocks(2 * c, 512))

            residual_product(S_WOUT, E_CONV_OUT, 0, bout_row)

            pe.wait_ge(res_done, 2)
            to_xt(E_FFN, z_b)
            for c in range(FF_CHUNKS):
                i = S_FFN + 4 * c
                if c:
                    pe.wait_ge(ff_silu, c)
                for kh in range(2):
                    if c == 0:
                        pe.wait_ge(xt_lo_done, 4 * E_FFN + 2 * kh + 2)
                    slab_mm(i + kh, 4 * kh, 4, FF_COLS, kh == 0, kh == 1, blocks(0, FF_COLS))
                if c:
                    pe.wait_ge(ff_act, c)
                for kh in range(2):
                    slab_mm(i + 2 + kh, 4 * kh, 4, FF_COLS, kh == 0, kh == 1, blocks(2, FF_COLS))
            pe.wait_ge(ff_act, FF_CHUNKS)

            def ff_transposes(d):
                if d >= 4:
                    pe.wait_ge(fft_lo, d - 3)
                for kk in range(2):
                    k = 2 * d + kk
                    n = min(P, FF - k * P)
                    for b in range(NB):
                        ins = transpose(tb[0:n, d % 4, kk * SEQ + b * P:kk * SEQ + b * P + P], act_ff[:, b, k * P:k * P + n])
                ins.then_inc(fft_tr, 1)

            halves = [(slice(P * b, P * b + P), slice(512 * c, 512 * c + 512), acc[:, 2 * c + b, :]) for c in range(2) for b in range(NB)]
            n_down = FF_KC // 2
            for d in range(3):
                ff_transposes(d)
            for d in range(n_down):
                if d + 3 < n_down:
                    ff_transposes(d + 3)
                pe.wait_ge(fft_lo, d + 1)
                slab_mm(S_DOWN + d, 2 * d, 2, D, d == 0, d == n_down - 1, halves, actt_hi, actt_lo,
                        [P, P if d < n_down - 1 else FF_TAIL])

            pe.wait_ge(res_done, 4)

            def head_transposes(half, m):
                n = 6 * half + (m if m < 3 else m - 3)
                pe.wait_ge(pr_kn, n + 1)
                if n >= 2:
                    pe.wait_ge(pr_t, n - 1)
                for kk in range(4):
                    for b in range(NB):
                        ins = transpose(tb[:, 2 * (n % 2) + kk // 2, (kk % 2) * SEQ + b * P:(kk % 2) * SEQ + b * P + P],
                                        kn[:, b, kk * P:kk * P + P])
                ins.then_inc(pr_tr, 1)

            def project(half):
                for m in range(9):
                    mm = 9 * half + m
                    if m in (0, 6):
                        event = E_KV + 2 * half + (m == 6)
                        if m == 6:
                            pe.wait_ge(pr_t, 6 * half + 3)
                        to_xt(event, z_c)
                    if m >= 2:
                        if 3 <= m - 2 < 6:
                            pe.wait_ge(pr_sq, mm - 1)
                        else:
                            pe.wait_ge(pr_kn, 6 * half + (m - 2 if m < 5 else m - 5) + 1)
                    i = S_KVQ + 2 * mm
                    for kh in range(2):
                        if m in (0, 6):
                            pe.wait_ge(xt_lo_done, 4 * event + 2 * kh + 2)
                        slab_mm(i + kh, 4 * kh, 4, 512, kh == 0, kh == 1, blocks(2 * (mm % 2), 512))
                    if 1 <= m <= 3 or m >= 7:
                        head_transposes(half, m - 1)
                head_transposes(half, 8)

            def qk(n):
                h, b = (n // 2) % 8, n % 2
                if n >= 2:
                    pe.wait_ge(at_max, n - 1)
                half = slice(DH * (h % 2), DH * (h % 2) + DH)
                nk = P * (b + 1)
                for g in range(NG):
                    t = g * 4 + h // 2
                    o = acc[:, 2 * (n % 2) + g // 2, (g % 2) * SEQ:(g % 2) * SEQ + nk]
                    ins = nc.tensor.matmul(o, q_t[half, t, b * P:b * P + P], k_t[half, t, 0:nk], start=True, stop=True)
                ins.then_inc(at_qk, 1)

            def probs_transposes(n):
                h, b = (n // 2) % 8, n % 2
                pe.wait_ge(at_exp, n + 1)
                if n:
                    pe.wait_ge(at_ta, n)
                    pe.wait_ge(at_tv, n)
                nk = P * (b + 1)
                for q in range(NG * (b + 1)):
                    ins = transpose(tb[:, q // 4, (q % 4) * P:(q % 4) * P + P], probs[n % 2][:, q * P:q * P + P])
                ins.then_inc(at_tr, 1)

            def pv(n):
                h, b = (n // 2) % 8, n % 2
                pe.wait_ge(at_ta, n + 1)
                pe.wait_ge(at_tv, n + 1)
                if n >= 2:
                    pe.wait_ge(at_o, n - 1)
                nq = NG * (b + 1)
                for q in range(nq):
                    g, kb = q // (b + 1), q % (b + 1)
                    c0 = g * 512 + h * DH
                    ins = nc.tensor.matmul(tb[:, 2 + n % 2, 0:DH], probs_t[:, n % 2, q * P:q * P + P],
                                           v_tok[:, kb, c0:c0 + DH], start=q == 0, stop=q == nq - 1)
                ins.then_inc(at_pv, 1)

            for half in range(2):
                project(half)
                pe.wait_ge(pr_t, 6 * (half + 1))
                pe.wait_ge(pr_sq, 9 * (half + 1))
                n0 = nu * half
                qk(n0)
                for n in range(n0, n0 + nu + 1):
                    if n + 1 < n0 + nu:
                        qk(n + 1)
                    if n < n0 + nu:
                        probs_transposes(n)
                    if n > n0:
                        pv(n - 1)
                pe.wait_ge(at_o, n0 + nu)
            to_xt(E_O, o_tok)
            residual_product(S_WO, E_O, 4)

            pe.wait_ge(z_done, E_O + 2)
            pe.wait_ge(xt_lo_done, 4 * (E_O + 1))
            for pair in range(4):
                for kk in range(2):
                    for b in range(NB):
                        k = 2 * pair + kk
                        ins = transpose(tb[:, pair, kk * SEQ + b * P:kk * SEQ + b * P + P], h_tok[:, b, k * P:k * P + P])
            ins.then_inc(xt_tr, 1)
            pe.wait_ge(ht_done, 1)
            for b in range(NB):
                for k in range(KC):
                    ins = nc.tensor.matmul(acc[:, b, 0:NE], h_t[:, k, b * P:b * P + P], router[:, k, :],
                                           start=k == 0, stop=k == KC - 1)
            ins.then_inc(rt_mm, 1)
            pe.wait_ge(rt_rank_in, 1)
            nc.tensor.matmul(acc[:, 2, 0:NE], before[:, :], chosen[:, 0, :], start=True, stop=True)
            nc.tensor.matmul(acc[:, 2, 8:8 + NE], ones[:, :], chosen[:, 0, :], start=True, stop=False, skip_group_check=True)
            nc.tensor.matmul(acc[:, 2, 8:8 + NE], before[:, :], chosen[:, 1, :], start=False, stop=True, skip_group_check=True)
            nc.tensor.matmul(acc[:, 3, 0:NE], ones[:, :], chosen[:, 0, :], start=True, stop=False)
            nc.tensor.matmul(acc[:, 3, 0:NE], ones[:, :], chosen[:, 1, :], start=False, stop=True).then_inc(rt_rank, 1)

            def gather(job):
                pe.wait_ge(pick_done, job + 1)
                for k in range(KC):
                    for b in range(NB):
                        ins = nc.tensor.matmul(tb[:, k // 4, (k % 4) * P:(k % 4) * P + P], h_tok[:, b, k * P:k * P + P],
                                               pick[:, b, :], start=b == 0, stop=b == NB - 1)
                ins.then_inc(gather_mm, 1)

            gather(0)

            def expert_slab(s, use, xh, xl, k0, k, n, first, last, outs):
                pe.wait_ge(lo_done[s], use + 1)
                wh, wl = slab_view(w_hi, s, k, n), slab_view(w_lo, s, k, n)
                for kk in range(k):
                    for col, o in outs:
                        ins = three(o, xh[:, k0 + kk, :], xl[:, k0 + kk, :], wh[:, kk, col], wl[:, kk, col],
                                    first and kk == 0, last and kk == k - 1)
                return ins

            def act_transposes(jc):
                pe.wait_ge(e_act, jc + 1)
                pe.wait_ge(et_lo, jc)
                for q in range(4):
                    ins = transpose(tb[:, 2, q * P:q * P + P], act_e[:, q * P:q * P + P])
                ins.then_inc(et_tr, 1)

            def scatter(j):
                pe.wait_ge(y_done, j + 1)
                pe.wait_ge(put_t_done, j + 1)
                for b in range(NB):
                    for c in range(2):
                        ins = nc.tensor.matmul(tb[:, 2 * b + c, :], put_t[:, b, :], y_e[:, c * 512:c * 512 + 512], start=True, stop=True)
                ins.then_inc(sc_mm, 1)

            def job(j):
                col = slice(0, 512)
                pe.wait_ge(xs_lo_done, j + 1)

                def chunk(c, first):
                    jc = j * FE_CHUNKS + c
                    pe.wait_ge(e_silu, jc + 1)
                    for q in range(2):
                        ins = expert_slab(q, BASE[q] + j * PER_JOB[q] + c, xs_hi, xs_lo, 4 * q, 4, 512, q == 0, q == 1, [(col, acc[:, 0, :])])
                        ins.then_inc(slab_used[q], 1)
                    if first:
                        scatter(j)
                    else:
                        pe.wait_ge(sum_done, j + 2)
                        act_transposes(jc)
                    pe.wait_ge(e_act, jc + 1)
                    for q in range(2):
                        s = 2 + q
                        ins = expert_slab(s, BASE[s] + j * PER_JOB[s] + c, xs_hi, xs_lo, 4 * q, 4, 512, q == 0, q == 1, [(col, acc[:, 1, :])])
                        ins.then_inc(slab_used[s], 1)

                chunk(0, True)
                with pe.Fori(1, FE_CHUNKS) as c:
                    chunk(c, False)
                outs = [(slice(512 * c, 512 * c + 512), acc[:, 2 + c, :]) for c in range(2)]
                n_down = FE_KC // 2
                for d in range(n_down):
                    s = d % RING
                    if d == 2:
                        act_transposes((j + 1) * FE_CHUNKS)
                        gather(j + 1)
                        pe.wait_ge(put_done, j + 1)
                        for b in range(NB):
                            ins = transpose(tb[:, 3, b * P:b * P + P], put[:, b, :])
                        ins.then_inc(put_tr, 1)
                    if d == n_down - 2:
                        pe.wait_ge(et_lo, (j + 1) * FE_CHUNKS + 1)
                    ins = expert_slab(s, j * PER_JOB[s] + (BASE[s] + FE_CHUNKS + d // RING), aet_hi, aet_lo, 2 * d, 2, D, d == 0, d == n_down - 1, outs)
                    ins.then_inc(slab_used[s], 1)

            scatter(job_loops(pe, lambda j, k: job(j), None))

        @block.scalar
        def _(act):
            state = {"split": 0, "step": 0}

            def step(ins):
                ins.then_inc(act_step, 1)
                state["step"] += 1

            def settle():
                act.wait_ge(act_step, state["step"])

            def split_slot(s, use):
                act.wait_ge(raw_in[s], use_bytes(s, use))
                if not (isinstance(use, int) and use == 0):
                    act.wait_ge(slab_used[s], use)
                nc.scalar.copy(w_hi[:, s, :], raw[:, s, :]).then_inc(hi_done[s], 1)

            def split_to(n):
                while state["split"] < min(n, S_END):
                    i = state["split"]
                    split_slot(i % RING, i // RING)
                    state["split"] += 1

            def to_xt(event, fn, per_bank=1):
                for pair in range(4):
                    act.wait_ge(xt_tr, 4 * event + pair + 1)
                    for kk in range(2):
                        k = 2 * pair + kk
                        ins = fn(k, tb[:, pair, kk * SEQ:(kk + 1) * SEQ])
                    ins.then_inc(xt_hi_done, 1)

            def gain_fn(col):
                return lambda k, t: nc.scalar.activation(xt_hi[:, k, :], t, ACT.Copy, scale=cols[:, k, col:col + 1])

            def norm_stats(n, scr):
                for b in range(NB):
                    ins = nc.scalar.activation(scr[:, b, :], x[:, b, :], ACT.Square, accum_out=ss[:, b:b + 1])
                ins.then_inc(sq_done, 1)
                act.wait_ge(ms_done, n + 1)
                nc.scalar.activation(sd, ms, ACT.Sqrt).then_inc(sd_done, 1)

            act.dma_start(ident[:, :], a["c_ident"]).then_inc(consts_in, 16)
            rows = [(a["conv_dw_b"], C_DWB), (a["conv_norm"], C_CN), (a["conv_ln_g"], C_LG), (a["conv_ln_b"], C_LB),
                    (a["kv_norm"].rearrange("(o d) -> o d", o=1), C_KVN), (a["attn_norm"], C_AN), (a["ffn_norm"][0:1], C_F0)]
            act.dma_start(vec_rows[0:CONV, :], a["conv_dw_w"][0]).then_inc(rows_in, 16)
            for src, r in rows:
                act.dma_start(vec_rows[r:r + 1, :], src).then_inc(rows_in, 16)
            for half in range(2):
                act.dma_start(kq_rows[0:NG, DH * half:DH * half + DH], a["k_norm"]).then_inc(rows_in, 16)
                act.dma_start(kq_rows[NG:2 * NG, DH * half:DH * half + DH], a["q_norm"][0]).then_inc(rows_in, 16)
            act.dma_start(bin_row[0:1, :], a["conv_b_in"]).then_inc(bias_in, 16)
            act.dma_start(bout_row[0:1, :], a["conv_b_out"]).then_inc(bias_in, 16)
            act.dma_start(rel_sb[:, :], a["rel_bias"]).then_inc(tables_in, 16)
            act.dma_start(hot_sb[:, :, :], a["c_hot"]).then_inc(tables_in, 16)
            act.dma_start(mask_sb[:, :, :], a["c_mask"]).then_inc(tables_in, 16)
            act.sem_inc(e_silu, 1)
            def conv_chunk_out(k):
                act.wait_ge(conv_mm, k - CONV_DVE + 1)
                nc.scalar.activation(conv_t[:, k, :], acc[:, k - CONV_DVE, 0:SEQ], ACT.Identity,
                                     bias=cols[:, k, C_DWB:C_DWB + 1]).then_inc(conv_out, 1)

            act.wait_ge(x_in, 16)
            norm_stats(0, z)
            split_to(2)
            act.wait_ge(cols_tr, 1)
            nc.scalar.copy(cols[:, :, 0:NCOL], acc[:, 0, 0:KC * 40].rearrange("p (k c) -> p k c", k=KC)[:, :, 0:NCOL]).then_inc(cols_done, 1)
            act.wait_ge(cols_done, 1)
            act.wait_ge(gains_done, 1)
            to_xt(E_CONV_IN, gain_fn(C_CN))
            split_to(4)
            for c in range(2):
                wait_slab(act, S_WIN + 4 * c + 3)
                nc.scalar.activation(sig[:, :, :], acc[:, 2:4, :], ACT.Sigmoid).then_inc(glu_sig, 1)
                split_to(8 + 4 * c - 4)
                for pair in range(2):
                    act.wait_ge(glu_tr, 2 * c + pair + 1)
                    k = 4 * c + 2 * pair
                    nc.scalar.copy(u_t[:, k:k + 2, CONV - 1:], tb[:, 2 * c + pair, :].rearrange("p (k t) -> p k t", k=2)).then_inc(glu_t, 1)
                split_to(8 + 4 * c)
            for n, (k, t) in enumerate(PE_TAPS):
                if n % 2 == 0:
                    if n >= DIAGS:
                        act.wait_ge(diag_used, n - DIAGS + 1)
                    nc.scalar.activation(diag[:, n % DIAGS, :], ident[:, :], ACT.Copy, scale=cols[:, k, t:t + 1]).then_inc(diag_a, 1)
                if t == 8 and k > CONV_DVE:
                    conv_chunk_out(k - 1)
            conv_chunk_out(KC - 1)
            act.wait_ge(var_done, 1)
            nc.scalar.activation(sd, ms, ACT.Sqrt).then_inc(lnsd_done, 1)
            for pair in range(4):
                act.wait_ge(xt_tr, 4 * E_CONV_OUT + pair + 1)
                for kk in range(2):
                    k = 2 * pair + kk
                    step(nc.scalar.activation(act_tmp[:, k, :], tb[:, pair, kk * SEQ:(kk + 1) * SEQ], ACT.Silu,
                                              scale=cols[:, k, C_LG:C_LG + 1], bias=cols[:, k, C_LB:C_LB + 1]))
                settle()
                nc.scalar.copy(xt_hi[:, 2 * pair:2 * pair + 2, :], act_tmp[:, 2 * pair:2 * pair + 2, :]).then_inc(xt_hi_done, 1)
            split_to(S_WOUT + 4)
            act.wait_ge(res_done, 2)
            norm_stats(1, z_b)
            split_to(S_FFN + 2)
            to_xt(E_FFN, gain_fn(C_F0))
            split_to(S_FFN + 4)
            for c in range(FF_CHUNKS):
                wait_slab(act, S_FFN + 4 * c + 1)
                if c:
                    act.wait_ge(ff_act, c)
                nc.scalar.activation(silu_ff[:, :, :], acc[:, 0:2, 0:FF_COLS], ACT.Silu).then_inc(ff_silu, 1)
                split_to(S_FFN + 4 * c + 8)
            n_down = FF_KC // 2
            for d in range(n_down):
                act.wait_ge(fft_tr, d + 1)
                if d < n_down - 1:
                    nc.scalar.copy(actt_hi[:, 2 * d:2 * d + 2, :], tb[:, d % 4, :].rearrange("p (k t) -> p k t", k=2)).then_inc(fft_hi, 1)
                else:
                    nc.scalar.copy(actt_hi[:, 2 * d, :], tb[:, d % 4, 0:SEQ])
                    nc.scalar.copy(actt_hi[0:FF_TAIL, 2 * d + 1, :], tb[0:FF_TAIL, d % 4, SEQ:2 * SEQ]).then_inc(fft_hi, 1)
                if d >= 3:
                    split_to(S_DOWN + d + 2)
            split_to(S_KVQ)
            act.wait_ge(res_done, 4)
            norm_stats(2, z_c)
            split_to(S_KVQ + 2)
            to_xt(E_KV, gain_fn(C_KVN))
            split_to(S_KVQ + 4)

            def heads_out(half, m):
                n = 6 * half + (m if m < 3 else m - 3)
                g = m % 3
                dst, gain = (k_t, qk_gain[:, g:g + 1]) if m < 3 else (q_t, qk_gain[:, NG + g:NG + g + 1])
                act.wait_ge(pr_tr, n + 1)
                for i in range(2):
                    k0 = 4 * g + 2 * i
                    ins = nc.scalar.activation(dst[:, k0:k0 + 2, :], tb[:, 2 * (n % 2) + i, :].rearrange("p (k t) -> p k t", k=2),
                                               ACT.Copy, scale=gain)
                ins.then_inc(pr_t, 1)

            def project(half):
                for m in range(9):
                    mm = 9 * half + m
                    if m == 6 or (m == 0 and half):
                        to_xt(E_KV + 2 * half + (m == 6), gain_fn(C_AN if m == 6 else C_KVN))
                    split_to(S_KVQ + 2 * mm + 4)
                    wait_slab(act, S_KVQ + 2 * mm + 1)
                    bank = 2 * (mm % 2)
                    if 3 <= m < 6:
                        nc.scalar.copy(v_tok[:, :, (m - 3) * 512:(m - 2) * 512], acc[:, bank:bank + 2, :]).then_inc(pr_sq, 1)
                        if m == 3:
                            heads_out(half, 2)
                        continue
                    n = 6 * half + (m if m < 3 else m - 3)
                    if n:
                        act.wait_ge(pr_ms, n)
                    nc.scalar.activation(sq[:, :, :], acc[:, bank:bank + 2, :], ACT.Square).then_inc(pr_sq, 1)
                    act.wait_ge(pr_ms, n + 1)
                    nc.scalar.activation(sd16[:, :, 0:8], ms16[:, :, 0:8], ACT.Sqrt).then_inc(pr_sd, 1)
                    if m not in (0, 6):
                        heads_out(half, m - 1)
                heads_out(half, 8)
                split_to(S_KVQ + 18 * (half + 1) + 4)

            for half in range(2):
                project(half)
                for n in range(nu * half, nu * half + nu):
                    b = n % 2
                    nk = P * (b + 1)
                    act.wait_ge(at_max, n + 1)
                    if n >= 2:
                        act.wait_ge(at_tr, n - 1)
                    nc.scalar.activation(probs[n % 2][:, 0:NG * nk], scores[:, n % 2, 0:NG * nk], ACT.Exp,
                                         bias=small[:, 20 + n % 2:21 + n % 2], accum_out=small[:, 24 + n % 4:25 + n % 4]).then_inc(at_exp, 1)
                    act.wait_ge(at_tr, n + 1)
                    if n >= 2:
                        act.wait_ge(at_pv, n - 1)
                    w = 3 * P if b == 0 else 4 * P
                    nc.scalar.copy(probs_t[:, n % 2, 0:w], tb[:, 0, 0:w]).then_inc(at_ta, 1)
            to_xt(E_O, lambda k, t: nc.scalar.copy(xt_hi[:, k, :], t))
            act.wait_ge(res_done, 7)
            norm_stats(3, h_tok)
            act.wait_ge(xt_tr, 4 * (E_O + 1) + 1)
            for i in range(4):
                ins = nc.scalar.copy(h_t[:, 2 * i:2 * i + 2, :], tb[:, i, :].rearrange("p (k t) -> p k t", k=2))
            ins.then_inc(ht_done, 1)
            nc.scalar.memzero(put_t[:, :, :]).then_inc(put_t_done, 1)
            act.wait_ge(rt_v, 1)
            nc.scalar.activation(gate2[:, :, 1], gate2[:, :, 0], ACT.Exp).then_inc(rt_e, 1)

            def gather_out(job):
                act.wait_ge(gather_mm, job + 1)
                nc.scalar.copy(xs_hi[:, :, :], tb[:, 0:2, :].rearrange("p i (k t) -> p (i k) t", t=P)).then_inc(xs_hi_done, 1)

            gather_out(0)

            def act_out(jc, kc):
                act.wait_ge(et_tr, jc + 1)
                nc.scalar.copy(aet_hi[:, kc, :], tb[:, 2, :].rearrange("p (k t) -> p k t", k=4)).then_inc(et_hi, 1)

            def job(j):
                def chunk(c, first):
                    jc = j * FE_CHUNKS + c
                    for s in range(RING):
                        split_slot(s, BASE[s] + j * PER_JOB[s] + c)
                    wait_expert_slab(act, 1, j, c + 1)
                    act.wait_ge(e_act, jc + 1)
                    nc.scalar.activation(silu_e[:, :], acc[:, 0, :], ACT.Silu).then_inc(e_silu, 1)
                    if not first:
                        act_out(jc, bass.ds(c * 4 - 4, 4))

                chunk(0, True)
                with act.Fori(1, FE_CHUNKS) as c:
                    chunk(c, False)
                for it in range(4):
                    for s in range(RING if it < 3 else 2):
                        split_slot(s, j * PER_JOB[s] + (BASE[s] + FE_CHUNKS + it))
                    if it == 0:
                        act_out((j + 1) * FE_CHUNKS, slice(24, 28))
                        gather_out(j + 1)
                        act.wait_ge(put_tr, j + 1)
                        nc.scalar.copy(put_t[:, :, :], tb[:, 3, 0:SEQ].rearrange("p (b t) -> p b t", b=NB)).then_inc(put_t_done, 1)

            job_loops(act, lambda j, k: job(j), None)

        @block.gpsimd
        def _(pool):
            pool.wait_ge(consts_in, 16)
            pool.wait_ge(cols_done, 1)
            for n, (k, t) in enumerate(PE_TAPS):
                if n % 2:
                    if n >= DIAGS:
                        pool.wait_ge(diag_used, n - DIAGS + 1)
                    nc.gpsimd.tensor_scalar(diag[:, n % DIAGS, :], ident[:, :], cols[:, k, t:t + 1], None, ALU.mult).then_inc(diag_p, 1)

        @block.vector
        def _(dve):
            V = nc.vector
            state = {"split": 0, "step": 0}

            def step(ins):
                ins.then_inc(dve_step, 1)
                state["step"] += 1

            def settle():
                dve.wait_ge(dve_step, state["step"])

            def split_slot(s, use):
                dve.wait_ge(hi_done[s], use + 1)
                V.tensor_tensor(w_lo[:, s, :], raw[:, s, :], w_hi[:, s, :].bitcast(f32), ALU.subtract).then_inc(lo_done[s], 1)

            def split_to(n):
                while state["split"] < min(n, S_END):
                    i = state["split"]
                    split_slot(i % RING, i // RING)
                    state["split"] += 1

            def norm(n, dst):
                dve.wait_ge(sq_done, n + 1)
                V.tensor_scalar(ms, ss, 1.0 / D, EPS, ALU.mult, ALU.add).then_inc(ms_done, 1)
                dve.wait_ge(sd_done, n + 1)
                step(V.reciprocal(rr, sd))
                settle()
                for b in range(NB):
                    ins = V.tensor_scalar(dst[:, b, :], x[:, b, :], rr[:, b:b + 1], None, ALU.mult)
                return ins

            def to_xt(event, fn):
                for pair in range(4):
                    dve.wait_ge(xt_hi_done, 4 * event + pair + 1)
                    for kk in range(2):
                        k = 2 * pair + kk
                        ins = fn(k, tb[:, pair, kk * SEQ:(kk + 1) * SEQ])
                    ins.then_inc(xt_lo_done, 1)

            def gain_fn(col):
                return lambda k, t: V.scalar_tensor_tensor(xt_lo[:, k, :], t, cols[:, k, col:col + 1],
                                                           xt_hi[:, k, :].bitcast(f32), ALU.mult, ALU.subtract)

            for s0 in (e_act, et_lo, sum_done):
                dve.sem_inc(s0, 1)
            V.memset(ones_row[0:1, :], 1.0).then_inc(pad_done, 1)
            V.memset(u_t[:, :, 0:CONV - 1], 0.0).then_inc(pad_done, 1)
            norm(0, z).then_inc(z_done, 1)
            split_to(2)
            dve.wait_ge(cols_tr, 1)
            V.tensor_scalar(qk_gain[:, 0:NG], acc[:, 1, 0:NG], 1.0, None, ALU.mult)
            V.tensor_scalar(qk_gain[:, NG:2 * NG], acc[:, 1, NG:2 * NG], DH ** -0.5, None, ALU.mult).then_inc(gains_done, 1)
            dve.wait_ge(cols_done, 1)
            to_xt(E_CONV_IN, gain_fn(C_CN))
            split_to(4)

            def conv(k0):
                n0 = CONV * k0
                for t in range(CONV):
                    for i in range(2):
                        k = k0 + i
                        if t == 0:
                            ins = V.tensor_scalar(conv_t[:, k, :], u_t[:, k, 0:SEQ], cols[:, k, 0:1], cols[:, k, C_DWB:C_DWB + 1], ALU.mult, ALU.add)
                        else:
                            dve.wait_ge(conv_done, n0 + 2 * t - 1 + i)
                            ins = V.scalar_tensor_tensor(conv_t[:, k, :], u_t[:, k, t:t + SEQ], cols[:, k, t:t + 1], conv_t[:, k, :], ALU.mult, ALU.add)
                        ins.then_inc(conv_done, 1)

            for c in range(2):
                dve.wait_ge(glu_sig, c + 1)
                V.tensor_tensor(u_tok[:, :, c * 512:c * 512 + 512], acc[:, 0:2, :], sig[:, :, :], ALU.mult).then_inc(glu_u, 1)
                split_to(4 + 4 * c)
                split_to(8 + 4 * c)
                for k in range(2 * c, CONV_DVE if c else 2, 2):
                    dve.wait_ge(glu_t, k // 2 + 1)
                    conv(k)
            dve.wait_ge(bias_mm, 1)
            V.tensor_tensor(bias_sb[:, :, :], acc[0:HEADS, 0:NG, 0:BW], mask_sb[:, :, :], ALU.add).then_inc(bias_rows, 1)
            dve.wait_ge(conv_tr, 1)
            for b in range(NB):
                for i in range(2):
                    step(V.bn_stats(bn[:, b, i, :], tb[:, 2 * b + i, :]))
            settle()
            for b in range(NB):
                step(V.bn_aggr(small[:, 12 + 2 * b:14 + 2 * b], bn[:, b, :, :].rearrange("p i s -> p (i s)")))
            settle()
            var = small[:, 12:16].rearrange("p (b i) -> p b i", b=NB)[:, :, 1]
            V.tensor_scalar(ms, var, EPS, None, ALU.add).then_inc(var_done, 1)
            dve.wait_ge(lnsd_done, 1)
            step(V.reciprocal(rr, sd))
            settle()
            for b in range(NB):
                ins = V.tensor_scalar(z[:, b, :], tb[:, 2 * b:2 * b + 2, :].rearrange("p i n -> p (i n)"),
                                      small[:, 12 + 2 * b:13 + 2 * b], rr[:, b:b + 1], ALU.subtract, ALU.mult)
            ins.then_inc(z_done, 1)
            to_xt(E_CONV_OUT, lambda k, t: V.tensor_tensor(xt_lo[:, k, :], act_tmp[:, k, :], xt_hi[:, k, :].bitcast(f32), ALU.subtract))

            def residual(last_slabs):
                for c, i in enumerate(last_slabs):
                    wait_slab(dve, i)
                    V.tensor_tensor(x[:, :, c * 512:c * 512 + 512], x[:, :, c * 512:c * 512 + 512], acc[:, 2 * c:2 * c + 2, :], ALU.add).then_inc(res_done, 1)

            residual((S_WOUT + 1, S_WOUT + 3))
            dve.wait_ge(res_done, 2)
            norm(1, z_b).then_inc(z_done, 1)
            split_to(S_FFN + 2)
            to_xt(E_FFN, gain_fn(C_F0))
            split_to(S_FFN + 4)
            dve.wait_ge(bias_out, 16)
            for c in range(FF_CHUNKS):
                split_to(S_FFN + 4 * c + 6)
                wait_slab(dve, S_FFN + 4 * c + 3)
                dve.wait_ge(ff_silu, c + 1)
                V.tensor_tensor(act_ff[:, :, c * FF_COLS:(c + 1) * FF_COLS], acc[:, 2:4, 0:FF_COLS], silu_ff[:, :, :], ALU.mult).then_inc(ff_act, 1)
                split_to(S_FFN + 4 * c + 8)
            n_down = FF_KC // 2
            for d in range(n_down):
                dve.wait_ge(fft_hi, d + 1)
                for kk, n in ((0, P), (1, P)) if d < n_down - 1 else ((0, P), (1, FF_TAIL)):
                    k = 2 * d + kk
                    ins = V.tensor_tensor(actt_lo[0:n, k, :], tb[0:n, d % 4, kk * SEQ:(kk + 1) * SEQ], actt_hi[0:n, k, :].bitcast(f32), ALU.subtract)
                ins.then_inc(fft_lo, 1)
                if d >= 3:
                    split_to(S_DOWN + d + 2)
            split_to(S_KVQ)
            residual((S_KVQ - 1, S_KVQ - 1))
            dve.wait_ge(res_done, 4)
            norm(2, z_c).then_inc(z_done, 4)
            V.engine_nop().then_inc(res_done, 1)
            split_to(S_KVQ + 2)
            to_xt(E_KV, gain_fn(C_KVN))
            split_to(S_KVQ + 4)
            def project(half):
                for m in range(9):
                    mm = 9 * half + m
                    if m == 6 or (m == 0 and half):
                        to_xt(E_KV + 2 * half + (m == 6), gain_fn(C_AN if m == 6 else C_KVN))
                    split_to(S_KVQ + 2 * mm + 4)
                    if 3 <= m < 6:
                        continue
                    n = 6 * half + (m if m < 3 else m - 3)
                    bank = 2 * (mm % 2)
                    dve.wait_ge(pr_sq, mm + 1)
                    step(V.tensor_reduce(ss16[:, :, 0:8], sq[:, :, :].rearrange("p b (h d) -> p b h d", d=DH), AX.X, ALU.add))
                    settle()
                    V.tensor_scalar(ms16[:, :, 0:8], ss16[:, :, 0:8], 1.0 / DH, EPS, ALU.mult, ALU.add).then_inc(pr_ms, 1)
                    dve.wait_ge(pr_sd, n + 1)
                    step(V.reciprocal(rr16[:, :, 0:8], sd16[:, :, 0:8]))
                    settle()
                    if n:
                        dve.wait_ge(pr_tr, n)
                    for b in range(NB):
                        ins = V.tensor_tensor(kn[:, b, :].rearrange("p (h d) -> p h d", d=DH), acc[:, bank + b, :].rearrange("p (h d) -> p h d", d=DH),
                                              rr16[:, b, 0:8].unsqueeze(2).to_broadcast([P, 8, DH]), ALU.mult)
                    ins.then_inc(pr_kn, 1)
                split_to(S_KVQ + 18 * (half + 1) + 4)

            def soft(n):
                h, b = n // 2, n % 2
                nk = P * (b + 1)
                dve.wait_ge(at_qk, n + 1)
                if b == 0:
                    dve.wait_ge(bias_t_in[h % 2], 32 * (h // 2 + 1))
                if n >= 2:
                    dve.wait_ge(at_exp, n - 1)
                sc = scores[:, n % 2, 0:NG * nk].rearrange("p (g k) -> p g k", g=NG)
                ps = acc[:, 2 * (n % 2):2 * (n % 2) + 2, :].rearrange("p i (g k) -> p (i g) k", g=2)[:, 0:NG, 0:nk]
                step(V.tensor_tensor(sc, ps, bias_t[:, h % 2, :, SEQ - nk:SEQ], ALU.add))
                settle()
                step(V.reduce_max(small[:, 22 + n % 2:23 + n % 2], scores[:, n % 2, 0:NG * nk], AX.X))
                settle()
                V.tensor_scalar(small[:, 20 + n % 2:21 + n % 2], small[:, 22 + n % 2:23 + n % 2], -1.0, None, ALU.mult).then_inc(at_max, 1)

            def rest(n):
                b = n % 2
                dve.wait_ge(at_tr, n + 1)
                if n >= 2:
                    dve.wait_ge(at_pv, n - 1)
                if b:
                    V.tensor_copy(probs_t[:, n % 2, 4 * P:6 * P], tb[:, 1, 0:2 * P]).then_inc(at_tv, 1)
                else:
                    V.engine_nop().then_inc(at_tv, 1)

            def normalise(n):
                h, b = n // 2, n % 2
                r = small[:, 28 + n % 4:29 + n % 4]
                step(V.reciprocal(r, small[:, 24 + n % 4:25 + n % 4]))
                dve.wait_ge(at_pv, n + 1)
                settle()
                V.tensor_scalar(o_tok[:, b, h * DH:(h + 1) * DH], tb[:, 2 + n % 2, 0:DH], r, None, ALU.mult).then_inc(at_o, 1)

            for half in range(2):
                project(half)
                n0 = nu * half
                soft(n0)
                for n in range(n0, n0 + nu + 1):
                    if n + 1 < n0 + nu:
                        soft(n + 1)
                    if n < n0 + nu:
                        rest(n)
                    if n > n0:
                        normalise(n - 1)
            dve.wait_ge(at_o, 2 * nu)
            V.engine_nop().then_inc(z_done, 1)
            to_xt(E_O, lambda k, t: V.tensor_tensor(xt_lo[:, k, :], t, xt_hi[:, k, :].bitcast(f32), ALU.subtract))
            residual((S_WO + 1, S_WO + 3))

            dve.wait_ge(res_done, 7)
            norm_ins = norm(3, h_tok)
            step(norm_ins)
            settle()
            dve.wait_ge(tables_in, 48 + 64)
            for b in range(NB):
                ins = V.tensor_tensor(h_tok[:, b, :], h_tok[:, b, :], gain_row[:, :], ALU.mult)
            ins.then_inc(z_done, 1)
            V.memset(ones[:, :], 1.0)
            V.memset(share[:, :, :], 0.0)
            step(V.memset(rank[:, :, :], 1000.0))
            dve.wait_ge(rt_mm, 1)
            step(V.tensor_copy(logits[:, :, :], acc[:, 0:2, 0:NE]))
            settle()
            for b in range(NB):
                step(V.max(top[:, b, :], logits[:, b, :]))
            settle()
            for b in range(NB):
                step(V.max_index(top_i[:, b, :], top[:, b, :], logits[:, b, :]))
            settle()
            step(V.tensor_copy(top_f[:, :, :], top_i[:, :, :]))
            V.tensor_tensor(gate2[:, :, 0], top[:, :, 1], top[:, :, 0], ALU.subtract).then_inc(rt_v, 1)
            settle()
            for b in range(NB):
                V.tensor_scalar(hot1[:, b, :], iota[:, 0:NE], top_f[:, b, 0:1], None, ALU.is_equal)
                step(V.tensor_scalar(hot2[:, b, :], iota[:, 0:NE], top_f[:, b, 1:2], None, ALU.is_equal))
            settle()
            V.tensor_tensor(chosen[:, :, :], hot1[:, :, :], hot2[:, :, :], ALU.add).then_inc(rt_rank_in, 1)
            dve.wait_ge(rt_e, 1)
            step(V.tensor_scalar(gate2[:, :, 2], gate2[:, :, 1], 1.0, None, ALU.add))
            settle()
            step(V.reciprocal(gate2[:, :, 3], gate2[:, :, 2]))
            settle()
            step(V.tensor_tensor(gate2[:, :, 4], gate2[:, :, 3], gate2[:, :, 1], ALU.mult))
            settle()
            for b in range(NB):
                step(V.tensor_scalar(hot1[:, b, :], hot1[:, b, :], gate2[:, b, 3:4], None, ALU.mult))
            settle()
            for b in range(NB):
                step(V.scalar_tensor_tensor(share[:, b, 0:NE], hot2[:, b, :], gate2[:, b, 4:5], hot1[:, b, :], ALU.mult, ALU.add))
            dve.wait_ge(rt_rank, 1)
            settle()
            step(V.tensor_scalar(hot2[:, :, :], chosen[:, :, :], -1000.0, 1000.0, ALU.mult, ALU.add))
            settle()
            step(V.tensor_tensor(rank[:, :, 0:NE], acc[:, 2, 0:2 * NE].rearrange("p (b e) -> p b e", b=NB), hot2[:, :, :], ALU.add))
            full = over[:, 0, :]
            step(V.tensor_scalar(full, acc[:, 3, 0:NE], float(P), None, ALU.is_gt))
            settle()
            step(V.tensor_copy(over[:, 1, 0:1], full[:, 0:1]))
            settle()
            for e in range(1, NE):
                step(V.tensor_tensor(over[:, 1, e:e + 1], over[:, 1, e - 1:e], full[:, e:e + 1], ALU.add))
                settle()
            for k in range(3):
                step(V.tensor_scalar(over[:, 2 + k, :], over[:, 1, :], float(k + 1), None, ALU.is_equal))
            settle()
            for k in range(3):
                step(V.tensor_tensor(over[:, 2 + k, :], over[:, 2 + k, :], full, ALU.mult))
            settle()
            for k in range(3):
                step(V.tensor_tensor(over[:, 5, :], over[:, 2 + k, :], iota[:, 0:NE], ALU.mult))
                settle()
                step(V.reduce_sum(small[:, 40 + k:41 + k], over[:, 5, :], AX.X))
                for b in range(NB):
                    settle()
                    step(V.tensor_tensor(over[:, 6, :], over[:, 2 + k, :], share[:, b, 0:NE], ALU.mult))
                    step(V.tensor_scalar(over[:, 7, :], rank[:, b, 0:NE], float(-P), None, ALU.add))
                    settle()
                    step(V.tensor_tensor(over[:, 7, :], over[:, 2 + k, :], over[:, 7, :], ALU.mult))
                    settle()
                    step(V.reduce_sum(share[:, b, NE + k:NE + k + 1], over[:, 6, :], AX.X))
                    step(V.reduce_sum(rank[:, b, NE + k:NE + k + 1], over[:, 7, :], AX.X))
            settle()
            step(V.tensor_copy(over_i[:, 0:3], small[:, 40:43]))
            V.tensor_copy(over_i[:, 4:5], over[:, 1, NE - 1:NE]).then_inc(rt_done, 1)
            dve.wait_ge(rt_done, 1)
            settle()

            def pick_of(job, value):
                V.tensor_copy(rk_now[:, :].unsqueeze(2), rank[:, :, bass.ds(job, 1)]).then_inc(rk_sem, 1)
                dve.wait_ge(rk_sem, value + 1)
                for b in range(NB):
                    ins = V.tensor_scalar(pick[:, b, :], iota[:, :], rk_now[:, b:b + 1], None, ALU.is_equal)
                ins.then_inc(pick_done, 1)

            def gather_out(job):
                dve.wait_ge(xs_hi_done, job + 1)
                V.tensor_tensor(xs_lo[:, :, :], tb[:, 0:2, :].rearrange("p i (k t) -> p (i k) t", t=P), xs_hi[:, :, :].bitcast(f32), ALU.subtract).then_inc(xs_lo_done, 1)

            pick_of(0, 0)
            gather_out(0)

            def e_mult(j, c):
                jc = j * FE_CHUNKS + c + 1
                wait_expert_slab(dve, 3, j, c + 1)
                dve.wait_ge(e_silu, jc + 1)
                dve.wait_ge(et_tr, jc)
                V.tensor_tensor(act_e[:, :], acc[:, 1, :], silu_e[:, :], ALU.mult).then_inc(e_act, 1)

            def act_out(jc, kc):
                dve.wait_ge(et_hi, jc)
                V.tensor_tensor(aet_lo[:, kc, :], tb[:, 2, :].rearrange("p (k t) -> p k t", k=4), aet_hi[:, kc, :].bitcast(f32), ALU.subtract).then_inc(et_lo, 1)

            def take_y(j):
                wait_expert_slab(dve, 1, j, 0)
                V.tensor_copy(y_e[:, :], acc[:, 2:4, :].rearrange("p i n -> p (i n)")).then_inc(y_done, 1)

            def add_sum(j):
                dve.wait_ge(sc_mm, j + 1)
                V.tensor_tensor(x[:, :, :].rearrange("p b d -> p (b d)"), x[:, :, :].rearrange("p b d -> p (b d)"),
                                tb[:, :, :].rearrange("p i n -> p (i n)"), ALU.add).then_inc(sum_done, 1)

            def job(j):
                V.tensor_copy(sh_now[:, :].unsqueeze(2), share[:, :, bass.ds(j, 1)]).then_inc(sh_sem, 1)
                dve.wait_ge(sh_sem, j + 1)
                dve.wait_ge(pick_done, j + 1)
                for b in range(NB):
                    ins = V.tensor_scalar(put[:, b, :], pick[:, b, :], sh_now[:, b:b + 1], None, ALU.mult)
                ins.then_inc(put_done, 1)
                dve.wait_ge(put_done, j + 1)
                pick_of(j + 1, j + 1)

                def chunk(c, first):
                    jc = j * FE_CHUNKS + c
                    for s in range(2):
                        split_slot(s, BASE[s] + j * PER_JOB[s] + c)
                    if first:
                        take_y(j)
                    else:
                        e_mult(j, c - 1)
                    for s in range(2, 4):
                        split_slot(s, BASE[s] + j * PER_JOB[s] + c)
                    if first:
                        add_sum(j)
                    else:
                        act_out(jc, bass.ds(c * 4 - 4, 4))

                chunk(0, True)
                with dve.Fori(1, FE_CHUNKS) as c:
                    chunk(c, False)
                for it in range(4):
                    for s in range(RING if it < 3 else 2):
                        split_slot(s, j * PER_JOB[s] + (BASE[s] + FE_CHUNKS + it))
                        if it == 0 and s == 1:
                            e_mult(j, FE_CHUNKS - 1)
                    if it == 0:
                        act_out((j + 1) * FE_CHUNKS, slice(24, 28))
                        gather_out(j + 1)

            n_jobs = job_loops(dve, lambda j, k: job(j), None)
            take_y(n_jobs)
            add_sum(n_jobs)

        return


def kernel(**inputs):
    import concourse.bacc as bacc
    from concourse.bass_utils import run_bass_kernel_spmd

    nc = bacc.Bacc("TRN2", target_bir_lowering=False, num_devices=1)
    arrays = {k: np.ascontiguousarray(v) for k, v in inputs.items()}
    arrays.update(host_constants())
    feed, args = {}, {}
    for name, v in arrays.items():
        feed["in_" + name] = v
        args[name] = nc.dram_tensor("in_" + name, v.shape, mybir.dt.from_np(v.dtype), kind="ExternalInput").ap()
    out = nc.dram_tensor("out_0", (1, SEQ, D), mybir.dt.float32, kind="ExternalOutput").ap()
    build(nc, args, out)
    r = run_bass_kernel_spmd(nc, [feed], core_ids=[0])
    return r.results[0]["out_0"]
```

```python
from contextlib import ExitStack
import math

import numpy as np
import concourse.bass as bass
from concourse import mybir

P = 128
D = 1024
SEQ = 256
NB = SEQ // P
KC = D // P
CONV = 31
HEADS = 16
DH = 64
GROUPS = ((128, 1), (512, 4), (2048, 16))
NG = len(GROUPS)
QW = NG * HEADS * DH
BUCKETS = 32
MAX_DISTANCE = 2048
FF = 2752
FF_COLS = 344
FF_CHUNKS = FF // FF_COLS
FF_KC = -(-FF // P)
FF_TAIL = FF - (FF_KC - 1) * P
NE = 8
FE = 3584
FE_CHUNKS = FE // 512
FE_KC = FE // P
EPS = 1e-6
NEG = -1e30
CONV_DVE = 5
DIAGS = 8
RING = 4
SLAB = 2048
BW = 384
COPIES = 64

S_WIN = 0
S_WOUT = S_WIN + 8
S_FFN = S_WOUT + 4
S_DOWN = S_FFN + 4 * FF_CHUNKS
S_KVQ = S_DOWN + FF_KC // 2
S_WO = S_KVQ + 2 * 18
S_END = S_WO + 4
BASE = [(S_END - s + RING - 1) // RING for s in range(RING)]
PER_JOB = [11, 11, 10, 10]
MAX_JOBS = NE + 4


def host_constants():
    ident = np.eye(P, dtype=np.float32)
    before = np.triu(np.ones((P, P), np.float32), 1)
    iota = np.tile(np.arange(P, dtype=np.float32), (P, 1))
    dist = 255 - np.arange(BW)
    exact = BUCKETS // 2
    n = np.clip(dist, 0, None)
    large = exact + (np.log(np.maximum(n, 1) / exact) / np.log(MAX_DISTANCE / exact)
                     * (BUCKETS - exact)).astype(np.int32)
    bucket = np.where(n < exact, n, np.minimum(large, BUCKETS - 1))
    hot = (bucket[None, :] == np.arange(BUCKETS)[:, None])
    ok = np.zeros((NG, BW), bool)
    for g, (window, d) in enumerate(GROUPS):
        ok[g] = (dist >= 0) & (dist <= window) & (dist % d == 0) & (dist // d <= P)
    hots = np.zeros((BUCKETS, NG, BW), np.float32)
    mask = np.zeros((HEADS, NG, BW), np.float32)
    for g in range(NG):
        hots[:, g] = hot & ok[g][None, :]
        mask[:, g] = np.where(ok[g], 0.0, NEG)[None, :]
    return {"c_ident": ident, "c_before": before, "c_iota": iota,
            "c_hot": hots, "c_mask": mask}


def build(nc, a, out):
    f32, f32r, u32 = mybir.dt.float32, mybir.dt.float32r, mybir.dt.uint32
    i32 = mybir.dt.int32
    ALU, ACT, AX = mybir.AluOpType, mybir.ActivationFunctionType, mybir.AxisListType

    scratch_bias = nc.dram_tensor("bias_rows", (COPIES, HEADS, NG, BW), f32).ap()

    with ExitStack() as ctx:
        def sb(name, shape, dt=f32, where=ctx):
            return where.enter_context(nc.sbuf_tensor("sb_" + name, shape, dt))

        def sem(name):
            return ctx.enter_context(nc.semaphore(name))

        raw = sb("raw", [P, RING, SLAB])
        w_hi = sb("w_hi", [P, RING, SLAB], f32r)
        w_lo = sb("w_lo", [P, RING, SLAB], f32r)
        x = sb("x", [P, NB, D])
        xt_hi = sb("xt_hi", [P, KC, SEQ], f32r)
        xt_lo = sb("xt_lo", [P, KC, SEQ], f32r)
        ident = sb("ident", [P, P])
        small = sb("small", [P, 64])
        ss, ms, sd, rr = (small[:, 2 * i:2 * i + 2] for i in range(4))
        cols = sb("cols", [P, KC, 40])
        qk_gain = sb("qk_gain", [P, 8])
        ss16, ms16, sd16, rr16 = (sb(f"h16_{i}", [P, 2, 16]) for i in range(4))
        def phase():
            return ExitStack()

        with phase() as ph:
            z = sb("z", [P, NB, D], where=ph)
            vec_rows = sb("vec_rows", [40, D], where=ph)
            kq_rows = sb("kq_rows", [8, P], where=ph)
            bin_row = sb("bin_row", [1, 2 * D], where=ph)
            bout_row = sb("bout_row", [1, D], where=ph)
            ones_row = sb("ones_row", [1, P], where=ph)
            sig = sb("sig", [P, NB, 512], where=ph)
            u_tok = sb("u_tok", [P, NB, D], where=ph)
            u_t = sb("u_t", [P, KC, CONV - 1 + SEQ], where=ph)
            diag = sb("diag", [P, DIAGS, P], where=ph)
            conv_t = sb("conv_t", [P, KC, SEQ], where=ph)
            act_tmp = sb("act_tmp", [P, KC, SEQ], where=ph)
            bn = sb("bn", [P, NB, 2, 6], where=ph)
            hot_sb = sb("hot_sb", [BUCKETS, NG, BW], where=ph)
            rel_sb = sb("rel_sb", [BUCKETS, NG * HEADS], where=ph)
            mask_sb = sb("mask_sb", [HEADS, NG, BW], where=ph)
            bias_sb = sb("bias_sb", [HEADS, NG, BW], where=ph)
        with phase() as ph:
            z_b = sb("z_b", [P, NB, D], where=ph)
            silu_ff = sb("silu_ff", [P, NB, FF_COLS], where=ph)
            act_ff = sb("act_ff", [P, NB, FF], where=ph)
            actt_hi = sb("actt_hi", [P, FF_KC, SEQ], f32r, where=ph)
            actt_lo = sb("actt_lo", [P, FF_KC, SEQ], f32r, where=ph)
        with phase() as ph:
            z_c = sb("z_c", [P, NB, D], where=ph)
            k_t = sb("k_t", [P, NG * 4, SEQ], where=ph)
            q_t = sb("q_t", [P, NG * 4, SEQ], where=ph)
            v_tok = sb("v_tok", [P, NB, QW // 2], where=ph)
            kn = sb("kn", [P, NB, 512], where=ph)
            sq = sb("sq", [P, NB, 512], where=ph)
            bias_t = sb("bias_t", [P, 2, NG, SEQ], where=ph)
            scores = sb("scores", [P, 2, NG * SEQ], where=ph)
            probs_t = sb("probs_t", [P, 2, NG, 3 * P], where=ph)
            o_t = sb("o_t", [P, KC, SEQ], where=ph)
        probs = [kn[:, :, :].rearrange("p b d -> p (b d)")[:, 0:NG * SEQ],
                 sq[:, :, :].rearrange("p b d -> p (b d)")[:, 0:NG * SEQ]]
        with phase() as ph:
            h_tok = sb("h_tok", [P, NB, D], where=ph)
            h_t = sb("h_t", [P, KC, SEQ], where=ph)
            gain_row = sb("gain_row", [P, D], where=ph)
            router = sb("router", [P, KC, NE], where=ph)
            xs_hi = sb("xs_hi", [P, KC, P], f32r, where=ph)
            xs_lo = sb("xs_lo", [P, KC, P], f32r, where=ph)
            silu_e = sb("silu_e", [P, 512], where=ph)
            act_e = sb("act_e", [P, 512], where=ph)
            aet_hi = sb("aet_hi", [P, FE_KC, P], f32r, where=ph)
            aet_lo = sb("aet_lo", [P, FE_KC, P], f32r, where=ph)
            y_e = sb("y_e", [P, D], where=ph)
            pick = sb("pick", [P, NB, P], where=ph)
            put = sb("put", [P, NB, P], where=ph)
            put_t = sb("put_t", [P, NB, P], where=ph)
            iota = sb("iota", [P, P], where=ph)
            before = sb("before", [P, P], where=ph)
            ones = sb("ones", [P, P], where=ph)
            logits = sb("logits", [P, NB, NE], where=ph)
            top = sb("top", [P, NB, 8], where=ph)
            top_i = sb("top_i", [P, NB, 8], u32, where=ph)
            top_f = sb("top_f", [P, NB, 8], where=ph)
            gate2 = sb("gate2", [P, NB, 8], where=ph)
            hot1 = sb("hot1", [P, NB, NE], where=ph)
            hot2 = sb("hot2", [P, NB, NE], where=ph)
            chosen = sb("chosen", [P, NB, NE], where=ph)
            rank = sb("rank", [P, NB, MAX_JOBS], where=ph)
            share = sb("share", [P, NB, MAX_JOBS], where=ph)
            over = sb("over", [P, 8, NE], where=ph)
            over_i = sb("over_i", [P, 8], i32, where=ph)
            rk_now = sb("rk_now", [P, NB], where=ph)
            sh_now = sb("sh_now", [P, NB], where=ph)

        acc = ctx.enter_context(nc.psum_tensor("acc", [P, 4, 512], f32))
        tb = ctx.enter_context(nc.psum_tensor("tb", [P, 4, 512], f32))

        raw_in = [sem(f"raw_in{s}") for s in range(RING)]
        hi_done = [sem(f"hi_done{s}") for s in range(RING)]
        lo_done = [sem(f"lo_done{s}") for s in range(RING)]
        slab_used = [sem(f"slab_used{s}") for s in range(RING)]
        x_in, consts_in, rows_in = sem("x_in"), sem("consts_in"), sem("rows_in")
        bias_in = sem("bias_in")
        tables_in = sem("tables_in")
        cols_tr, cols_done, gains_done = sem("cols_tr"), sem("cols_done"), sem("gains_done")
        bias_mm, bias_rows, bias_out = sem("bias_mm"), sem("bias_rows"), sem("bias_out")
        sq_done, ms_done, sd_done, z_done = sem("sq_done"), sem("ms_done"), sem("sd_done"), sem("z_done")
        xt_tr, xt_hi_done, xt_lo_done = sem("xt_tr"), sem("xt_hi_done"), sem("xt_lo_done")
        act_step, dve_step, pool_step = sem("act_step"), sem("dve_step"), sem("pool_step")
        pad_done = sem("pad_done")
        glu_sig, glu_u, glu_tr, glu_t = sem("glu_sig"), sem("glu_u"), sem("glu_tr"), sem("glu_t")
        diag_a, diag_p, diag_used, conv_mm, conv_out = (sem(n) for n in ("diag_a", "diag_p", "diag_used", "conv_mm", "conv_out"))
        conv_done, conv_tr, var_done, lnsd_done = sem("conv_done"), sem("conv_tr"), sem("var_done"), sem("lnsd_done")
        res_done = sem("res_done")
        ff_silu, ff_act = sem("ff_silu"), sem("ff_act")
        fft_tr, fft_hi, fft_lo = sem("fft_tr"), sem("fft_hi"), sem("fft_lo")
        pr_sq, pr_ms, pr_sd, pr_kn, pr_tr, pr_t = (sem(n) for n in
            ("pr_sq", "pr_ms", "pr_sd", "pr_kn", "pr_tr", "pr_t"))
        bias_t_in = [sem("bias_t_in0"), sem("bias_t_in1")]
        at_qk, at_add, at_max, at_exp, at_norm, at_tr, at_ta, at_pv, at_o = (sem(n) for n in
            ("at_qk", "at_add", "at_max", "at_exp", "at_norm", "at_tr", "at_ta", "at_pv", "at_o"))
        rt_mm, rt_v, rt_e, rt_rank_in, rt_rank, rt_counts, rt_done = (sem(n) for n in
            ("rt_mm", "rt_v", "rt_e", "rt_rank_in", "rt_rank", "rt_counts", "rt_done"))
        ht_done = sem("ht_done")
        pick_done, put_done, rk_sem, sh_sem = sem("pick_done"), sem("put_done"), sem("rank_taken"), sem("share_taken")
        gather_mm, xs_hi_done, xs_lo_done = sem("gather_mm"), sem("xs_hi_done"), sem("xs_lo_done")
        e_silu, e_act = sem("e_silu"), sem("e_act")
        et_tr, et_hi, et_lo = sem("et_tr"), sem("et_hi"), sem("et_lo")
        put_tr, put_t_done = sem("put_tr"), sem("put_t_done")
        y_done, sc_mm, sum_done = sem("y_done"), sem("sc_mm"), sem("sum_done")
        out_done = sem("out_done")

        C_DWB, C_CN, C_LG, C_LB, C_KVN, C_AN, C_F0 = range(CONV, CONV + 7)
        NCOL = CONV + 7


        def wait_slab(eng, i):
            eng.wait_ge(slab_used[i % RING], i // RING + 1)

        def wait_expert_slab(eng, s, j, n):
            eng.wait_ge(slab_used[s], BASE[s] + j * PER_JOB[s] + n)

        PE_TAPS = [(k, t) for k in range(CONV_DVE, KC) for t in range(CONV)]

        def slab_view(t, s, k, n):
            return t[:, s, 0:k * n].rearrange("p (k n) -> p k n", k=k)

        def w_src(w, k0, k, c0, n):
            return w[k0 * P:(k0 + k) * P, c0:c0 + n].rearrange("(k p) n -> p k n", p=P)

        def fixed_slabs():
            w_in, w_out = a["conv_w_in"][0], a["conv_w_out"][0]
            for c in range(2):
                for half in range(2):
                    for kh in range(2):
                        yield w_src(w_in, 4 * kh, 4, D * half + 512 * c, 512), 4, 512
            for c in range(2):
                for kh in range(2):
                    yield w_src(w_out, 4 * kh, 4, 512 * c, 512), 4, 512
            for c in range(FF_CHUNKS):
                for w in (a["ffn_w_gate"][0], a["ffn_w_up"][0]):
                    for kh in range(2):
                        yield w_src(w, 4 * kh, 4, FF_COLS * c, FF_COLS), 4, FF_COLS
            for d in range(FF_KC // 2):
                yield (w_src(a["ffn_w_down"][0], 2 * d, 2, 0, D) if d < FF_KC // 2 - 1 else None), 2, D
            for half in range(2):
                for w, c0 in ((a["w_q"][0], 0), (a["w_kv"], 0), (a["w_kv"], QW)):
                    for g in range(NG):
                        for kh in range(2):
                            yield w_src(w, 4 * kh, 4, c0 + g * D + 512 * half, 512), 4, 512
            for c in range(2):
                for kh in range(2):
                    yield w_src(a["w_o"][0], 4 * kh, 4, 512 * c, 512), 4, 512

        n_over_ap = over_i[0:1, 4:5]

        def job_loops(eng, body, after_routing):
            with eng.Fori(0, NE) as j:
                body(j, j)
            eng.wait_ge(rt_done, 1)
            n_over = eng.value_load(n_over_ap, min_val=0, max_val=3)
            with eng.If(n_over > 0):
                with eng.Fori(0, n_over) as k:
                    body(k + NE, k)
            return n_over + NE

        block = ctx.enter_context(nc.Block())

        def use_bytes(s, use):
            i = S_DOWN + FF_KC // 2 - 1
            if isinstance(use, int):
                extra = 16 if (s == i % RING and use >= i // RING) else 0
                return 16 * (use + 1) + extra
            return use * 16 + (16 + (16 if s == i % RING else 0))

        @block.sync
        def _(sp):
            sp.dma_start(x[:, :, :], a["x"][0].rearrange("(b p) d -> p b d", p=P)).then_inc(x_in, 16)
            slabs = list(fixed_slabs())
            assert len(slabs) == S_END

            def load(i):
                s, use = i % RING, i // RING
                src, k, n = slabs[i]
                if use:
                    sp.wait_ge(lo_done[s], use)
                if src is None:
                    w = a["ffn_w_down"][0]
                    k0 = FF_KC - 2
                    sp.dma_start(raw[:, s, 0:D], w[k0 * P:(k0 + 1) * P, :]).then_inc(raw_in[s], 16)
                    sp.dma_start(raw[0:FF_TAIL, s, D:2 * D], w[(k0 + 1) * P:FF, :]).then_inc(raw_in[s], 16)
                else:
                    sp.dma_start(slab_view(raw, s, k, n), src).then_inc(raw_in[s], 16)

            for i in range(4):
                load(i)
            for i in range(4, S_FFN):
                load(i)
            sp.wait_ge(bias_rows, 1)
            sp.dma_start(scratch_bias.rearrange("c h g w -> h c (g w)"),
                         bias_sb[:, :, :].rearrange("h g w -> h (g w)").unsqueeze(1).to_broadcast([HEADS, COPIES, NG * BW])).then_inc(bias_out, 16)
            for i in range(S_FFN, S_KVQ + 18):
                load(i)
            sp.wait_ge(bias_out, 16)

            def load_bias(h):
                if h >= 2:
                    sp.wait_ge(at_add, 2 * (h - 1))
                for top_row in range(0, P, COPIES):
                    src = bass.AP(scratch_bias.tensor, h * NG * BW + P - 1 - top_row,
                                  [[HEADS * NG * BW - 1, COPIES], [BW, NG], [1, SEQ]])
                    sp.dma_start(bias_t[top_row:top_row + COPIES, h % 2, :, :], src).then_inc(bias_t_in[h % 2], 16)

            sp.wait_ge(res_done, 5 + 0)
            load_bias(0)
            load_bias(1)
            first = S_KVQ + 18
            for i in range(first, first + RING):
                load(i)
            for h in range(2, 8):
                load_bias(h)
                if h >= 4:
                    load(first + RING + h - 4)
            for i in range(first + 2 * RING, S_WO):
                load(i)
            load_bias(8)
            load_bias(9)
            for i in range(S_WO, S_END):
                load(i)

            def load_expert_slab(s, use, src, k, n):
                sp.wait_ge(lo_done[s], use)
                sp.dma_start(slab_view(raw, s, k, n), src).then_inc(raw_in[s], 16)

            for h in range(10, HEADS):
                load_bias(h)
            sp.wait_ge(res_done, 7)
            sp.dma_start(gain_row[:, :], a["ffn_norm"][1:2].to_broadcast([P, D])).then_inc(tables_in, 16)
            sp.dma_start(router[:, :, :], a["moe_router"][0].rearrange("(k p) e -> p k e", p=P)).then_inc(tables_in, 16)
            sp.dma_start(iota[:, :], a["c_iota"]).then_inc(tables_in, 16)
            sp.dma_start(before[:, :], a["c_before"]).then_inc(tables_in, 16)

            def job(j, expert):
                wg, wu, wd = (a[n][0, bass.ds(expert, 1)].rearrange("o k n -> (o k) n") for n in ("moe_w_gate", "moe_w_up", "moe_w_down"))
                with sp.Fori(0, FE_CHUNKS) as c:
                    for q, (w, kh) in enumerate(((wg, 0), (wg, 1), (wu, 0), (wu, 1))):
                        s = q
                        load_expert_slab(s, BASE[s] + j * PER_JOB[s] + c,
                                         w[kh * 512:(kh + 1) * 512, bass.ds(c * 512, 512)].rearrange("(k p) n -> p k n", p=P), 4, 512)
                for d in range(FE_KC // 2):
                    s = d % RING
                    load_expert_slab(s, j * PER_JOB[s] + (BASE[s] + FE_CHUNKS + d // RING), wd[2 * d * P:(2 * d + 2) * P, :].rearrange("(k p) n -> p k n", p=P), 2, D)

            with sp.Fori(0, NE) as j:
                job(j, j)
            sp.wait_ge(rt_done, 1)
            n_over = sp.value_load(over_i[0:1, 4:5], min_val=0, max_val=3)
            with sp.If(n_over > 0):
                with sp.Fori(0, n_over) as k:
                    expert = sp.value_load(over_i[0:1, bass.ds(k, 1)], min_val=0, max_val=NE - 1)
                    job(k + NE, expert)
            sp.wait_ge(sum_done, n_over + (NE + 2))
            sp.dma_start(out[0].rearrange("(b p) d -> p b d", p=P), x[:, :, :]).then_inc(out_done, 16)
            sp.wait_ge(out_done, 16)

        E_CONV_IN, E_CONV_OUT, E_FFN, E_QKV, _, _, _, E_O = range(8)
        nu = HEADS

        @block.tensor
        def _(pe):
            def transpose(o, i):
                n = i.shape[0]
                return nc.tensor.transpose(o, i, ident[0:n, 0:n])

            def three(o, hi_x, lo_x, hi_w, lo_w, start, stop):
                nc.tensor.matmul(o, hi_x, hi_w, start=start, stop=False)
                nc.tensor.matmul(o, hi_x, lo_w, start=False, stop=False)
                return nc.tensor.matmul(o, lo_x, hi_w, start=False, stop=stop)

            def slab_mm(i, k0, k, n, first, last, outs, xh=xt_hi, xl=xt_lo, rows=None):
                s, use = i % RING, i // RING
                pe.wait_ge(lo_done[s], use + 1)
                wh, wl = slab_view(w_hi, s, k, n), slab_view(w_lo, s, k, n)
                for kk in range(k):
                    r = slice(0, P if rows is None else rows[kk])
                    for tok, col, o in outs:
                        ins = three(o, xh[r, k0 + kk, tok], xl[r, k0 + kk, tok], wh[r, kk, col], wl[r, kk, col],
                                    first and kk == 0, last and kk == k - 1)
                ins.then_inc(slab_used[s], 1)
                return ins

            def blocks(bank, n):
                return [(slice(P * b, P * b + P), slice(0, n), acc[:, bank + b, 0:n]) for b in range(NB)]

            def to_xt(event, src):
                if event:
                    pe.wait_ge(xt_lo_done, 4 * event)
                pe.wait_ge(z_done, event + 1)
                for pair in range(4):
                    for kk in range(2):
                        for b in range(NB):
                            k = 2 * pair + kk
                            ins = transpose(tb[:, pair, kk * SEQ + b * P:kk * SEQ + b * P + P], src[:, b, k * P:k * P + P])
                    ins.then_inc(xt_tr, 1)

            pe.sem_inc(et_tr, 1)
            pe.wait_ge(consts_in, 16)
            pe.wait_ge(rows_in, 16 * 12)
            for k in range(KC):
                transpose(acc[:, 0, k * 40:k * 40 + NCOL], vec_rows[0:NCOL, k * P:k * P + P])
            transpose(acc[:, 1, 0:2 * NG], kq_rows[0:2 * NG, :]).then_inc(cols_tr, 1)

            to_xt(E_CONV_IN, z)
            pe.wait_ge(cols_done, 1)
            pe.wait_ge(gains_done, 1)
            pe.wait_ge(bias_in, 32)
            pe.wait_ge(pad_done, 2)
            for c in range(2):
                if c:
                    pe.wait_ge(glu_u, c)
                for half in range(2):
                    for b in range(NB):
                        nc.tensor.matmul(acc[:, 2 * half + b, :], ones_row[0:1, :],
                                         bin_row[0:1, half * D + c * 512:half * D + c * 512 + 512], start=True, stop=False)
                    for kh in range(2):
                        if c == 0 and half == 0:
                            pe.wait_ge(xt_lo_done, 4 * E_CONV_IN + 2 * kh + 2)
                        ins = slab_mm(S_WIN + 4 * c + 2 * half + kh, 4 * kh, 4, 512, False, kh == 1, blocks(2 * half, 512))
                pe.wait_ge(glu_u, c + 1)
                for pair in range(2):
                    for kk in range(2):
                        for b in range(NB):
                            k = 4 * c + 2 * pair + kk
                            ins = transpose(tb[:, 2 * c + pair, kk * SEQ + b * P:kk * SEQ + b * P + P], u_tok[:, b, k * P:k * P + P])
                    ins.then_inc(glu_tr, 1)
            pe.wait_ge(glu_t, 4)
            for n, (k, t) in enumerate(PE_TAPS):
                pe.wait_ge(diag_p if n % 2 else diag_a, n // 2 + 1)
                ins = nc.tensor.matmul(acc[:, k - CONV_DVE, 0:SEQ], diag[:, n % DIAGS, :], u_t[:, k, t:t + SEQ],
                                       start=t == 0, stop=t == CONV - 1)
                ins.then_inc(diag_used, 1)
                if t == CONV - 1:
                    pe.wait_ge(diag_used, n + 1)
                    pe.sem_inc(conv_mm, 1)
            pe.wait_ge(conv_out, KC - CONV_DVE)
            pe.wait_ge(tables_in, 48)
            for g in range(NG):
                ins = nc.tensor.matmul(acc[0:HEADS, g, 0:BW], rel_sb[:, g * HEADS:(g + 1) * HEADS], hot_sb[:, g, :],
                                       start=True, stop=True)
            ins.then_inc(bias_mm, 1)
            pe.wait_ge(conv_done, CONV * CONV_DVE)
            for b in range(NB):
                for k in range(KC):
                    ins = transpose(tb[:, 2 * b + k // 4, (k % 4) * P:(k % 4) * P + P], conv_t[:, k, b * P:b * P + P])
            ins.then_inc(conv_tr, 1)
            to_xt(E_CONV_OUT, z)
            pe.wait_ge(bias_rows, 1)

            def residual_product(s0, event, n0, bias_row=None):
                pe.wait_ge(xt_lo_done, 4 * event + 2)
                for c in range(2):
                    if bias_row is not None:
                        for b in range(NB):
                            nc.tensor.matmul(acc[:, 2 * c + b, :], ones_row[0:1, :], bias_row[0:1, c * 512:c * 512 + 512],
                                             start=True, stop=False)
                    for kh in range(2):
                        if c == 0 and kh:
                            pe.wait_ge(xt_lo_done, 4 * (event + 1))
                        ins = slab_mm(s0 + 2 * c + kh, 4 * kh, 4, 512, bias_row is None and kh == 0, kh == 1, blocks(2 * c, 512))

            residual_product(S_WOUT, E_CONV_OUT, 0, bout_row)

            pe.wait_ge(res_done, 2)
            to_xt(E_FFN, z_b)
            for c in range(FF_CHUNKS):
                i = S_FFN + 4 * c
                if c:
                    pe.wait_ge(ff_silu, c)
                for kh in range(2):
                    if c == 0:
                        pe.wait_ge(xt_lo_done, 4 * E_FFN + 2 * kh + 2)
                    slab_mm(i + kh, 4 * kh, 4, FF_COLS, kh == 0, kh == 1, blocks(0, FF_COLS))
                if c:
                    pe.wait_ge(ff_act, c)
                for kh in range(2):
                    slab_mm(i + 2 + kh, 4 * kh, 4, FF_COLS, kh == 0, kh == 1, blocks(2, FF_COLS))
            pe.wait_ge(ff_act, FF_CHUNKS)

            def ff_transposes(d):
                if d >= 4:
                    pe.wait_ge(fft_lo, d - 3)
                for kk in range(2):
                    k = 2 * d + kk
                    n = min(P, FF - k * P)
                    for b in range(NB):
                        ins = transpose(tb[0:n, d % 4, kk * SEQ + b * P:kk * SEQ + b * P + P], act_ff[:, b, k * P:k * P + n])
                ins.then_inc(fft_tr, 1)

            halves = [(slice(P * b, P * b + P), slice(512 * c, 512 * c + 512), acc[:, 2 * c + b, :]) for c in range(2) for b in range(NB)]
            n_down = FF_KC // 2
            for d in range(3):
                ff_transposes(d)
            for d in range(n_down):
                if d + 3 < n_down:
                    ff_transposes(d + 3)
                pe.wait_ge(fft_lo, d + 1)
                slab_mm(S_DOWN + d, 2 * d, 2, D, d == 0, d == n_down - 1, halves, actt_hi, actt_lo,
                        [P, P if d < n_down - 1 else FF_TAIL])

            pe.wait_ge(res_done, 4)

            def head_transposes(half, m):
                n = 6 * half + m
                pe.wait_ge(pr_kn, n + 1)
                if n >= 2:
                    pe.wait_ge(pr_t, n - 1)
                for kk in range(4):
                    for b in range(NB):
                        ins = transpose(tb[:, 2 * (n % 2) + kk // 2, (kk % 2) * SEQ + b * P:(kk % 2) * SEQ + b * P + P],
                                        kn[:, b, kk * P:kk * P + P])
                ins.then_inc(pr_tr, 1)

            def project(half):
                for m in range(9):
                    mm = 9 * half + m
                    event = E_QKV + 2 * half + (m == 3)
                    if m in (0, 3):
                        if m == 3:
                            pe.wait_ge(pr_t, 6 * half + 2)
                        to_xt(event, z_c)
                    if m >= 2:
                        if m - 2 < 6:
                            pe.wait_ge(pr_kn, 6 * half + m - 1)
                        else:
                            pe.wait_ge(pr_sq, mm - 1)
                    for kh in range(2):
                        if m in (0, 3):
                            pe.wait_ge(xt_lo_done, 4 * event + 2 * kh + 2)
                        slab_mm(S_KVQ + 2 * mm + kh, 4 * kh, 4, 512, kh == 0, kh == 1, blocks(2 * (mm % 2), 512))
                    if 1 <= m <= 6:
                        head_transposes(half, m - 1)

            def qk(n):
                h, b = (n // 2) % 8, n % 2
                if n >= 2:
                    pe.wait_ge(at_add, n - 1)
                half = slice(DH * (h % 2), DH * (h % 2) + DH)
                nk = P * (b + 1)
                for g in range(NG):
                    t = g * 4 + h // 2
                    o = acc[:, 2 * (n % 2) + g // 2, (g % 2) * SEQ:(g % 2) * SEQ + nk]
                    ins = nc.tensor.matmul(o, q_t[half, t, b * P:b * P + P], k_t[half, t, 0:nk], start=True, stop=True)
                ins.then_inc(at_qk, 1)

            def probs_transposes(n):
                b = n % 2
                pe.wait_ge(at_norm, n + 1)
                if n:
                    pe.wait_ge(at_ta, n)
                nk = P * (b + 1)
                for q in range(NG * (b + 1)):
                    ins = transpose(tb[:, q // 4, (q % 4) * P:(q % 4) * P + P], probs[n % 2][:, q * P:q * P + P])
                ins.then_inc(at_tr, 1)

            def pv(head):
                h = head % 8
                pe.wait_ge(at_ta, 2 * head + 2)
                if head >= 4:
                    pe.wait_ge(at_o, head // 2 - 1)
                pt = probs_t[:, head % 2, :, :]
                o = tb[DH * (h % 2):DH * (h % 2) + DH, 2 + (h // 2) % 2, 0:SEQ]
                for g in range(NG):
                    v = slice(g * 512 + h * DH, g * 512 + h * DH + DH)
                    nc.tensor.matmul(o, v_tok[:, 0, v], pt[:, g, 0:SEQ], start=g == 0, stop=False)
                    ins = nc.tensor.matmul(o[:, P:SEQ], v_tok[:, 1, v], pt[:, g, SEQ:SEQ + P], start=False, stop=g == NG - 1)
                ins.then_inc(at_pv, 1)

            for half in range(2):
                project(half)
                pe.wait_ge(pr_t, 6 * (half + 1))
                pe.wait_ge(pr_kn, 6 * (half + 1))
                n0 = nu * half
                pe.wait_ge(pr_sq, 9 * (half + 1))
                qk(n0)
                qk(n0 + 1)
                for n in range(n0, n0 + nu):
                    if n + 2 < n0 + nu:
                        qk(n + 2)
                    if n > n0:
                        probs_transposes(n - 1)
                    if n % 2 and n - n0 >= 3:
                        pv((n - 3) // 2)
                probs_transposes(n0 + nu - 1)
                pv((n0 + nu) // 2 - 1)
                pe.wait_ge(at_o, 4 * (half + 1))
            residual_product(S_WO, E_O, 4)

            pe.wait_ge(z_done, E_O + 1)
            pe.wait_ge(xt_lo_done, 4 * (E_O + 1))
            for pair in range(4):
                for kk in range(2):
                    for b in range(NB):
                        k = 2 * pair + kk
                        ins = transpose(tb[:, pair, kk * SEQ + b * P:kk * SEQ + b * P + P], h_tok[:, b, k * P:k * P + P])
            ins.then_inc(xt_tr, 1)
            pe.wait_ge(ht_done, 1)
            for b in range(NB):
                for k in range(KC):
                    ins = nc.tensor.matmul(acc[:, b, 0:NE], h_t[:, k, b * P:b * P + P], router[:, k, :],
                                           start=k == 0, stop=k == KC - 1)
            ins.then_inc(rt_mm, 1)
            pe.wait_ge(rt_rank_in, 1)
            nc.tensor.matmul(acc[:, 2, 0:NE], before[:, :], chosen[:, 0, :], start=True, stop=True)
            nc.tensor.matmul(acc[:, 2, 8:8 + NE], ones[:, :], chosen[:, 0, :], start=True, stop=False, skip_group_check=True)
            nc.tensor.matmul(acc[:, 2, 8:8 + NE], before[:, :], chosen[:, 1, :], start=False, stop=True, skip_group_check=True)
            nc.tensor.matmul(acc[:, 3, 0:NE], ones[:, :], chosen[:, 0, :], start=True, stop=False)
            nc.tensor.matmul(acc[:, 3, 0:NE], ones[:, :], chosen[:, 1, :], start=False, stop=True).then_inc(rt_rank, 1)

            def gather(job):
                pe.wait_ge(pick_done, job + 1)
                for k in range(KC):
                    for b in range(NB):
                        ins = nc.tensor.matmul(tb[:, k // 4, (k % 4) * P:(k % 4) * P + P], h_tok[:, b, k * P:k * P + P],
                                               pick[:, b, :], start=b == 0, stop=b == NB - 1)
                ins.then_inc(gather_mm, 1)

            gather(0)

            def expert_slab(s, use, xh, xl, k0, k, n, first, last, outs):
                pe.wait_ge(lo_done[s], use + 1)
                wh, wl = slab_view(w_hi, s, k, n), slab_view(w_lo, s, k, n)
                for kk in range(k):
                    for col, o in outs:
                        ins = three(o, xh[:, k0 + kk, :], xl[:, k0 + kk, :], wh[:, kk, col], wl[:, kk, col],
                                    first and kk == 0, last and kk == k - 1)
                return ins

            def act_transposes(jc):
                pe.wait_ge(e_act, jc + 1)
                pe.wait_ge(et_lo, jc)
                for q in range(4):
                    ins = transpose(tb[:, 2, q * P:q * P + P], act_e[:, q * P:q * P + P])
                ins.then_inc(et_tr, 1)

            def scatter(j):
                pe.wait_ge(y_done, j + 1)
                pe.wait_ge(put_t_done, j + 1)
                for b in range(NB):
                    for c in range(2):
                        ins = nc.tensor.matmul(tb[:, 2 * b + c, :], put_t[:, b, :], y_e[:, c * 512:c * 512 + 512], start=True, stop=True)
                ins.then_inc(sc_mm, 1)

            def job(j):
                col = slice(0, 512)
                pe.wait_ge(xs_lo_done, j + 1)

                def chunk(c, first):
                    jc = j * FE_CHUNKS + c
                    pe.wait_ge(e_silu, jc + 1)
                    for q in range(2):
                        ins = expert_slab(q, BASE[q] + j * PER_JOB[q] + c, xs_hi, xs_lo, 4 * q, 4, 512, q == 0, q == 1, [(col, acc[:, 0, :])])
                        ins.then_inc(slab_used[q], 1)
                    if first:
                        scatter(j)
                    else:
                        pe.wait_ge(sum_done, j + 2)
                        act_transposes(jc)
                    pe.wait_ge(e_act, jc + 1)
                    for q in range(2):
                        s = 2 + q
                        ins = expert_slab(s, BASE[s] + j * PER_JOB[s] + c, xs_hi, xs_lo, 4 * q, 4, 512, q == 0, q == 1, [(col, acc[:, 1, :])])
                        ins.then_inc(slab_used[s], 1)

                chunk(0, True)
                with pe.Fori(1, FE_CHUNKS) as c:
                    chunk(c, False)
                outs = [(slice(512 * c, 512 * c + 512), acc[:, 2 + c, :]) for c in range(2)]
                n_down = FE_KC // 2
                for d in range(n_down):
                    s = d % RING
                    if d == 2:
                        act_transposes((j + 1) * FE_CHUNKS)
                        gather(j + 1)
                        pe.wait_ge(put_done, j + 1)
                        for b in range(NB):
                            ins = transpose(tb[:, 3, b * P:b * P + P], put[:, b, :])
                        ins.then_inc(put_tr, 1)
                    if d == n_down - 2:
                        pe.wait_ge(et_lo, (j + 1) * FE_CHUNKS + 1)
                    ins = expert_slab(s, j * PER_JOB[s] + (BASE[s] + FE_CHUNKS + d // RING), aet_hi, aet_lo, 2 * d, 2, D, d == 0, d == n_down - 1, outs)
                    ins.then_inc(slab_used[s], 1)

            scatter(job_loops(pe, lambda j, k: job(j), None))

        @block.scalar
        def _(act):
            state = {"split": 0, "step": 0}

            def step(ins):
                ins.then_inc(act_step, 1)
                state["step"] += 1

            def settle():
                act.wait_ge(act_step, state["step"])

            def split_slot(s, use):
                act.wait_ge(raw_in[s], use_bytes(s, use))
                if not (isinstance(use, int) and use == 0):
                    act.wait_ge(slab_used[s], use)
                nc.scalar.copy(w_hi[:, s, :], raw[:, s, :]).then_inc(hi_done[s], 1)

            def split_to(n):
                while state["split"] < min(n, S_END):
                    i = state["split"]
                    split_slot(i % RING, i // RING)
                    state["split"] += 1

            def to_xt(event, fn, per_bank=1):
                for pair in range(4):
                    act.wait_ge(xt_tr, 4 * event + pair + 1)
                    for kk in range(2):
                        k = 2 * pair + kk
                        ins = fn(k, tb[:, pair, kk * SEQ:(kk + 1) * SEQ])
                    ins.then_inc(xt_hi_done, 1)

            def gain_fn(col):
                return lambda k, t: nc.scalar.activation(xt_hi[:, k, :], t, ACT.Copy, scale=cols[:, k, col:col + 1])

            def norm_stats(n, scr):
                for b in range(NB):
                    ins = nc.scalar.activation(scr[:, b, :], x[:, b, :], ACT.Square, accum_out=ss[:, b:b + 1])
                ins.then_inc(sq_done, 1)
                act.wait_ge(ms_done, n + 1)
                nc.scalar.activation(sd, ms, ACT.Sqrt).then_inc(sd_done, 1)

            act.dma_start(ident[:, :], a["c_ident"]).then_inc(consts_in, 16)
            rows = [(a["conv_dw_b"], C_DWB), (a["conv_norm"], C_CN), (a["conv_ln_g"], C_LG), (a["conv_ln_b"], C_LB),
                    (a["kv_norm"].rearrange("(o d) -> o d", o=1), C_KVN), (a["attn_norm"], C_AN), (a["ffn_norm"][0:1], C_F0)]
            act.dma_start(vec_rows[0:CONV, :], a["conv_dw_w"][0]).then_inc(rows_in, 16)
            for src, r in rows:
                act.dma_start(vec_rows[r:r + 1, :], src).then_inc(rows_in, 16)
            for half in range(2):
                act.dma_start(kq_rows[0:NG, DH * half:DH * half + DH], a["k_norm"]).then_inc(rows_in, 16)
                act.dma_start(kq_rows[NG:2 * NG, DH * half:DH * half + DH], a["q_norm"][0]).then_inc(rows_in, 16)
            act.dma_start(bin_row[0:1, :], a["conv_b_in"]).then_inc(bias_in, 16)
            act.dma_start(bout_row[0:1, :], a["conv_b_out"]).then_inc(bias_in, 16)
            act.dma_start(rel_sb[:, :], a["rel_bias"]).then_inc(tables_in, 16)
            act.dma_start(hot_sb[:, :, :], a["c_hot"]).then_inc(tables_in, 16)
            act.dma_start(mask_sb[:, :, :], a["c_mask"]).then_inc(tables_in, 16)
            act.sem_inc(e_silu, 1)
            def conv_chunk_out(k):
                act.wait_ge(conv_mm, k - CONV_DVE + 1)
                nc.scalar.activation(conv_t[:, k, :], acc[:, k - CONV_DVE, 0:SEQ], ACT.Identity,
                                     bias=cols[:, k, C_DWB:C_DWB + 1]).then_inc(conv_out, 1)

            act.wait_ge(x_in, 16)
            norm_stats(0, z)
            split_to(2)
            act.wait_ge(cols_tr, 1)
            nc.scalar.copy(cols[:, :, 0:NCOL], acc[:, 0, 0:KC * 40].rearrange("p (k c) -> p k c", k=KC)[:, :, 0:NCOL]).then_inc(cols_done, 1)
            act.wait_ge(cols_done, 1)
            act.wait_ge(gains_done, 1)
            to_xt(E_CONV_IN, gain_fn(C_CN))
            split_to(4)
            for c in range(2):
                wait_slab(act, S_WIN + 4 * c + 3)
                nc.scalar.activation(sig[:, :, :], acc[:, 2:4, :], ACT.Sigmoid).then_inc(glu_sig, 1)
                split_to(8 + 4 * c - 4)
                for pair in range(2):
                    act.wait_ge(glu_tr, 2 * c + pair + 1)
                    k = 4 * c + 2 * pair
                    nc.scalar.copy(u_t[:, k:k + 2, CONV - 1:], tb[:, 2 * c + pair, :].rearrange("p (k t) -> p k t", k=2)).then_inc(glu_t, 1)
                split_to(8 + 4 * c)
            for n, (k, t) in enumerate(PE_TAPS):
                if n % 2 == 0:
                    if n >= DIAGS:
                        act.wait_ge(diag_used, n - DIAGS + 1)
                    nc.scalar.activation(diag[:, n % DIAGS, :], ident[:, :], ACT.Copy, scale=cols[:, k, t:t + 1]).then_inc(diag_a, 1)
                if t == 8 and k > CONV_DVE:
                    conv_chunk_out(k - 1)
            conv_chunk_out(KC - 1)
            act.wait_ge(var_done, 1)
            nc.scalar.activation(sd, ms, ACT.Sqrt).then_inc(lnsd_done, 1)
            for pair in range(4):
                act.wait_ge(xt_tr, 4 * E_CONV_OUT + pair + 1)
                for kk in range(2):
                    k = 2 * pair + kk
                    step(nc.scalar.activation(act_tmp[:, k, :], tb[:, pair, kk * SEQ:(kk + 1) * SEQ], ACT.Silu,
                                              scale=cols[:, k, C_LG:C_LG + 1], bias=cols[:, k, C_LB:C_LB + 1]))
                settle()
                nc.scalar.copy(xt_hi[:, 2 * pair:2 * pair + 2, :], act_tmp[:, 2 * pair:2 * pair + 2, :]).then_inc(xt_hi_done, 1)
            split_to(S_WOUT + 4)
            act.wait_ge(res_done, 2)
            norm_stats(1, z_b)
            split_to(S_FFN + 2)
            to_xt(E_FFN, gain_fn(C_F0))
            split_to(S_FFN + 4)
            for c in range(FF_CHUNKS):
                wait_slab(act, S_FFN + 4 * c + 1)
                if c:
                    act.wait_ge(ff_act, c)
                nc.scalar.activation(silu_ff[:, :, :], acc[:, 0:2, 0:FF_COLS], ACT.Silu).then_inc(ff_silu, 1)
                split_to(S_FFN + 4 * c + 8)
            n_down = FF_KC // 2
            for d in range(n_down):
                act.wait_ge(fft_tr, d + 1)
                if d < n_down - 1:
                    nc.scalar.copy(actt_hi[:, 2 * d:2 * d + 2, :], tb[:, d % 4, :].rearrange("p (k t) -> p k t", k=2)).then_inc(fft_hi, 1)
                else:
                    nc.scalar.copy(actt_hi[:, 2 * d, :], tb[:, d % 4, 0:SEQ])
                    nc.scalar.copy(actt_hi[0:FF_TAIL, 2 * d + 1, :], tb[0:FF_TAIL, d % 4, SEQ:2 * SEQ]).then_inc(fft_hi, 1)
                if d >= 3:
                    split_to(S_DOWN + d + 2)
            split_to(S_KVQ)
            act.wait_ge(res_done, 4)
            norm_stats(2, z_c)
            split_to(S_KVQ + 2)
            to_xt(E_QKV, gain_fn(C_AN))
            split_to(S_KVQ + 4)

            def heads_out(half, m):
                n = 6 * half + m
                g = m % 3
                dst, gain = (q_t, qk_gain[:, NG + g:NG + g + 1]) if m < 3 else (k_t, qk_gain[:, g:g + 1])
                act.wait_ge(pr_tr, n + 1)
                for i in range(2):
                    k0 = 4 * g + 2 * i
                    ins = nc.scalar.activation(dst[:, k0:k0 + 2, :], tb[:, 2 * (n % 2) + i, :].rearrange("p (k t) -> p k t", k=2),
                                               ACT.Copy, scale=gain)
                ins.then_inc(pr_t, 1)

            def project(half):
                for m in range(9):
                    mm = 9 * half + m
                    if m == 3 or (m == 0 and half):
                        to_xt(E_QKV + 2 * half + (m == 3), gain_fn(C_AN if m == 0 else C_KVN))
                    split_to(min(S_KVQ + 2 * mm + 4, S_KVQ + 18 * (half + 1)))
                    wait_slab(act, S_KVQ + 2 * mm + 1)
                    bank = 2 * (mm % 2)
                    if m >= 6:
                        nc.scalar.copy(v_tok[:, :, (m - 6) * 512:(m - 5) * 512], acc[:, bank:bank + 2, :]).then_inc(pr_sq, 1)
                        if m == 6:
                            heads_out(half, 5)
                        continue
                    n = 6 * half + m
                    if n:
                        act.wait_ge(pr_ms, n)
                    nc.scalar.activation(sq[:, :, :], acc[:, bank:bank + 2, :], ACT.Square).then_inc(pr_sq, 1)
                    act.wait_ge(pr_ms, n + 1)
                    nc.scalar.activation(sd16[:, :, 0:8], ms16[:, :, 0:8], ACT.Sqrt).then_inc(pr_sd, 1)
                    if m:
                        heads_out(half, m - 1)

            def probs_out(n):
                b, head = n % 2, n // 2
                act.wait_ge(at_tr, n + 1)
                if head >= 2:
                    act.wait_ge(at_pv, head - 1)
                nk = P * (b + 1)
                nc.scalar.copy(probs_t[:, head % 2, :, b * P:b * P + nk],
                               tb[:, 0:2, :].rearrange("p i n -> p (i n)")[:, 0:NG * nk].rearrange("p (g k) -> p g k", g=NG)).then_inc(at_ta, 1)

            def o_out(pair):
                act.wait_ge(at_pv, 2 * pair + 2)
                nc.scalar.copy(o_t[:, pair, :], tb[:, 2 + pair % 2, 0:SEQ]).then_inc(at_o, 1)

            for half in range(2):
                project(half)
                n0 = nu * half
                for n in range(n0, n0 + nu):
                    nk = P * (n % 2 + 1)
                    act.wait_ge(at_max, n + 1)
                    if n >= 2:
                        act.wait_ge(at_tr, n - 1)
                    nc.scalar.activation(probs[n % 2][:, 0:NG * nk], scores[:, n % 2, 0:NG * nk], ACT.Exp,
                                         bias=small[:, 20 + n % 2:21 + n % 2], accum_out=small[:, 24 + n % 4:25 + n % 4]).then_inc(at_exp, 1)
                    if n > n0:
                        probs_out(n - 1)
                    if (n - n0) % 4 == 2 and n - n0 >= 6:
                        o_out((n - 6) // 4)
                    if (n - n0) in (4, 6, 8, 10):
                        split_to(S_KVQ + 18 * (half + 1) + (n - n0 - 2) // 2)
                probs_out(n0 + nu - 1)
                o_out((n0 + nu) // 4 - 1)
            act.wait_ge(at_o, 8)
            for pair in range(4):
                nc.scalar.copy(xt_hi[:, 2 * pair:2 * pair + 2, :], o_t[:, 2 * pair:2 * pair + 2, :]).then_inc(xt_hi_done, 1)
            act.wait_ge(res_done, 7)
            norm_stats(3, h_tok)
            act.wait_ge(xt_tr, 4 * E_O + 1)
            for i in range(4):
                ins = nc.scalar.copy(h_t[:, 2 * i:2 * i + 2, :], tb[:, i, :].rearrange("p (k t) -> p k t", k=2))
            ins.then_inc(ht_done, 1)
            nc.scalar.memzero(put_t[:, :, :]).then_inc(put_t_done, 1)
            act.wait_ge(rt_v, 1)
            nc.scalar.activation(gate2[:, :, 1], gate2[:, :, 0], ACT.Exp).then_inc(rt_e, 1)

            def gather_out(job):
                act.wait_ge(gather_mm, job + 1)
                nc.scalar.copy(xs_hi[:, :, :], tb[:, 0:2, :].rearrange("p i (k t) -> p (i k) t", t=P)).then_inc(xs_hi_done, 1)

            gather_out(0)

            def act_out(jc, kc):
                act.wait_ge(et_tr, jc + 1)
                nc.scalar.copy(aet_hi[:, kc, :], tb[:, 2, :].rearrange("p (k t) -> p k t", k=4)).then_inc(et_hi, 1)

            def job(j):
                def chunk(c, first):
                    jc = j * FE_CHUNKS + c
                    for s in range(RING):
                        split_slot(s, BASE[s] + j * PER_JOB[s] + c)
                    wait_expert_slab(act, 1, j, c + 1)
                    act.wait_ge(e_act, jc + 1)
                    nc.scalar.activation(silu_e[:, :], acc[:, 0, :], ACT.Silu).then_inc(e_silu, 1)
                    if not first:
                        act_out(jc, bass.ds(c * 4 - 4, 4))

                chunk(0, True)
                with act.Fori(1, FE_CHUNKS) as c:
                    chunk(c, False)
                for it in range(4):
                    for s in range(RING if it < 3 else 2):
                        split_slot(s, j * PER_JOB[s] + (BASE[s] + FE_CHUNKS + it))
                    if it == 0:
                        act_out((j + 1) * FE_CHUNKS, slice(24, 28))
                        gather_out(j + 1)
                        act.wait_ge(put_tr, j + 1)
                        nc.scalar.copy(put_t[:, :, :], tb[:, 3, 0:SEQ].rearrange("p (b t) -> p b t", b=NB)).then_inc(put_t_done, 1)

            job_loops(act, lambda j, k: job(j), None)

        @block.gpsimd
        def _(pool):
            pool.wait_ge(consts_in, 16)
            pool.wait_ge(cols_done, 1)
            for n, (k, t) in enumerate(PE_TAPS):
                if n % 2:
                    if n >= DIAGS:
                        pool.wait_ge(diag_used, n - DIAGS + 1)
                    nc.gpsimd.tensor_scalar(diag[:, n % DIAGS, :], ident[:, :], cols[:, k, t:t + 1], None, ALU.mult).then_inc(diag_p, 1)

            G = nc.gpsimd
            state = {"step": 0}

            def step(ins):
                ins.then_inc(pool_step, 1)
                state["step"] += 1
                pool.wait_ge(pool_step, state["step"])

            def total(o, v):
                step(G.tensor_tensor(v[:, 0:4], v[:, 0:4], v[:, 4:8], ALU.add))
                step(G.tensor_tensor(v[:, 0:2], v[:, 0:2], v[:, 2:4], ALU.add))
                step(G.tensor_tensor(o, v[:, 0:1], v[:, 1:2], ALU.add))

            pool.wait_ge(rt_counts, 1)
            full, upto = over[:, 0, :], over[:, 1, :]
            step(G.tensor_scalar(full, over[:, 7, :], float(P), None, ALU.is_gt))
            step(G.tensor_copy(upto[:, 0:1], full[:, 0:1]))
            for e in range(1, NE):
                step(G.tensor_tensor(upto[:, e:e + 1], upto[:, e - 1:e], full[:, e:e + 1], ALU.add))
            for k in range(3):
                mine = over[:, 2 + k, :]
                step(G.tensor_scalar(mine, upto, float(k + 1), None, ALU.is_equal))
                step(G.tensor_tensor(mine, mine, full, ALU.mult))
                step(G.tensor_tensor(over[:, 5, :], mine, iota[:, 0:NE], ALU.mult))
                total(small[:, 40 + k:41 + k], over[:, 5, :])
                for b in range(NB):
                    step(G.tensor_tensor(over[:, 6, :], mine, share[:, b, 0:NE], ALU.mult))
                    total(share[:, b, NE + k:NE + k + 1], over[:, 6, :])
                    step(G.tensor_scalar(over[:, 6, :], rank[:, b, 0:NE], float(-P), None, ALU.add))
                    step(G.tensor_tensor(over[:, 6, :], mine, over[:, 6, :], ALU.mult))
                    total(rank[:, b, NE + k:NE + k + 1], over[:, 6, :])
            step(G.tensor_copy(over_i[:, 0:3], small[:, 40:43]))
            G.tensor_copy(over_i[:, 4:5], upto[:, NE - 1:NE]).then_inc(rt_done, 1)

        @block.vector
        def _(dve):
            V = nc.vector
            state = {"split": 0, "step": 0}

            def step(ins):
                ins.then_inc(dve_step, 1)
                state["step"] += 1

            def settle():
                dve.wait_ge(dve_step, state["step"])

            def split_slot(s, use):
                dve.wait_ge(hi_done[s], use + 1)
                V.tensor_tensor(w_lo[:, s, :], raw[:, s, :], w_hi[:, s, :].bitcast(f32), ALU.subtract).then_inc(lo_done[s], 1)

            def split_to(n):
                while state["split"] < min(n, S_END):
                    i = state["split"]
                    split_slot(i % RING, i // RING)
                    state["split"] += 1

            def norm(n, dst):
                dve.wait_ge(sq_done, n + 1)
                V.tensor_scalar(ms, ss, 1.0 / D, EPS, ALU.mult, ALU.add).then_inc(ms_done, 1)
                dve.wait_ge(sd_done, n + 1)
                step(V.reciprocal(rr, sd))
                settle()
                for b in range(NB):
                    ins = V.tensor_scalar(dst[:, b, :], x[:, b, :], rr[:, b:b + 1], None, ALU.mult)
                return ins

            def to_xt(event, fn):
                for pair in range(4):
                    dve.wait_ge(xt_hi_done, 4 * event + pair + 1)
                    for kk in range(2):
                        k = 2 * pair + kk
                        ins = fn(k, tb[:, pair, kk * SEQ:(kk + 1) * SEQ])
                    ins.then_inc(xt_lo_done, 1)

            def gain_fn(col):
                return lambda k, t: V.scalar_tensor_tensor(xt_lo[:, k, :], t, cols[:, k, col:col + 1],
                                                           xt_hi[:, k, :].bitcast(f32), ALU.mult, ALU.subtract)

            for s0 in (e_act, et_lo, sum_done):
                dve.sem_inc(s0, 1)
            V.memset(ones_row[0:1, :], 1.0).then_inc(pad_done, 1)
            V.memset(u_t[:, :, 0:CONV - 1], 0.0).then_inc(pad_done, 1)
            norm(0, z).then_inc(z_done, 1)
            split_to(2)
            dve.wait_ge(cols_tr, 1)
            V.tensor_scalar(qk_gain[:, 0:NG], acc[:, 1, 0:NG], 1.0, None, ALU.mult)
            V.tensor_scalar(qk_gain[:, NG:2 * NG], acc[:, 1, NG:2 * NG], DH ** -0.5, None, ALU.mult).then_inc(gains_done, 1)
            dve.wait_ge(cols_done, 1)
            to_xt(E_CONV_IN, gain_fn(C_CN))
            split_to(4)

            def conv(*chunks):
                n0, n = CONV * chunks[0], len(chunks)
                for t in range(CONV):
                    for i, k in enumerate(chunks):
                        if t == 0:
                            ins = V.tensor_scalar(conv_t[:, k, :], u_t[:, k, 0:SEQ], cols[:, k, 0:1], cols[:, k, C_DWB:C_DWB + 1], ALU.mult, ALU.add)
                        else:
                            dve.wait_ge(conv_done, n0 + n * (t - 1) + i + 1)
                            ins = V.scalar_tensor_tensor(conv_t[:, k, :], u_t[:, k, t:t + SEQ], cols[:, k, t:t + 1], conv_t[:, k, :], ALU.mult, ALU.add)
                        ins.then_inc(conv_done, 1)

            for c in range(2):
                dve.wait_ge(glu_sig, c + 1)
                V.tensor_tensor(u_tok[:, :, c * 512:c * 512 + 512], acc[:, 0:2, :], sig[:, :, :], ALU.mult).then_inc(glu_u, 1)
                split_to(4 + 4 * c)
                split_to(8 + 4 * c)
                if c == 0:
                    dve.wait_ge(glu_t, 1)
                    conv(0, 1)
                else:
                    dve.wait_ge(glu_t, 3)
                    conv(*range(2, CONV_DVE))
            dve.wait_ge(bias_mm, 1)
            V.tensor_tensor(bias_sb[:, :, :], acc[0:HEADS, 0:NG, 0:BW], mask_sb[:, :, :], ALU.add).then_inc(bias_rows, 1)
            dve.wait_ge(conv_tr, 1)
            for b in range(NB):
                for i in range(2):
                    step(V.bn_stats(bn[:, b, i, :], tb[:, 2 * b + i, :]))
            settle()
            for b in range(NB):
                step(V.bn_aggr(small[:, 12 + 2 * b:14 + 2 * b], bn[:, b, :, :].rearrange("p i s -> p (i s)")))
            settle()
            var = small[:, 12:16].rearrange("p (b i) -> p b i", b=NB)[:, :, 1]
            V.tensor_scalar(ms, var, EPS, None, ALU.add).then_inc(var_done, 1)
            dve.wait_ge(lnsd_done, 1)
            step(V.reciprocal(rr, sd))
            settle()
            for b in range(NB):
                ins = V.tensor_scalar(z[:, b, :], tb[:, 2 * b:2 * b + 2, :].rearrange("p i n -> p (i n)"),
                                      small[:, 12 + 2 * b:13 + 2 * b], rr[:, b:b + 1], ALU.subtract, ALU.mult)
            ins.then_inc(z_done, 1)
            to_xt(E_CONV_OUT, lambda k, t: V.tensor_tensor(xt_lo[:, k, :], act_tmp[:, k, :], xt_hi[:, k, :].bitcast(f32), ALU.subtract))

            def residual(last_slabs):
                for c, i in enumerate(last_slabs):
                    wait_slab(dve, i)
                    V.tensor_tensor(x[:, :, c * 512:c * 512 + 512], x[:, :, c * 512:c * 512 + 512], acc[:, 2 * c:2 * c + 2, :], ALU.add).then_inc(res_done, 1)

            residual((S_WOUT + 1, S_WOUT + 3))
            dve.wait_ge(res_done, 2)
            norm(1, z_b).then_inc(z_done, 1)
            split_to(S_FFN + 2)
            to_xt(E_FFN, gain_fn(C_F0))
            split_to(S_FFN + 4)
            dve.wait_ge(bias_out, 16)
            for c in range(FF_CHUNKS):
                split_to(S_FFN + 4 * c + 6)
                wait_slab(dve, S_FFN + 4 * c + 3)
                dve.wait_ge(ff_silu, c + 1)
                V.tensor_tensor(act_ff[:, :, c * FF_COLS:(c + 1) * FF_COLS], acc[:, 2:4, 0:FF_COLS], silu_ff[:, :, :], ALU.mult).then_inc(ff_act, 1)
                split_to(S_FFN + 4 * c + 8)
            n_down = FF_KC // 2
            for d in range(n_down):
                dve.wait_ge(fft_hi, d + 1)
                for kk, n in ((0, P), (1, P)) if d < n_down - 1 else ((0, P), (1, FF_TAIL)):
                    k = 2 * d + kk
                    ins = V.tensor_tensor(actt_lo[0:n, k, :], tb[0:n, d % 4, kk * SEQ:(kk + 1) * SEQ], actt_hi[0:n, k, :].bitcast(f32), ALU.subtract)
                ins.then_inc(fft_lo, 1)
                if d >= 3:
                    split_to(S_DOWN + d + 2)
            split_to(S_KVQ)
            residual((S_KVQ - 1, S_KVQ - 1))
            dve.wait_ge(res_done, 4)
            norm(2, z_c).then_inc(z_done, 4)
            V.engine_nop().then_inc(res_done, 1)
            split_to(S_KVQ + 2)
            to_xt(E_QKV, gain_fn(C_AN))
            split_to(S_KVQ + 4)
            def project(half):
                for m in range(9):
                    mm = 9 * half + m
                    if m == 3 or (m == 0 and half):
                        to_xt(E_QKV + 2 * half + (m == 3), gain_fn(C_AN if m == 0 else C_KVN))
                    split_to(min(S_KVQ + 2 * mm + 4, S_KVQ + 18 * (half + 1)))
                    if m >= 6:
                        continue
                    n = 6 * half + m
                    bank = 2 * (mm % 2)
                    dve.wait_ge(pr_sq, mm + 1)
                    step(V.tensor_reduce(ss16[:, :, 0:8], sq[:, :, :].rearrange("p b (h d) -> p b h d", d=DH), AX.X, ALU.add))
                    settle()
                    V.tensor_scalar(ms16[:, :, 0:8], ss16[:, :, 0:8], 1.0 / DH, EPS, ALU.mult, ALU.add).then_inc(pr_ms, 1)
                    dve.wait_ge(pr_sd, n + 1)
                    step(V.reciprocal(rr16[:, :, 0:8], sd16[:, :, 0:8]))
                    settle()
                    if n:
                        dve.wait_ge(pr_tr, n)
                    for b in range(NB):
                        ins = V.tensor_tensor(kn[:, b, :].rearrange("p (h d) -> p h d", d=DH), acc[:, bank + b, :].rearrange("p (h d) -> p h d", d=DH),
                                              rr16[:, b, 0:8].unsqueeze(2).to_broadcast([P, 8, DH]), ALU.mult)
                    ins.then_inc(pr_kn, 1)

            def soft(n):
                h, b = n // 2, n % 2
                nk = P * (b + 1)
                dve.wait_ge(at_qk, n + 1)
                if b == 0:
                    dve.wait_ge(bias_t_in[h % 2], 32 * (h // 2 + 1))
                if n >= 2:
                    dve.wait_ge(at_exp, n - 1)
                sc = scores[:, n % 2, 0:NG * nk].rearrange("p (g k) -> p g k", g=NG)
                ps = acc[:, 2 * (n % 2):2 * (n % 2) + 2, :].rearrange("p i (g k) -> p (i g) k", g=2)[:, 0:NG, 0:nk]
                V.tensor_tensor(sc, ps, bias_t[:, h % 2, :, SEQ - nk:SEQ], ALU.add).then_inc(at_add, 1)
                dve.wait_ge(at_add, n + 1)
                V.reduce_max(small[:, 20 + n % 2:21 + n % 2], scores[:, n % 2, 0:NG * nk], AX.X, negate=True).then_inc(at_max, 1)

            def normalise(n):
                nk = P * (n % 2 + 1)
                r = small[:, 28 + n % 4:29 + n % 4]
                dve.wait_ge(at_exp, n + 1)
                step(V.reciprocal(r, small[:, 24 + n % 4:25 + n % 4]))
                settle()
                p = probs[n % 2][:, 0:NG * nk]
                V.tensor_scalar(p, p, r, None, ALU.mult).then_inc(at_norm, 1)

            for half in range(2):
                project(half)
                n0 = nu * half
                soft(n0)
                for n in range(n0, n0 + nu):
                    if n + 1 < n0 + nu:
                        soft(n + 1)
                    normalise(n)
                    if (n - n0) in (4, 6, 8, 10):
                        split_to(S_KVQ + 18 * (half + 1) + (n - n0 - 2) // 2)
            for pair in range(4):
                dve.wait_ge(xt_hi_done, 4 * E_O + pair + 1)
                k2 = slice(2 * pair, 2 * pair + 2)
                V.tensor_tensor(xt_lo[:, k2, :], o_t[:, k2, :], xt_hi[:, k2, :].bitcast(f32), ALU.subtract).then_inc(xt_lo_done, 1)
            residual((S_WO + 1, S_WO + 3))

            dve.wait_ge(res_done, 7)
            norm_ins = norm(3, h_tok)
            step(norm_ins)
            settle()
            dve.wait_ge(tables_in, 48 + 64)
            for b in range(NB):
                ins = V.tensor_tensor(h_tok[:, b, :], h_tok[:, b, :], gain_row[:, :], ALU.mult)
            ins.then_inc(z_done, 1)
            V.memset(ones[:, :], 1.0)
            V.memset(share[:, :, NE:], 0.0)
            step(V.memset(rank[:, :, NE:], 1000.0))
            dve.wait_ge(rt_mm, 1)
            step(V.tensor_copy(logits[:, :, :], acc[:, 0:2, 0:NE]))
            settle()
            for b in range(NB):
                step(V.max(top[:, b, :], logits[:, b, :]))
            settle()
            for b in range(NB):
                step(V.max_index(top_i[:, b, :], top[:, b, :], logits[:, b, :]))
            settle()
            step(V.tensor_copy(top_f[:, :, :], top_i[:, :, :]))
            V.tensor_tensor(gate2[:, :, 0], top[:, :, 1], top[:, :, 0], ALU.subtract).then_inc(rt_v, 1)
            settle()
            for b in range(NB):
                V.tensor_scalar(hot1[:, b, :], iota[:, 0:NE], top_f[:, b, 0:1], None, ALU.is_equal)
                step(V.tensor_scalar(hot2[:, b, :], iota[:, 0:NE], top_f[:, b, 1:2], None, ALU.is_equal))
            settle()
            V.tensor_tensor(chosen[:, :, :], hot1[:, :, :], hot2[:, :, :], ALU.add).then_inc(rt_rank_in, 1)
            dve.wait_ge(rt_e, 1)
            step(V.tensor_scalar(gate2[:, :, 2], gate2[:, :, 1], 1.0, None, ALU.add))
            settle()
            step(V.reciprocal(gate2[:, :, 3], gate2[:, :, 2]))
            settle()
            step(V.tensor_tensor(gate2[:, :, 4], gate2[:, :, 3], gate2[:, :, 1], ALU.mult))
            settle()
            for b in range(NB):
                step(V.tensor_scalar(hot1[:, b, :], hot1[:, b, :], gate2[:, b, 3:4], None, ALU.mult))
            settle()
            for b in range(NB):
                step(V.scalar_tensor_tensor(share[:, b, 0:NE], hot2[:, b, :], gate2[:, b, 4:5], hot1[:, b, :], ALU.mult, ALU.add))
            dve.wait_ge(rt_rank, 1)
            settle()
            step(V.tensor_scalar(hot2[:, :, :], chosen[:, :, :], -1000.0, 1000.0, ALU.mult, ALU.add))
            settle()
            step(V.tensor_tensor(rank[:, :, 0:NE], acc[:, 2, 0:2 * NE].rearrange("p (b e) -> p b e", b=NB), hot2[:, :, :], ALU.add))
            V.tensor_copy(over[:, 7, :], acc[:, 3, 0:NE]).then_inc(rt_counts, 1)
            settle()

            def pick_of(job, value):
                V.tensor_copy(rk_now[:, :].unsqueeze(2), rank[:, :, bass.ds(job, 1)]).then_inc(rk_sem, 1)
                dve.wait_ge(rk_sem, value + 1)
                for b in range(NB):
                    ins = V.tensor_scalar(pick[:, b, :], iota[:, :], rk_now[:, b:b + 1], None, ALU.is_equal)
                ins.then_inc(pick_done, 1)

            def gather_out(job):
                dve.wait_ge(xs_hi_done, job + 1)
                V.tensor_tensor(xs_lo[:, :, :], tb[:, 0:2, :].rearrange("p i (k t) -> p (i k) t", t=P), xs_hi[:, :, :].bitcast(f32), ALU.subtract).then_inc(xs_lo_done, 1)

            pick_of(0, 0)
            gather_out(0)

            def e_mult(j, c):
                jc = j * FE_CHUNKS + c + 1
                wait_expert_slab(dve, 3, j, c + 1)
                dve.wait_ge(e_silu, jc + 1)
                dve.wait_ge(et_tr, jc)
                V.tensor_tensor(act_e[:, :], acc[:, 1, :], silu_e[:, :], ALU.mult).then_inc(e_act, 1)

            def act_out(jc, kc):
                dve.wait_ge(et_hi, jc)
                V.tensor_tensor(aet_lo[:, kc, :], tb[:, 2, :].rearrange("p (k t) -> p k t", k=4), aet_hi[:, kc, :].bitcast(f32), ALU.subtract).then_inc(et_lo, 1)

            def take_y(j):
                wait_expert_slab(dve, 1, j, 0)
                V.tensor_copy(y_e[:, :], acc[:, 2:4, :].rearrange("p i n -> p (i n)")).then_inc(y_done, 1)

            def add_sum(j):
                dve.wait_ge(sc_mm, j + 1)
                V.tensor_tensor(x[:, :, :].rearrange("p b d -> p (b d)"), x[:, :, :].rearrange("p b d -> p (b d)"),
                                tb[:, :, :].rearrange("p i n -> p (i n)"), ALU.add).then_inc(sum_done, 1)

            def job(j):
                def chunk(c, first):
                    jc = j * FE_CHUNKS + c
                    for s in range(2):
                        split_slot(s, BASE[s] + j * PER_JOB[s] + c)
                    if first:
                        take_y(j)
                    else:
                        e_mult(j, c - 1)
                    for s in range(2, 4):
                        split_slot(s, BASE[s] + j * PER_JOB[s] + c)
                    if first:
                        add_sum(j)
                    else:
                        act_out(jc, bass.ds(c * 4 - 4, 4))

                chunk(0, True)
                with dve.Fori(1, FE_CHUNKS) as c:
                    chunk(c, False)
                V.tensor_copy(sh_now[:, :].unsqueeze(2), share[:, :, bass.ds(j, 1)]).then_inc(sh_sem, 1)
                dve.wait_ge(sh_sem, j + 1)
                dve.wait_ge(pick_done, j + 1)
                for b in range(NB):
                    ins = V.tensor_scalar(put[:, b, :], pick[:, b, :], sh_now[:, b:b + 1], None, ALU.mult)
                ins.then_inc(put_done, 1)
                dve.wait_ge(put_done, j + 1)
                dve.wait_ge(rt_done, 1)
                pick_of(j + 1, j + 1)
                for it in range(4):
                    for s in range(RING if it < 3 else 2):
                        split_slot(s, j * PER_JOB[s] + (BASE[s] + FE_CHUNKS + it))
                        if it == 0 and s == 1:
                            e_mult(j, FE_CHUNKS - 1)
                    if it == 0:
                        act_out((j + 1) * FE_CHUNKS, slice(24, 28))
                        gather_out(j + 1)

            n_jobs = job_loops(dve, lambda j, k: job(j), None)
            take_y(n_jobs)
            add_sum(n_jobs)

        return


def kernel(**inputs):
    import concourse.bacc as bacc
    from concourse.bass_utils import run_bass_kernel_spmd

    nc = bacc.Bacc("TRN2", target_bir_lowering=False, num_devices=1)
    arrays = {k: np.ascontiguousarray(v) for k, v in inputs.items()}
    arrays.update(host_constants())
    feed, args = {}, {}
    for name, v in arrays.items():
        feed["in_" + name] = v
        args[name] = nc.dram_tensor("in_" + name, v.shape, mybir.dt.from_np(v.dtype), kind="ExternalInput").ap()
    out = nc.dram_tensor("out_0", (1, SEQ, D), mybir.dt.float32, kind="ExternalOutput").ap()
    build(nc, args, out)
    r = run_bass_kernel_spmd(nc, [feed], core_ids=[0])
    return r.results[0]["out_0"]
```

```python
from contextlib import ExitStack
import math

import numpy as np
import concourse.bass as bass
from concourse import mybir

P = 128
D = 1024
SEQ = 256
NB = SEQ // P
KC = D // P
CONV = 31
HEADS = 16
DH = 64
GROUPS = ((128, 1), (512, 4), (2048, 16))
NG = len(GROUPS)
QW = NG * HEADS * DH
BUCKETS = 32
MAX_DISTANCE = 2048
FF = 2752
FF_COLS = 344
FF_CHUNKS = FF // FF_COLS
FF_KC = -(-FF // P)
FF_TAIL = FF - (FF_KC - 1) * P
NE = 8
FE = 3584
FE_CHUNKS = FE // 512
FE_KC = FE // P
EPS = 1e-6
NEG = -1e30
CONV_DVE = 5
DIAGS = 8
RING = 4
SLAB = 2048
BW = 384
COPIES = 64

S_WIN = 0
S_WOUT = S_WIN + 8
S_FFN = S_WOUT + 4
S_DOWN = S_FFN + 4 * FF_CHUNKS
S_KVQ = S_DOWN + FF_KC // 2
S_WO = S_KVQ + 2 * 18
S_END = S_WO + 4
BASE = [(S_END - s + RING - 1) // RING for s in range(RING)]
JOB_SLABS = 4 * FE_CHUNKS + FE_KC // 2
MAX_JOBS = NE + 4


def host_constants():
    ident = np.eye(P, dtype=np.float32)
    before = np.triu(np.ones((P, P), np.float32), 1)
    iota = np.tile(np.arange(P, dtype=np.float32), (P, 1))
    dist = 255 - np.arange(BW)
    exact = BUCKETS // 2
    n = np.clip(dist, 0, None)
    large = exact + (np.log(np.maximum(n, 1) / exact) / np.log(MAX_DISTANCE / exact)
                     * (BUCKETS - exact)).astype(np.int32)
    bucket = np.where(n < exact, n, np.minimum(large, BUCKETS - 1))
    hot = (bucket[None, :] == np.arange(BUCKETS)[:, None])
    ok = np.zeros((NG, BW), bool)
    for g, (window, d) in enumerate(GROUPS):
        ok[g] = (dist >= 0) & (dist <= window) & (dist % d == 0) & (dist // d <= P)
    hots = np.zeros((BUCKETS, NG, BW), np.float32)
    mask = np.zeros((HEADS, NG, BW), np.float32)
    for g in range(NG):
        hots[:, g] = hot & ok[g][None, :]
        mask[:, g] = np.where(ok[g], 0.0, NEG)[None, :]
    return {"c_ident": ident, "c_before": before, "c_iota": iota,
            "c_hot": hots, "c_mask": mask}


def build(nc, a, out):
    f32, f32r, u32 = mybir.dt.float32, mybir.dt.float32r, mybir.dt.uint32
    i32 = mybir.dt.int32
    ALU, ACT, AX = mybir.AluOpType, mybir.ActivationFunctionType, mybir.AxisListType

    scratch_bias = nc.dram_tensor("bias_rows", (COPIES, HEADS, NG, BW), f32).ap()

    with ExitStack() as ctx:
        def sb(name, shape, dt=f32, where=ctx):
            return where.enter_context(nc.sbuf_tensor("sb_" + name, shape, dt))

        def sem(name):
            return ctx.enter_context(nc.semaphore(name))

        raw = sb("raw", [P, RING, SLAB])
        w_hi = sb("w_hi", [P, RING, SLAB], f32r)
        w_lo = sb("w_lo", [P, RING, SLAB], f32r)
        x = sb("x", [P, NB, D])
        xt_hi = sb("xt_hi", [P, KC, SEQ], f32r)
        xt_lo = sb("xt_lo", [P, KC, SEQ], f32r)
        ident = sb("ident", [P, P])
        small = sb("small", [P, 64])
        ss, ms, sd, rr = (small[:, 2 * i:2 * i + 2] for i in range(4))
        ss_c = [small[:, 34:36], small[:, 36:38]]
        cols = sb("cols", [P, KC, 40])
        qk_gain = sb("qk_gain", [P, 8])
        ss16, ms16, sd16, rr16 = (sb(f"h16_{i}", [P, 2, 16]) for i in range(4))
        def phase():
            return ExitStack()

        with phase() as ph:
            z = sb("z", [P, NB, D], where=ph)
            vec_rows = sb("vec_rows", [40, D], where=ph)
            kq_rows = sb("kq_rows", [8, P], where=ph)
            bin_row = sb("bin_row", [1, 2 * D], where=ph)
            ones_row = sb("ones_row", [1, P], where=ph)
            ones_r = sb("ones_r", [1, P], f32r, where=ph)
            row_hi = sb("row_hi", [1, D], f32r, where=ph)
            row_lo = sb("row_lo", [1, D], f32r, where=ph)
            sig = sb("sig", [P, NB, 512], where=ph)
            u_tok = sb("u_tok", [P, NB, D], where=ph)
            u_t = sb("u_t", [P, KC, CONV - 1 + SEQ], where=ph)
            diag = sb("diag", [P, DIAGS, P], where=ph)
            conv_t = sb("conv_t", [P, KC, SEQ], where=ph)
            act_tmp = sb("act_tmp", [P, KC, SEQ], where=ph)
            bout_row = act_tmp[0:1, :, :].rearrange("p k t -> p (k t)")[:, 0:D]
            bn = sb("bn", [P, NB, 2, 6], where=ph)
            hot_sb = sb("hot_sb", [BUCKETS, NG, BW], where=ph)
            rel_sb = sb("rel_sb", [BUCKETS, NG * HEADS], where=ph)
            mask_sb = sb("mask_sb", [HEADS, NG, BW], where=ph)
            bias_sb = sb("bias_sb", [HEADS, NG, BW], where=ph)
        with phase() as ph:
            z_b = sb("z_b", [P, NB, D], where=ph)
            silu_ff = sb("silu_ff", [P, NB, FF_COLS], where=ph)
            act_ff = sb("act_ff", [P, NB, FF], where=ph)
            actt_hi = sb("actt_hi", [P, FF_KC, SEQ], f32r, where=ph)
            actt_lo = sb("actt_lo", [P, FF_KC, SEQ], f32r, where=ph)
        with phase() as ph:
            z_c = sb("z_c", [P, NB, D], where=ph)
            k_t = sb("k_t", [P, NG * 4, SEQ], where=ph)
            q_t = sb("q_t", [P, NG * 4, SEQ], where=ph)
            v_tok = sb("v_tok", [P, NB, QW // 2], where=ph)
            kn = sb("kn", [P, NB, 512], where=ph)
            sq = sb("sq", [P, NB, 512], where=ph)
            bias_t = sb("bias_t", [P, 2, NG, SEQ], where=ph)
            scores = sb("scores", [P, 2, NG * SEQ], where=ph)
            probs_t = sb("probs_t", [P, 2, NG, 3 * P], where=ph)
            o_t = sb("o_t", [P, KC, SEQ], where=ph)
        probs = [kn[:, :, :].rearrange("p b d -> p (b d)")[:, 0:NG * SEQ],
                 sq[:, :, :].rearrange("p b d -> p (b d)")[:, 0:NG * SEQ]]
        with phase() as ph:
            h_tok = sb("h_tok", [P, NB, D], where=ph)
            h_t = sb("h_t", [P, KC, SEQ], where=ph)
            gain_row = sb("gain_row", [P, D], where=ph)
            router = sb("router", [P, KC, NE], where=ph)
            xs_hi = sb("xs_hi", [P, KC, P], f32r, where=ph)
            xs_lo = sb("xs_lo", [P, KC, P], f32r, where=ph)
            silu_e = sb("silu_e", [P, 512], where=ph)
            act_e = sb("act_e", [P, 512], where=ph)
            aet_hi = sb("aet_hi", [P, FE_KC, P], f32r, where=ph)
            aet_lo = sb("aet_lo", [P, FE_KC, P], f32r, where=ph)
            y_e = sb("y_e", [P, D], where=ph)
            pick = sb("pick", [P, NB, P], where=ph)
            put = sb("put", [P, NB, P], where=ph)
            put_t = sb("put_t", [P, NB, P], where=ph)
            iota = sb("iota", [P, P], where=ph)
            before = sb("before", [P, P], where=ph)
            ones = sb("ones", [P, P], where=ph)
            logits = sb("logits", [P, NB, NE], where=ph)
            top = sb("top", [P, NB, 8], where=ph)
            top_i = sb("top_i", [P, NB, 8], u32, where=ph)
            top_f = sb("top_f", [P, NB, 8], where=ph)
            gate2 = sb("gate2", [P, NB, 8], where=ph)
            hot1 = sb("hot1", [P, NB, NE], where=ph)
            hot2 = sb("hot2", [P, NB, NE], where=ph)
            chosen = sb("chosen", [P, NB, NE], where=ph)
            rank = sb("rank", [P, NB, MAX_JOBS], where=ph)
            share = sb("share", [P, NB, MAX_JOBS], where=ph)
            over = sb("over", [P, 8, NE], where=ph)
            job_list = sb("job_list", [P, 16], i32, where=ph)
            rk_now = sb("rk_now", [P, NB], where=ph)
            sh_now = sb("sh_now", [P, NB], where=ph)

        acc = ctx.enter_context(nc.psum_tensor("acc", [P, 4, 512], f32))
        tb = ctx.enter_context(nc.psum_tensor("tb", [P, 4, 512], f32))

        raw_in = [sem(f"raw_in{s}") for s in range(RING)]
        hi_done = [sem(f"hi_done{s}") for s in range(RING)]
        lo_done = [sem(f"lo_done{s}") for s in range(RING)]
        slab_used = [sem(f"slab_used{s}") for s in range(RING)]
        x_in, consts_in, rows_in, heads_in = sem("x_in"), sem("consts_in"), sem("rows_in"), sem("heads_in")
        bias_in, bout_in = sem("bias_in"), sem("bout_in")
        row_hi_done, row_lo_done = sem("row_hi_done"), sem("row_lo_done")
        tables_in = sem("tables_in")
        cols_tr, cols_done, gains_done = sem("cols_tr"), sem("cols_done"), sem("gains_done")
        bias_mm, bias_rows, bias_out = sem("bias_mm"), sem("bias_rows"), sem("bias_out")
        sq_done, ms_done, sd_done, z_done = sem("sq_done"), sem("ms_done"), sem("sd_done"), sem("z_done")
        xt_tr, xt_hi_done, xt_lo_done = sem("xt_tr"), sem("xt_hi_done"), sem("xt_lo_done")
        act_step, dve_step, pool_step = sem("act_step"), sem("dve_step"), sem("pool_step")
        pad_done = sem("pad_done")
        glu_sig, glu_u, glu_tr, glu_t = sem("glu_sig"), sem("glu_u"), sem("glu_tr"), sem("glu_t")
        diag_a, diag_p, diag_used, conv_mm, conv_out = (sem(n) for n in ("diag_a", "diag_p", "diag_used", "conv_mm", "conv_out"))
        conv_done, conv_tr, var_done, lnsd_done = sem("conv_done"), sem("conv_tr"), sem("var_done"), sem("lnsd_done")
        res_done = sem("res_done")
        ff_silu, ff_act = sem("ff_silu"), sem("ff_act")
        fft_tr, fft_hi, fft_lo = sem("fft_tr"), sem("fft_hi"), sem("fft_lo")
        pr_sq, pr_ms, pr_sd, pr_kn, pr_tr, pr_t = (sem(n) for n in
            ("pr_sq", "pr_ms", "pr_sd", "pr_kn", "pr_tr", "pr_t"))
        bias_t_in = [sem("bias_t_in0"), sem("bias_t_in1")]
        at_qk, at_add, at_max, at_exp, at_norm, at_tr, at_ta, at_pv, at_o = (sem(n) for n in
            ("at_qk", "at_add", "at_max", "at_exp", "at_norm", "at_tr", "at_ta", "at_pv", "at_o"))
        rt_mm, rt_v, rt_e, rt_rank_in, rt_rank, rt_counts, rt_done = (sem(n) for n in
            ("rt_mm", "rt_v", "rt_e", "rt_rank_in", "rt_rank", "rt_counts", "rt_done"))
        ht_done = sem("ht_done")
        pick_done, put_done, rk_sem, sh_sem = sem("pick_done"), sem("put_done"), sem("rank_taken"), sem("share_taken")
        gather_mm, xs_hi_done, xs_lo_done = sem("gather_mm"), sem("xs_hi_done"), sem("xs_lo_done")
        e_silu, e_act = sem("e_silu"), sem("e_act")
        et_tr, et_hi, et_lo = sem("et_tr"), sem("et_hi"), sem("et_lo")
        put_tr, put_t_done = sem("put_tr"), sem("put_t_done")
        y_done, sc_mm, sum_done = sem("y_done"), sem("sc_mm"), sem("sum_done")
        out_done = sem("out_done")

        C_DWB, C_CN, C_LG, C_LB, C_KVN, C_AN, C_F0 = range(CONV, CONV + 7)
        NCOL = CONV + 7


        def wait_slab(eng, i):
            eng.wait_ge(slab_used[i % RING], i // RING + 1)

        class Job:
            def __init__(self, j, turn, use):
                self.j, self.turn, self.use = j, turn, use

            def slot(self, q):
                return (q + 2 * self.turn) % RING

            def gate_up(self, q, c):
                s = self.slot(q)
                return s, self.use[s] + c

            def down(self, d):
                s = self.slot(d)
                return s, self.use[s] + (FE_CHUNKS + d // RING)

            def next(self):
                slabs = [sum(self.slot(q) == s for q in range(JOB_SLABS)) for s in range(RING)]
                return Job(self.j + 1, 1 - self.turn, [self.use[s] + slabs[s] for s in range(RING)])

        FIRST_JOB = Job(0, 0, BASE)

        def wait_multiplied(eng, slot_use):
            s, use = slot_use
            eng.wait_ge(slab_used[s], use + 1)

        PE_TAPS = [(k, t) for k in range(CONV_DVE, KC) for t in range(CONV)]

        def slab_view(t, s, k, n):
            return t[:, s, 0:k * n].rearrange("p (k n) -> p k n", k=k)

        def w_src(w, k0, k, c0, n):
            return w[k0 * P:(k0 + k) * P, c0:c0 + n].rearrange("(k p) n -> p k n", p=P)

        def fixed_slabs():
            w_in, w_out = a["conv_w_in"][0], a["conv_w_out"][0]
            for c in range(2):
                for half in range(2):
                    for kh in range(2):
                        yield w_src(w_in, 4 * kh, 4, D * half + 512 * c, 512), 4, 512
            for c in range(2):
                for kh in range(2):
                    yield w_src(w_out, 4 * kh, 4, 512 * c, 512), 4, 512
            for c in range(FF_CHUNKS):
                for w in (a["ffn_w_gate"][0], a["ffn_w_up"][0]):
                    for kh in range(2):
                        yield w_src(w, 4 * kh, 4, FF_COLS * c, FF_COLS), 4, FF_COLS
            for d in range(FF_KC // 2):
                yield (w_src(a["ffn_w_down"][0], 2 * d, 2, 0, D) if d < FF_KC // 2 - 1 else None), 2, D
            for half in range(2):
                for w, c0 in ((a["w_q"][0], 0), (a["w_kv"], 0), (a["w_kv"], QW)):
                    for g in range(NG):
                        for kh in range(2):
                            yield w_src(w, 4 * kh, 4, c0 + g * D + 512 * half, 512), 4, 512
            for c in range(2):
                for kh in range(2):
                    yield w_src(a["w_o"][0], 4 * kh, 4, 512 * c, 512), 4, 512

        JOB_COUNT = 15

        def job_loops(eng, body):
            per_pair = 2 * JOB_SLABS // RING
            with eng.Fori(0, NE // 2) as i:
                job = Job(i * 2, 0, [i * per_pair + BASE[s] for s in range(RING)])
                body(job)
                body(job.next())
            eng.wait_ge(rt_done, 1)
            n_over = eng.value_load(job_list[0:1, JOB_COUNT:JOB_COUNT + 1], min_val=0, max_val=3)
            done = [BASE[s] + NE // 2 * per_pair for s in range(RING)]
            slabs = [sum(FIRST_JOB.slot(q) == s for q in range(JOB_SLABS)) for s in range(RING)]
            with eng.If(n_over > 0):
                with eng.Fori(0, n_over) as k:
                    body(Job(k + NE, 0, [k * slabs[s] + done[s] for s in range(RING)]), further=True)
            return Job(n_over + NE, 0, [n_over * slabs[s] + done[s] for s in range(RING)])

        bin_second = bin_row[0:1, :].rearrange("o (h c n) -> o h c n", h=2, c=2)[:, :, 1, :]

        block = ctx.enter_context(nc.Block())

        def use_bytes(s, use):
            i = S_DOWN + FF_KC // 2 - 1
            if isinstance(use, int):
                extra = 16 if (s == i % RING and use >= i // RING) else 0
                return 16 * (use + 1) + extra
            return use * 16 + (16 + (16 if s == i % RING else 0))

        @block.sync
        def _(sp):
            sp.dma_start(x[:, :, :], a["x"][0].rearrange("(b p) d -> p b d", p=P)).then_inc(x_in, 16)
            rows = [(a["conv_dw_b"], C_DWB), (a["conv_norm"], C_CN), (a["conv_ln_g"], C_LG), (a["conv_ln_b"], C_LB),
                    (a["kv_norm"].rearrange("(o d) -> o d", o=1), C_KVN), (a["attn_norm"], C_AN), (a["ffn_norm"][0:1], C_F0)]
            sp.dma_start(vec_rows[0:CONV, :], a["conv_dw_w"][0]).then_inc(rows_in, 16)
            for src, r in rows:
                sp.dma_start(vec_rows[r:r + 1, :], src).then_inc(rows_in, 16)
            slabs = list(fixed_slabs())
            assert len(slabs) == S_END

            def load(i):
                s, use = i % RING, i // RING
                src, k, n = slabs[i]
                if use:
                    sp.wait_ge(lo_done[s], use)
                if src is None:
                    w = a["ffn_w_down"][0]
                    k0 = FF_KC - 2
                    sp.dma_start(raw[:, s, 0:D], w[k0 * P:(k0 + 1) * P, :]).then_inc(raw_in[s], 16)
                    sp.dma_start(raw[0:FF_TAIL, s, D:2 * D], w[(k0 + 1) * P:FF, :]).then_inc(raw_in[s], 16)
                else:
                    sp.dma_start(slab_view(raw, s, k, n), src).then_inc(raw_in[s], 16)

            for i in range(RING):
                load(i)
            sp.dma_start(bout_row[0:1, :], a["conv_b_out"]).then_inc(bout_in, 16)
            sp.dma_start(rel_sb[:, :], a["rel_bias"]).then_inc(tables_in, 16)
            sp.dma_start(hot_sb[:, :, :], a["c_hot"]).then_inc(tables_in, 16)
            sp.dma_start(mask_sb[:, :, :], a["c_mask"]).then_inc(tables_in, 16)
            for i in range(4, S_FFN):
                load(i)
            sp.wait_ge(bias_rows, 1)
            sp.dma_start(scratch_bias.rearrange("c h g w -> h c (g w)"),
                         bias_sb[:, :, :].rearrange("h g w -> h (g w)").unsqueeze(1).to_broadcast([HEADS, COPIES, NG * BW])).then_inc(bias_out, 16)
            for i in range(S_FFN, S_KVQ + 18):
                load(i)
            sp.wait_ge(bias_out, 16)

            def load_bias(h):
                if h >= 2:
                    sp.wait_ge(at_add, 2 * (h - 1))
                for top_row in range(0, P, COPIES):
                    src = bass.AP(scratch_bias.tensor, h * NG * BW + P - 1 - top_row,
                                  [[HEADS * NG * BW - 1, COPIES], [BW, NG], [1, SEQ]])
                    sp.dma_start(bias_t[top_row:top_row + COPIES, h % 2, :, :], src).then_inc(bias_t_in[h % 2], 16)

            sp.wait_ge(res_done, 5)
            load_bias(0)
            load_bias(1)
            first = S_KVQ + 18
            for i in range(first, first + RING):
                load(i)
            for h in range(2, 8):
                load_bias(h)
                if h in (4, 6):
                    load(first + RING + (h - 4) // 2)
            for i in range(first + RING + 2, S_WO):
                load(i)
            load_bias(8)
            load_bias(9)
            for i in range(S_WO, S_END):
                load(i)

            def load_expert_slab(s, use, src, k, n):
                sp.wait_ge(lo_done[s], use)
                sp.dma_start(slab_view(raw, s, k, n), src).then_inc(raw_in[s], 16)

            for h in range(10, HEADS):
                load_bias(h)
            def gate_up_slab(job, expert, q, c):
                w = a[("moe_w_gate", "moe_w_up")[q // 2]][0, bass.ds(expert, 1)].rearrange("o k n -> (o k) n")
                kh = q % 2
                load_expert_slab(*job.gate_up(q, c), w[kh * 512:(kh + 1) * 512, bass.ds(c * 512, 512)].rearrange("(k p) n -> p k n", p=P), 4, 512)

            def job_loads(job, further=False):
                expert = sp.value_load(job_list[0:1, bass.ds(job.j, 1)], min_val=0, max_val=NE - 1) if further else job.j
                for q in range(2, 4):
                    gate_up_slab(job, expert, q, 0)
                with sp.Fori(1, FE_CHUNKS) as c:
                    for q in range(4):
                        gate_up_slab(job, expert, q, c)
                wd = a["moe_w_down"][0, bass.ds(expert, 1)].rearrange("o k n -> (o k) n")
                for d in range(FE_KC // 2):
                    load_expert_slab(*job.down(d), wd[2 * d * P:(2 * d + 2) * P, :].rearrange("(k p) n -> p k n", p=P), 2, D)
                after = job.next() if not further else Job(job.j + 1, 0, job.next().use)
                sp.wait_ge(rt_done, 1)
                expert = sp.value_load(job_list[0:1, bass.ds(after.j, 1)], min_val=0, max_val=NE - 1)
                for q in range(2):
                    gate_up_slab(after, expert, q, 0)

            for q in range(2):
                gate_up_slab(FIRST_JOB, 0, q, 0)
            end = job_loops(sp, job_loads)
            for b in range(NB):
                sp.wait_ge(sum_done, end.j + (2 + b))
                sp.dma_start(out[0, b * P:(b + 1) * P], x[:, b, :]).then_inc(out_done, 16)
            sp.wait_ge(out_done, 16 * NB)

        E_CONV_IN, E_CONV_OUT, E_FFN, E_QKV, _, _, _, E_O = range(8)
        nu = HEADS

        @block.tensor
        def _(pe):
            def transpose(o, i):
                n = i.shape[0]
                return nc.tensor.transpose(o, i, ident[0:n, 0:n])

            def three(o, hi_x, lo_x, hi_w, lo_w, start, stop):
                nc.tensor.matmul(o, hi_x, hi_w, start=start, stop=False)
                nc.tensor.matmul(o, hi_x, lo_w, start=False, stop=False)
                return nc.tensor.matmul(o, lo_x, hi_w, start=False, stop=stop)

            def slab_mm(i, k0, k, n, first, last, outs, xh=xt_hi, xl=xt_lo, rows=None):
                s, use = i % RING, i // RING
                pe.wait_ge(lo_done[s], use + 1)
                wh, wl = slab_view(w_hi, s, k, n), slab_view(w_lo, s, k, n)
                for kk in range(k):
                    r = slice(0, P if rows is None else rows[kk])
                    for tok, col, o in outs:
                        ins = three(o, xh[r, k0 + kk, tok], xl[r, k0 + kk, tok], wh[r, kk, col], wl[r, kk, col],
                                    first and kk == 0, last and kk == k - 1)
                ins.then_inc(slab_used[s], 1)
                return ins

            def blocks(bank, n):
                return [(slice(P * b, P * b + P), slice(0, n), acc[:, bank + b, 0:n]) for b in range(NB)]

            def to_xt(event, src):
                if event:
                    pe.wait_ge(xt_lo_done, 4 * event)
                pe.wait_ge(z_done, event + 1)
                for pair in range(4):
                    for kk in range(2):
                        for b in range(NB):
                            k = 2 * pair + kk
                            ins = transpose(tb[:, pair, kk * SEQ + b * P:kk * SEQ + b * P + P], src[:, b, k * P:k * P + P])
                    ins.then_inc(xt_tr, 1)

            def bin_products(c, half):
                for b in range(NB):
                    nc.tensor.matmul(acc[:, 2 * half + b, :], ones_row[0:1, :],
                                     bin_row[0:1, half * D + c * 512:half * D + c * 512 + 512], start=True, stop=False)

            def row_products(bank, col):
                for b in range(NB):
                    for part in (row_hi, row_lo):
                        nc.tensor.matmul(acc[:, bank + b, :], ones_r[0:1, :], part[0:1, col:col + 512], start=part is row_hi, stop=False)

            pe.sem_inc(et_tr, 1)
            pe.wait_ge(bias_in, 16)
            pe.wait_ge(pad_done, 3)
            bin_products(0, 0)
            pe.wait_ge(consts_in, 16)
            pe.wait_ge(rows_in, 16 * 8)
            pe.wait_ge(heads_in, 16 * 4)
            for k in range(KC):
                transpose(acc[:, 2, k * 40:k * 40 + NCOL], vec_rows[0:NCOL, k * P:k * P + P])
            transpose(acc[:, 3, 0:2 * NG], kq_rows[0:2 * NG, :]).then_inc(cols_tr, 1)

            to_xt(E_CONV_IN, z)
            pe.wait_ge(cols_done, 1)
            pe.wait_ge(gains_done, 1)
            bin_products(0, 1)
            for c in range(2):
                for half in range(2):
                    for kh in range(2):
                        if c == 0 and half == 0:
                            pe.wait_ge(xt_lo_done, 4 * E_CONV_IN + 2 * kh + 2)
                        ins = slab_mm(S_WIN + 4 * c + 2 * half + kh, 4 * kh, 4, 512, False, kh == 1, blocks(2 * half, 512))
                if c == 0:
                    pe.wait_ge(glu_sig, 1)
                    pe.wait_ge(row_lo_done, 1)
                    row_products(2, 512)
                pe.wait_ge(glu_u, c + 1)
                for pair in range(2):
                    for kk in range(2):
                        for b in range(NB):
                            k = 4 * c + 2 * pair + kk
                            ins = transpose(tb[:, 2 * c + pair, kk * SEQ + b * P:kk * SEQ + b * P + P], u_tok[:, b, k * P:k * P + P])
                    ins.then_inc(glu_tr, 1)
                if c == 0:
                    row_products(0, 0)
            pe.wait_ge(glu_t, 4)
            for n, (k, t) in enumerate(PE_TAPS):
                pe.wait_ge(diag_p if n % 2 else diag_a, n // 2 + 1)
                ins = nc.tensor.matmul(acc[:, k - CONV_DVE, 0:SEQ], diag[:, n % DIAGS, :], u_t[:, k, t:t + SEQ],
                                       start=t == 0, stop=t == CONV - 1)
                ins.then_inc(diag_used, 1)
                if t == CONV - 1:
                    pe.wait_ge(diag_used, n + 1)
                    pe.sem_inc(conv_mm, 1)
            pe.wait_ge(conv_out, KC - CONV_DVE)
            pe.wait_ge(conv_done, CONV * CONV_DVE)
            for b in range(NB):
                for k in range(KC):
                    ins = transpose(tb[:, 2 * b + k // 4, (k % 4) * P:(k % 4) * P + P], conv_t[:, k, b * P:b * P + P])
                ins.then_inc(conv_tr, 1)
            pe.wait_ge(tables_in, 48)
            for g in range(NG):
                ins = nc.tensor.matmul(acc[0:HEADS, g, 0:BW], rel_sb[:, g * HEADS:(g + 1) * HEADS], hot_sb[:, g, :],
                                       start=True, stop=True)
            ins.then_inc(bias_mm, 1)
            to_xt(E_CONV_OUT, z)
            pe.wait_ge(bias_rows, 1)

            def residual_product(s0, event, with_row=False):
                pe.wait_ge(xt_lo_done, 4 * event + 2)
                for c in range(2):
                    if with_row:
                        row_products(2 * c, 512 * c)
                    for kh in range(2):
                        if c == 0 and kh:
                            pe.wait_ge(xt_lo_done, 4 * (event + 1))
                        ins = slab_mm(s0 + 2 * c + kh, 4 * kh, 4, 512, not with_row and kh == 0, kh == 1, blocks(2 * c, 512))

            pe.wait_ge(row_lo_done, 2)
            residual_product(S_WOUT, E_CONV_OUT, True)

            def ff_transposes(d):
                pe.wait_ge(ff_act, (min(FF, 2 * P * (d + 1)) + FF_COLS - 1) // FF_COLS)
                if d >= 4:
                    pe.wait_ge(fft_lo, d - 3)
                for kk in range(2):
                    k = 2 * d + kk
                    n = min(P, FF - k * P)
                    for b in range(NB):
                        ins = transpose(tb[0:n, d % 4, kk * SEQ + b * P:kk * SEQ + b * P + P], act_ff[:, b, k * P:k * P + n])
                ins.then_inc(fft_tr, 1)

            pe.wait_ge(res_done, 2)
            to_xt(E_FFN, z_b)
            for c in range(FF_CHUNKS):
                i = S_FFN + 4 * c
                if c:
                    pe.wait_ge(ff_silu, c)
                for kh in range(2):
                    if c == 0:
                        pe.wait_ge(xt_lo_done, 4 * E_FFN + 2 * kh + 2)
                    slab_mm(i + kh, 4 * kh, 4, FF_COLS, kh == 0, kh == 1, blocks(0, FF_COLS))
                if c == FF_CHUNKS - 1:
                    for d in range(3):
                        ff_transposes(d)
                if c:
                    pe.wait_ge(ff_act, c)
                for kh in range(2):
                    slab_mm(i + 2 + kh, 4 * kh, 4, FF_COLS, kh == 0, kh == 1, blocks(2, FF_COLS))
            halves = [(slice(P * b, P * b + P), slice(512 * c, 512 * c + 512), acc[:, 2 * c + b, :]) for c in range(2) for b in range(NB)]
            n_down = FF_KC // 2
            for d in range(n_down):
                if d + 3 < n_down:
                    ff_transposes(d + 3)
                pe.wait_ge(fft_lo, d + 1)
                if d == 0:
                    pe.wait_ge(ff_act, FF_CHUNKS)
                slab_mm(S_DOWN + d, 2 * d, 2, D, d == 0, d == n_down - 1, halves, actt_hi, actt_lo,
                        [P, P if d < n_down - 1 else FF_TAIL])

            pe.wait_ge(res_done, 4)

            def head_transposes(half, m):
                n = 6 * half + m
                pe.wait_ge(pr_kn, n + 1)
                if n >= 2:
                    pe.wait_ge(pr_t, n - 1)
                for kk in range(4):
                    for b in range(NB):
                        ins = transpose(tb[:, 2 * (n % 2) + kk // 2, (kk % 2) * SEQ + b * P:(kk % 2) * SEQ + b * P + P],
                                        kn[:, b, kk * P:kk * P + P])
                ins.then_inc(pr_tr, 1)

            def project(half):
                for m in range(9):
                    mm = 9 * half + m
                    event = E_QKV + 2 * half + (m == 3)
                    if m in (0, 3):
                        if m == 3:
                            pe.wait_ge(pr_t, 6 * half + 2)
                        to_xt(event, z_c)
                    if m >= 2:
                        if m - 2 < 6:
                            pe.wait_ge(pr_kn, 6 * half + m - 1)
                        else:
                            pe.wait_ge(pr_sq, mm - 1)
                    for kh in range(2):
                        if m in (0, 3):
                            pe.wait_ge(xt_lo_done, 4 * event + 2 * kh + 2)
                        slab_mm(S_KVQ + 2 * mm + kh, 4 * kh, 4, 512, kh == 0, kh == 1, blocks(2 * (mm % 2), 512))
                    if 1 <= m <= 6:
                        head_transposes(half, m - 1)

            def qk(n):
                h, b = (n // 2) % 8, n % 2
                if n >= 2:
                    pe.wait_ge(at_add, n - 1)
                half = slice(DH * (h % 2), DH * (h % 2) + DH)
                nk = P * (b + 1)
                for g in range(NG):
                    t = g * 4 + h // 2
                    o = acc[:, 2 * (n % 2) + g // 2, (g % 2) * SEQ:(g % 2) * SEQ + nk]
                    ins = nc.tensor.matmul(o, q_t[half, t, b * P:b * P + P], k_t[half, t, 0:nk], start=True, stop=True)
                ins.then_inc(at_qk, 1)

            def probs_transposes(n):
                b = n % 2
                pe.wait_ge(at_norm, n + 1)
                if n:
                    pe.wait_ge(at_ta, n)
                nk = P * (b + 1)
                for q in range(NG * (b + 1)):
                    ins = transpose(tb[:, q // 4, (q % 4) * P:(q % 4) * P + P], probs[n % 2][:, q * P:q * P + P])
                ins.then_inc(at_tr, 1)

            def pv(head):
                h = head % 8
                pe.wait_ge(at_ta, 2 * head + 2)
                if head >= 4:
                    pe.wait_ge(at_o, head // 2 - 1)
                pt = probs_t[:, head % 2, :, :]
                o = tb[DH * (h % 2):DH * (h % 2) + DH, 2 + (h // 2) % 2, 0:SEQ]
                for g in range(NG):
                    v = slice(g * 512 + h * DH, g * 512 + h * DH + DH)
                    nc.tensor.matmul(o, v_tok[:, 0, v], pt[:, g, 0:SEQ], start=g == 0, stop=False)
                    ins = nc.tensor.matmul(o[:, P:SEQ], v_tok[:, 1, v], pt[:, g, SEQ:SEQ + P], start=False, stop=g == NG - 1)
                ins.then_inc(at_pv, 1)

            for half in range(2):
                project(half)
                pe.wait_ge(pr_t, 6 * (half + 1))
                pe.wait_ge(pr_kn, 6 * (half + 1))
                n0 = nu * half
                pe.wait_ge(pr_sq, 9 * (half + 1))
                qk(n0)
                qk(n0 + 1)
                for n in range(n0, n0 + nu):
                    if n + 2 < n0 + nu:
                        qk(n + 2)
                    if n > n0:
                        probs_transposes(n - 1)
                    if n % 2 and n - n0 >= 3:
                        pv((n - 3) // 2)
                probs_transposes(n0 + nu - 1)
                pv((n0 + nu) // 2 - 1)
                pe.wait_ge(at_o, 4 * (half + 1))
            residual_product(S_WO, E_O)

            pe.wait_ge(z_done, E_O + 1)
            pe.wait_ge(xt_lo_done, 4 * (E_O + 1))
            for pair in range(4):
                for kk in range(2):
                    for b in range(NB):
                        k = 2 * pair + kk
                        ins = transpose(tb[:, pair, kk * SEQ + b * P:kk * SEQ + b * P + P], h_tok[:, b, k * P:k * P + P])
            ins.then_inc(xt_tr, 1)
            pe.wait_ge(ht_done, 1)
            for b in range(NB):
                for k in range(KC):
                    ins = nc.tensor.matmul(acc[:, b, 0:NE], h_t[:, k, b * P:b * P + P], router[:, k, :],
                                           start=k == 0, stop=k == KC - 1)
            ins.then_inc(rt_mm, 1)
            pe.wait_ge(rt_rank_in, 1)
            nc.tensor.matmul(acc[:, 2, 0:NE], before[:, :], chosen[:, 0, :], start=True, stop=True)
            nc.tensor.matmul(acc[:, 2, 8:8 + NE], ones[:, :], chosen[:, 0, :], start=True, stop=False, skip_group_check=True)
            nc.tensor.matmul(acc[:, 2, 8:8 + NE], before[:, :], chosen[:, 1, :], start=False, stop=True, skip_group_check=True)
            nc.tensor.matmul(acc[:, 3, 0:NE], ones[:, :], chosen[:, 0, :], start=True, stop=False)
            nc.tensor.matmul(acc[:, 3, 0:NE], ones[:, :], chosen[:, 1, :], start=False, stop=True).then_inc(rt_rank, 1)

            def gather(job):
                pe.wait_ge(pick_done, job + 1)
                for k in range(KC):
                    for b in range(NB):
                        ins = nc.tensor.matmul(tb[:, k // 4, (k % 4) * P:(k % 4) * P + P], h_tok[:, b, k * P:k * P + P],
                                               pick[:, b, :], start=b == 0, stop=b == NB - 1)
                ins.then_inc(gather_mm, 1)

            gather(0)

            def expert_slab(slot_use, xh, xl, k0, k, n, first, last, outs):
                s, use = slot_use
                pe.wait_ge(lo_done[s], use + 1)
                wh, wl = slab_view(w_hi, s, k, n), slab_view(w_lo, s, k, n)
                for kk in range(k):
                    for col, o in outs:
                        ins = three(o, xh[:, k0 + kk, :], xl[:, k0 + kk, :], wh[:, kk, col], wl[:, kk, col],
                                    first and kk == 0, last and kk == k - 1)
                ins.then_inc(slab_used[s], 1)

            def act_transposes(jc):
                pe.wait_ge(e_act, jc + 1)
                pe.wait_ge(et_lo, jc)
                for q in range(4):
                    ins = transpose(tb[:, 2, q * P:q * P + P], act_e[:, q * P:q * P + P])
                ins.then_inc(et_tr, 1)

            def scatter(j, last=False):
                pe.wait_ge(y_done, j + 1)
                pe.wait_ge(put_t_done, j + 1)
                for b in range(NB):
                    for c in range(2):
                        ins = nc.tensor.matmul(tb[:, 2 * b + c, :], put_t[:, b, :], y_e[:, c * 512:c * 512 + 512], start=True, stop=True)
                    if last or b == NB - 1:
                        ins.then_inc(sc_mm, 1)

            def job_products(job, further=False):
                j = job.j
                col = slice(0, 512)
                pe.wait_ge(xs_lo_done, j + 1)

                def chunk(c, first):
                    jc = j * FE_CHUNKS + c
                    pe.wait_ge(e_silu, jc + 1)
                    for q in range(2):
                        expert_slab(job.gate_up(q, c), xs_hi, xs_lo, 4 * q, 4, 512, q == 0, q == 1, [(col, acc[:, 0, :])])
                    if first:
                        scatter(j)
                    else:
                        pe.wait_ge(sum_done, j + 2)
                        act_transposes(jc)
                    pe.wait_ge(e_act, jc + 1)
                    for q in range(2):
                        expert_slab(job.gate_up(2 + q, c), xs_hi, xs_lo, 4 * q, 4, 512, q == 0, q == 1, [(col, acc[:, 1, :])])

                chunk(0, True)
                with pe.Fori(1, FE_CHUNKS) as c:
                    chunk(c, False)
                outs = [(slice(512 * c, 512 * c + 512), acc[:, 2 + c, :]) for c in range(2)]
                n_down = FE_KC // 2
                for d in range(n_down):
                    if d == 2:
                        act_transposes((j + 1) * FE_CHUNKS)
                        gather(j + 1)
                        pe.wait_ge(put_done, j + 1)
                        for b in range(NB):
                            ins = transpose(tb[:, 3, b * P:b * P + P], put[:, b, :])
                        ins.then_inc(put_tr, 1)
                    if d == n_down - 2:
                        pe.wait_ge(et_lo, (j + 1) * FE_CHUNKS + 1)
                    expert_slab(job.down(d), aet_hi, aet_lo, 2 * d, 2, D, d == 0, d == n_down - 1, outs)

            scatter(job_loops(pe, job_products).j, last=True)

        @block.scalar
        def _(act):
            state = {"split": 0, "step": 0}

            def step(ins):
                ins.then_inc(act_step, 1)
                state["step"] += 1

            def settle():
                act.wait_ge(act_step, state["step"])

            def split_slot(s, use):
                act.wait_ge(raw_in[s], use_bytes(s, use))
                if not (isinstance(use, int) and use == 0):
                    act.wait_ge(slab_used[s], use)
                nc.scalar.copy(w_hi[:, s, :], raw[:, s, :]).then_inc(hi_done[s], 1)

            def split_to(n):
                while state["split"] < min(n, S_END):
                    i = state["split"]
                    split_slot(i % RING, i // RING)
                    state["split"] += 1

            def to_xt(event, fn):
                for pair in range(4):
                    act.wait_ge(xt_tr, 4 * event + pair + 1)
                    for kk in range(2):
                        k = 2 * pair + kk
                        ins = fn(k, tb[:, pair, kk * SEQ:(kk + 1) * SEQ])
                    ins.then_inc(xt_hi_done, 1)

            def gain_fn(col):
                return lambda k, t: nc.scalar.activation(xt_hi[:, k, :], t, ACT.Copy, scale=cols[:, k, col:col + 1])

            def warm(func):
                nc.scalar.activation(small[:, 32:33], small[:, 33:34], func)

            def norm_stats(n, scr):
                for c in range(2):
                    if n:
                        act.wait_ge(res_done, (0, 1, 3, 6)[n] + c)
                    for b in range(NB):
                        col = slice(c * 512, c * 512 + 512)
                        ins = nc.scalar.activation(scr[:, b, col], x[:, b, col], ACT.Square, accum_out=ss_c[c][:, b:b + 1])
                    ins.then_inc(sq_done, 1)
                act.wait_ge(ms_done, n + 1)
                nc.scalar.activation(sd, ms, ACT.Sqrt).then_inc(sd_done, 1)

            act.dma_start(ident[:, :], a["c_ident"]).then_inc(consts_in, 16)
            act.dma_start(bin_row[0:1, :], a["conv_b_in"]).then_inc(bias_in, 16)
            for half in range(2):
                act.dma_start(kq_rows[0:NG, DH * half:DH * half + DH], a["k_norm"]).then_inc(heads_in, 16)
                act.dma_start(kq_rows[NG:2 * NG, DH * half:DH * half + DH], a["q_norm"][0]).then_inc(heads_in, 16)
            act.sem_inc(e_silu, 1)
            def conv_chunk_out(k):
                act.wait_ge(conv_mm, k - CONV_DVE + 1)
                nc.scalar.activation(conv_t[:, k, :], acc[:, k - CONV_DVE, 0:SEQ], ACT.Identity,
                                     bias=cols[:, k, C_DWB:C_DWB + 1]).then_inc(conv_out, 1)

            act.wait_ge(pad_done, 3)
            warm(ACT.Sqrt)
            act.wait_ge(x_in, 16)
            norm_stats(0, z)
            act.wait_ge(cols_tr, 1)
            nc.scalar.copy(cols[:, :, 0:NCOL], acc[:, 2, 0:KC * 40].rearrange("p (k c) -> p k c", k=KC)[:, :, 0:NCOL]).then_inc(cols_done, 1)
            act.wait_ge(cols_done, 1)
            act.wait_ge(gains_done, 1)
            split_to(1)
            to_xt(E_CONV_IN, gain_fn(C_CN))
            split_to(4)
            nc.scalar.copy(ones_r[0:1, :], ones_row[0:1, :])
            nc.scalar.copy(row_hi[0:1, :].rearrange("o (h n) -> o h n", h=2), bin_second).then_inc(row_hi_done, 1)

            def diag_out(n):
                k, t = PE_TAPS[n]
                if n >= DIAGS:
                    act.wait_ge(diag_used, n - DIAGS + 1)
                nc.scalar.activation(diag[:, n % DIAGS, :], ident[:, :], ACT.Copy, scale=cols[:, k, t:t + 1]).then_inc(diag_a, 1)

            for c in range(2):
                if c:
                    for n in range(0, DIAGS, 2):
                        diag_out(n)
                split_to(4 * c + 7)
                wait_slab(act, S_WIN + 4 * c + 3)
                nc.scalar.activation(sig[:, :, :], acc[:, 2:4, :], ACT.Sigmoid).then_inc(glu_sig, 1)
                for pair in range(2):
                    act.wait_ge(glu_tr, 2 * c + pair + 1)
                    k = 4 * c + 2 * pair
                    nc.scalar.copy(u_t[:, k:k + 2, CONV - 1:], tb[:, 2 * c + pair, :].rearrange("p (k t) -> p k t", k=2)).then_inc(glu_t, 1)
                if c == 0:
                    split_to(8)
            for n, (k, t) in enumerate(PE_TAPS):
                if n % 2 == 0 and n >= DIAGS:
                    diag_out(n)
                if n == 2 * DIAGS:
                    split_to(S_WOUT + 4)
                if n == 6 * DIAGS:
                    act.wait_ge(bout_in, 16)
                    nc.scalar.copy(row_hi[0:1, :], bout_row[0:1, :]).then_inc(row_hi_done, 1)
                if t == 8 and k > CONV_DVE:
                    conv_chunk_out(k - 1)
            conv_chunk_out(KC - 1)
            act.wait_ge(var_done, 1)
            nc.scalar.activation(sd, ms, ACT.Sqrt).then_inc(lnsd_done, 1)
            act.wait_ge(row_lo_done, 2)
            for pair in range(4):
                act.wait_ge(xt_tr, 4 * E_CONV_OUT + pair + 1)
                for kk in range(2):
                    k = 2 * pair + kk
                    step(nc.scalar.activation(act_tmp[:, k, :], tb[:, pair, kk * SEQ:(kk + 1) * SEQ], ACT.Silu,
                                              scale=cols[:, k, C_LG:C_LG + 1], bias=cols[:, k, C_LB:C_LB + 1]))
                settle()
                nc.scalar.copy(xt_hi[:, 2 * pair:2 * pair + 2, :], act_tmp[:, 2 * pair:2 * pair + 2, :]).then_inc(xt_hi_done, 1)
            warm(ACT.Sqrt)
            norm_stats(1, z_b)
            split_to(S_FFN + 2)
            to_xt(E_FFN, gain_fn(C_F0))
            split_to(S_FFN + 4)
            n_down = FF_KC // 2

            def ff_hi(d):
                act.wait_ge(fft_tr, d + 1)
                if d < n_down - 1:
                    nc.scalar.copy(actt_hi[:, 2 * d:2 * d + 2, :], tb[:, d % 4, :].rearrange("p (k t) -> p k t", k=2)).then_inc(fft_hi, 1)
                else:
                    nc.scalar.copy(actt_hi[:, 2 * d, :], tb[:, d % 4, 0:SEQ])
                    nc.scalar.copy(actt_hi[0:FF_TAIL, 2 * d + 1, :], tb[0:FF_TAIL, d % 4, SEQ:2 * SEQ]).then_inc(fft_hi, 1)

            for c in range(FF_CHUNKS):
                wait_slab(act, S_FFN + 4 * c + 1)
                if c:
                    act.wait_ge(ff_act, c)
                nc.scalar.activation(silu_ff[:, :, :], acc[:, 0:2, 0:FF_COLS], ACT.Silu).then_inc(ff_silu, 1)
                if c == FF_CHUNKS - 1:
                    for d in range(3):
                        ff_hi(d)
                split_to(S_FFN + 4 * c + 8)
            for d in range(3, n_down):
                ff_hi(d)
                split_to(S_DOWN + d + 2)
            split_to(S_KVQ)
            warm(ACT.Sqrt)
            norm_stats(2, z_c)
            split_to(S_KVQ + 2)
            to_xt(E_QKV, gain_fn(C_AN))
            split_to(S_KVQ + 4)

            def heads_out(half, m):
                n = 6 * half + m
                g = m % 3
                dst, gain = (q_t, qk_gain[:, NG + g:NG + g + 1]) if m < 3 else (k_t, qk_gain[:, g:g + 1])
                act.wait_ge(pr_tr, n + 1)
                for i in range(2):
                    k0 = 4 * g + 2 * i
                    ins = nc.scalar.activation(dst[:, k0:k0 + 2, :], tb[:, 2 * (n % 2) + i, :].rearrange("p (k t) -> p k t", k=2),
                                               ACT.Copy, scale=gain)
                ins.then_inc(pr_t, 1)

            def project(half):
                for m in range(9):
                    mm = 9 * half + m
                    if m == 3 or (m == 0 and half):
                        to_xt(E_QKV + 2 * half + (m == 3), gain_fn(C_AN if m == 0 else C_KVN))
                    split_to(min(S_KVQ + 2 * mm + 4, S_KVQ + 18 * (half + 1)))
                    wait_slab(act, S_KVQ + 2 * mm + 1)
                    bank = 2 * (mm % 2)
                    if m >= 6:
                        nc.scalar.copy(v_tok[:, :, (m - 6) * 512:(m - 5) * 512], acc[:, bank:bank + 2, :]).then_inc(pr_sq, 1)
                        if m == 6:
                            heads_out(half, 5)
                        continue
                    n = 6 * half + m
                    if n:
                        act.wait_ge(pr_ms, n)
                    nc.scalar.activation(sq[:, :, :], acc[:, bank:bank + 2, :], ACT.Square).then_inc(pr_sq, 1)
                    act.wait_ge(pr_ms, n + 1)
                    nc.scalar.activation(sd16[:, :, 0:8], ms16[:, :, 0:8], ACT.Sqrt).then_inc(pr_sd, 1)
                    if m:
                        heads_out(half, m - 1)

            def probs_out(n):
                b, head = n % 2, n // 2
                act.wait_ge(at_tr, n + 1)
                if head >= 2:
                    act.wait_ge(at_pv, head - 1)
                nk = P * (b + 1)
                nc.scalar.copy(probs_t[:, head % 2, :, b * P:b * P + nk],
                               tb[:, 0:2, :].rearrange("p i n -> p (i n)")[:, 0:NG * nk].rearrange("p (g k) -> p g k", g=NG)).then_inc(at_ta, 1)

            def o_hi(pair):
                act.wait_ge(at_o, 2 * pair + 2)
                nc.scalar.copy(xt_hi[:, 2 * pair:2 * pair + 2, :], o_t[:, 2 * pair:2 * pair + 2, :]).then_inc(xt_hi_done, 1)

            def o_out(pair):
                act.wait_ge(at_pv, 2 * pair + 2)
                nc.scalar.copy(o_t[:, pair, :], tb[:, 2 + pair % 2, 0:SEQ]).then_inc(at_o, 1)

            for half in range(2):
                project(half)
                n0 = nu * half
                for n in range(n0, n0 + nu):
                    nk = P * (n % 2 + 1)
                    act.wait_ge(at_max, n + 1)
                    if n >= 2:
                        act.wait_ge(at_tr, n - 1)
                    nc.scalar.activation(probs[n % 2][:, 0:NG * nk], scores[:, n % 2, 0:NG * nk], ACT.Exp,
                                         bias=small[:, 20 + n % 2:21 + n % 2], accum_out=small[:, 24 + n % 4:25 + n % 4]).then_inc(at_exp, 1)
                    if n > n0:
                        probs_out(n - 1)
                    if (n - n0) % 4 == 2 and n - n0 >= 6:
                        o_out((n - 6) // 4)
                    if (n - n0) in (4, 9, 14):
                        split_to(S_KVQ + 18 * (half + 1) + (n - n0 + 1) // 5)
                    if half and (n - n0) in (2, 6, 12):
                        o_hi((2, 6, 12).index(n - n0))
                probs_out(n0 + nu - 1)
                o_out((n0 + nu) // 4 - 1)
            o_hi(3)
            split_to(S_END)
            warm(ACT.Sqrt)
            act.wait_ge(res_done, 7)
            nc.scalar.dma_start(gain_row[:, :], a["ffn_norm"][1:2].to_broadcast([P, D])).then_inc(tables_in, 16)
            nc.scalar.dma_start(router[:, :, :], a["moe_router"][0].rearrange("(k p) e -> p k e", p=P)).then_inc(tables_in, 16)
            nc.scalar.dma_start(iota[:, :], a["c_iota"]).then_inc(tables_in, 16)
            nc.scalar.dma_start(before[:, :], a["c_before"]).then_inc(tables_in, 16)
            norm_stats(3, h_tok)
            for q in range(2):
                split_slot(*FIRST_JOB.gate_up(q, 0))
            act.wait_ge(xt_tr, 4 * E_O + 1)
            for i in range(4):
                ins = nc.scalar.copy(h_t[:, 2 * i:2 * i + 2, :], tb[:, i, :].rearrange("p (k t) -> p k t", k=2))
            ins.then_inc(ht_done, 1)
            nc.scalar.memzero(put_t[:, :, :]).then_inc(put_t_done, 1)
            act.wait_ge(rt_v, 1)
            nc.scalar.activation(gate2[:, :, 1], gate2[:, :, 0], ACT.Exp).then_inc(rt_e, 1)

            def gather_out(job):
                act.wait_ge(gather_mm, job + 1)
                nc.scalar.copy(xs_hi[:, :, :], tb[:, 0:2, :].rearrange("p i (k t) -> p (i k) t", t=P)).then_inc(xs_hi_done, 1)

            gather_out(0)

            def act_out(jc, kc):
                act.wait_ge(et_tr, jc + 1)
                nc.scalar.copy(aet_hi[:, kc, :], tb[:, 2, :].rearrange("p (k t) -> p k t", k=4)).then_inc(et_hi, 1)

            def job_rounding(job, further=False):
                j = job.j

                def chunk(c, first):
                    jc = j * FE_CHUNKS + c
                    for q in range(2 if first else 0, 4):
                        split_slot(*job.gate_up(q, c))
                    wait_multiplied(act, job.gate_up(1, c))
                    act.wait_ge(e_act, jc + 1)
                    nc.scalar.activation(silu_e[:, :], acc[:, 0, :], ACT.Silu).then_inc(e_silu, 1)
                    if not first:
                        act_out(jc, bass.ds(c * 4 - 4, 4))

                chunk(0, True)
                with act.Fori(1, FE_CHUNKS) as c:
                    chunk(c, False)
                for d in range(FE_KC // 2):
                    split_slot(*job.down(d))
                    if d == 3:
                        act_out((j + 1) * FE_CHUNKS, slice(24, 28))
                        gather_out(j + 1)
                        act.wait_ge(put_tr, j + 1)
                        nc.scalar.copy(put_t[:, :, :], tb[:, 3, 0:SEQ].rearrange("p (b t) -> p b t", b=NB)).then_inc(put_t_done, 1)

                after = job.next() if not further else Job(j + 1, 0, job.next().use)
                for q in range(2):
                    split_slot(*after.gate_up(q, 0))

            job_loops(act, job_rounding)

        @block.gpsimd
        def _(pool):
            pool.wait_ge(consts_in, 16)
            pool.wait_ge(cols_done, 1)
            for n, (k, t) in enumerate(PE_TAPS):
                if n % 2:
                    if n >= DIAGS:
                        pool.wait_ge(diag_used, n - DIAGS + 1)
                    nc.gpsimd.tensor_scalar(diag[:, n % DIAGS, :], ident[:, :], cols[:, k, t:t + 1], None, ALU.mult).then_inc(diag_p, 1)

            G = nc.gpsimd
            state = {"step": 0}

            def step(ins):
                ins.then_inc(pool_step, 1)
                state["step"] += 1
                pool.wait_ge(pool_step, state["step"])

            def total(o, v):
                step(G.tensor_tensor(v[:, 0:4], v[:, 0:4], v[:, 4:8], ALU.add))
                step(G.tensor_tensor(v[:, 0:2], v[:, 0:2], v[:, 2:4], ALU.add))
                step(G.tensor_tensor(o, v[:, 0:1], v[:, 1:2], ALU.add))

            pool.wait_ge(rt_counts, 1)
            full, upto = over[:, 0, :], over[:, 1, :]
            step(G.tensor_scalar(full, over[:, 7, :], float(P), None, ALU.is_gt))
            step(G.tensor_copy(upto[:, 0:1], full[:, 0:1]))
            for e in range(1, NE):
                step(G.tensor_tensor(upto[:, e:e + 1], upto[:, e - 1:e], full[:, e:e + 1], ALU.add))
            for k in range(3):
                mine = over[:, 2 + k, :]
                step(G.tensor_scalar(mine, upto, float(k + 1), None, ALU.is_equal))
                step(G.tensor_tensor(mine, mine, full, ALU.mult))
                step(G.tensor_tensor(over[:, 5, :], mine, iota[:, 0:NE], ALU.mult))
                total(small[:, 40 + k:41 + k], over[:, 5, :])
                for b in range(NB):
                    step(G.tensor_tensor(over[:, 6, :], mine, share[:, b, 0:NE], ALU.mult))
                    total(share[:, b, NE + k:NE + k + 1], over[:, 6, :])
                    step(G.tensor_scalar(over[:, 6, :], rank[:, b, 0:NE], float(-P), None, ALU.add))
                    step(G.tensor_tensor(over[:, 6, :], mine, over[:, 6, :], ALU.mult))
                    total(rank[:, b, NE + k:NE + k + 1], over[:, 6, :])
            step(G.memset(job_list[:, NE + 3:], 0))
            step(G.tensor_copy(job_list[:, 0:NE], iota[:, 0:NE]))
            step(G.tensor_copy(job_list[:, NE:NE + 3], small[:, 40:43]))
            G.tensor_copy(job_list[:, JOB_COUNT:JOB_COUNT + 1], upto[:, NE - 1:NE]).then_inc(rt_done, 1)

        @block.vector
        def _(dve):
            V = nc.vector
            state = {"split": 0, "step": 0}

            def step(ins):
                ins.then_inc(dve_step, 1)
                state["step"] += 1

            def settle():
                dve.wait_ge(dve_step, state["step"])

            def split_slot(s, use):
                dve.wait_ge(hi_done[s], use + 1)
                V.tensor_tensor(w_lo[:, s, :], raw[:, s, :], w_hi[:, s, :].bitcast(f32), ALU.subtract).then_inc(lo_done[s], 1)

            def split_to(n):
                while state["split"] < min(n, S_END):
                    i = state["split"]
                    split_slot(i % RING, i // RING)
                    state["split"] += 1

            def norm_scale(n):
                dve.wait_ge(sq_done, 2 * n + 1)
                step(V.tensor_scalar(ss, ss_c[0], 1.0 / D, EPS, ALU.mult, ALU.add))
                dve.wait_ge(sq_done, 2 * n + 2)
                settle()
                V.scalar_tensor_tensor(ms, ss_c[1], 1.0 / D, ss, ALU.mult, ALU.add).then_inc(ms_done, 1)
                dve.wait_ge(sd_done, n + 1)
                step(V.reciprocal(rr, sd))
                settle()

            def norm(n, dst):
                norm_scale(n)
                for b in range(NB):
                    ins = V.tensor_scalar(dst[:, b, :], x[:, b, :], rr[:, b:b + 1], None, ALU.mult)
                return ins

            def to_xt(event, fn):
                for pair in range(4):
                    dve.wait_ge(xt_hi_done, 4 * event + pair + 1)
                    for kk in range(2):
                        k = 2 * pair + kk
                        ins = fn(k, tb[:, pair, kk * SEQ:(kk + 1) * SEQ])
                    ins.then_inc(xt_lo_done, 1)

            def gain_fn(col):
                return lambda k, t: V.scalar_tensor_tensor(xt_lo[:, k, :], t, cols[:, k, col:col + 1],
                                                           xt_hi[:, k, :].bitcast(f32), ALU.mult, ALU.subtract)

            for s0 in (e_act, et_lo, sum_done):
                dve.sem_inc(s0, 1)
            V.memset(small[:, 33:34], 1.0).then_inc(pad_done, 1)
            V.memset(ones_row[0:1, :], 1.0).then_inc(pad_done, 1)
            V.memset(u_t[:, :, 0:CONV - 1], 0.0).then_inc(pad_done, 1)
            norm(0, z).then_inc(z_done, 1)
            dve.wait_ge(cols_tr, 1)
            V.tensor_scalar(qk_gain[:, 0:NG], acc[:, 3, 0:NG], 1.0, None, ALU.mult)
            V.tensor_scalar(qk_gain[:, NG:2 * NG], acc[:, 3, NG:2 * NG], DH ** -0.5, None, ALU.mult).then_inc(gains_done, 1)
            dve.wait_ge(cols_done, 1)
            split_to(1)
            to_xt(E_CONV_IN, gain_fn(C_CN))
            split_to(4)

            def glu(c):
                dve.wait_ge(glu_sig, c + 1)
                V.tensor_tensor(u_tok[:, :, c * 512:c * 512 + 512], acc[:, 0:2, :], sig[:, :, :], ALU.mult).then_inc(glu_u, 1)

            def conv(*chunks, glu_at=None):
                n0, n = CONV * chunks[0], len(chunks)
                for t in range(CONV):
                    if t == glu_at:
                        glu(1)
                    for i, k in enumerate(chunks):
                        if t == 0:
                            ins = V.tensor_scalar(conv_t[:, k, :], u_t[:, k, 0:SEQ], cols[:, k, 0:1], cols[:, k, C_DWB:C_DWB + 1], ALU.mult, ALU.add)
                        else:
                            dve.wait_ge(conv_done, n0 + n * (t - 1) + i + 1)
                            ins = V.scalar_tensor_tensor(conv_t[:, k, :], u_t[:, k, t:t + SEQ], cols[:, k, t:t + 1], conv_t[:, k, :], ALU.mult, ALU.add)
                        ins.then_inc(conv_done, 1)

            dve.wait_ge(row_hi_done, 1)
            V.tensor_tensor(row_lo[0:1, :].rearrange("o (h n) -> o h n", h=2), bin_second,
                            row_hi[0:1, :].bitcast(f32).rearrange("o (h n) -> o h n", h=2), ALU.subtract).then_inc(row_lo_done, 1)
            split_to(7)
            glu(0)
            split_to(8)
            dve.wait_ge(glu_t, 1)
            conv(0, 1, glu_at=23)
            dve.wait_ge(glu_t, 3)
            conv(*range(2, CONV_DVE))
            dve.wait_ge(row_hi_done, 2)
            V.tensor_tensor(row_lo[0:1, :], bout_row[0:1, :], row_hi[0:1, :].bitcast(f32), ALU.subtract).then_inc(row_lo_done, 1)
            split_to(S_WOUT + 2)
            for b in range(NB):
                dve.wait_ge(conv_tr, b + 1)
                for i in range(2):
                    step(V.bn_stats(bn[:, b, i, :], tb[:, 2 * b + i, :]))
            settle()
            for b in range(NB):
                step(V.bn_aggr(small[:, 12 + 2 * b:14 + 2 * b], bn[:, b, :, :].rearrange("p i s -> p (i s)")))
            settle()
            var = small[:, 12:16].rearrange("p (b i) -> p b i", b=NB)[:, :, 1]
            V.tensor_scalar(ms, var, EPS, None, ALU.add).then_inc(var_done, 1)
            dve.wait_ge(lnsd_done, 1)
            step(V.reciprocal(rr, sd))
            settle()
            for b in range(NB):
                ins = V.tensor_scalar(z[:, b, :], tb[:, 2 * b:2 * b + 2, :].rearrange("p i n -> p (i n)"),
                                      small[:, 12 + 2 * b:13 + 2 * b], rr[:, b:b + 1], ALU.subtract, ALU.mult)
            ins.then_inc(z_done, 1)
            dve.wait_ge(bias_mm, 1)
            V.tensor_tensor(bias_sb[:, :, :], acc[0:HEADS, 0:NG, 0:BW], mask_sb[:, :, :], ALU.add).then_inc(bias_rows, 1)
            to_xt(E_CONV_OUT, lambda k, t: V.tensor_tensor(xt_lo[:, k, :], act_tmp[:, k, :], xt_hi[:, k, :].bitcast(f32), ALU.subtract))
            split_to(S_WOUT + 4)

            def residual(last_slabs):
                for c, i in enumerate(last_slabs):
                    wait_slab(dve, i)
                    V.tensor_tensor(x[:, :, c * 512:c * 512 + 512], x[:, :, c * 512:c * 512 + 512], acc[:, 2 * c:2 * c + 2, :], ALU.add).then_inc(res_done, 1)

            residual((S_WOUT + 1, S_WOUT + 3))
            dve.wait_ge(res_done, 2)
            norm(1, z_b).then_inc(z_done, 1)
            split_to(S_FFN + 2)
            to_xt(E_FFN, gain_fn(C_F0))
            split_to(S_FFN + 4)
            dve.wait_ge(bias_out, 16)
            n_down = FF_KC // 2

            def ff_lo(d):
                dve.wait_ge(fft_hi, d + 1)
                for kk, n in ((0, P), (1, P)) if d < n_down - 1 else ((0, P), (1, FF_TAIL)):
                    k = 2 * d + kk
                    ins = V.tensor_tensor(actt_lo[0:n, k, :], tb[0:n, d % 4, kk * SEQ:(kk + 1) * SEQ], actt_hi[0:n, k, :].bitcast(f32), ALU.subtract)
                ins.then_inc(fft_lo, 1)

            for c in range(FF_CHUNKS):
                if c == FF_CHUNKS - 1:
                    for d in range(3):
                        ff_lo(d)
                split_to(S_FFN + 4 * c + 6)
                wait_slab(dve, S_FFN + 4 * c + 3)
                dve.wait_ge(ff_silu, c + 1)
                V.tensor_tensor(act_ff[:, :, c * FF_COLS:(c + 1) * FF_COLS], acc[:, 2:4, 0:FF_COLS], silu_ff[:, :, :], ALU.mult).then_inc(ff_act, 1)
                split_to(S_FFN + 4 * c + 8)
            for d in range(3, n_down):
                ff_lo(d)
                split_to(S_DOWN + d + 2)
            split_to(S_KVQ)
            residual((S_KVQ - 1, S_KVQ - 1))
            dve.wait_ge(res_done, 4)
            norm(2, z_c).then_inc(z_done, 4)
            V.engine_nop().then_inc(res_done, 1)
            split_to(S_KVQ + 2)
            to_xt(E_QKV, gain_fn(C_AN))
            split_to(S_KVQ + 4)
            def project(half):
                for m in range(9):
                    mm = 9 * half + m
                    if m == 3 or (m == 0 and half):
                        to_xt(E_QKV + 2 * half + (m == 3), gain_fn(C_AN if m == 0 else C_KVN))
                    split_to(min(S_KVQ + 2 * mm + 4, S_KVQ + 18 * (half + 1)))
                    if m >= 6:
                        continue
                    n = 6 * half + m
                    bank = 2 * (mm % 2)
                    dve.wait_ge(pr_sq, mm + 1)
                    step(V.tensor_reduce(ss16[:, :, 0:8], sq[:, :, :].rearrange("p b (h d) -> p b h d", d=DH), AX.X, ALU.add))
                    settle()
                    V.tensor_scalar(ms16[:, :, 0:8], ss16[:, :, 0:8], 1.0 / DH, EPS, ALU.mult, ALU.add).then_inc(pr_ms, 1)
                    dve.wait_ge(pr_sd, n + 1)
                    step(V.reciprocal(rr16[:, :, 0:8], sd16[:, :, 0:8]))
                    settle()
                    if n:
                        dve.wait_ge(pr_tr, n)
                    for b in range(NB):
                        ins = V.tensor_tensor(kn[:, b, :].rearrange("p (h d) -> p h d", d=DH), acc[:, bank + b, :].rearrange("p (h d) -> p h d", d=DH),
                                              rr16[:, b, 0:8].unsqueeze(2).to_broadcast([P, 8, DH]), ALU.mult)
                    ins.then_inc(pr_kn, 1)

            def soft(n):
                h, b = n // 2, n % 2
                nk = P * (b + 1)
                dve.wait_ge(at_qk, n + 1)
                if b == 0:
                    dve.wait_ge(bias_t_in[h % 2], 32 * (h // 2 + 1))
                if n >= 2:
                    dve.wait_ge(at_exp, n - 1)
                sc = scores[:, n % 2, 0:NG * nk].rearrange("p (g k) -> p g k", g=NG)
                ps = acc[:, 2 * (n % 2):2 * (n % 2) + 2, :].rearrange("p i (g k) -> p (i g) k", g=2)[:, 0:NG, 0:nk]
                V.tensor_tensor(sc, ps, bias_t[:, h % 2, :, SEQ - nk:SEQ], ALU.add).then_inc(at_add, 1)
                dve.wait_ge(at_add, n + 1)
                V.reduce_max(small[:, 20 + n % 2:21 + n % 2], scores[:, n % 2, 0:NG * nk], AX.X, negate=True).then_inc(at_max, 1)

            def normalise(n):
                nk = P * (n % 2 + 1)
                r = small[:, 28 + n % 4:29 + n % 4]
                dve.wait_ge(at_exp, n + 1)
                step(V.reciprocal(r, small[:, 24 + n % 4:25 + n % 4]))
                settle()
                p = probs[n % 2][:, 0:NG * nk]
                V.tensor_scalar(p, p, r, None, ALU.mult).then_inc(at_norm, 1)

            def o_lo(pair):
                dve.wait_ge(xt_hi_done, 4 * E_O + pair + 1)
                k2 = slice(2 * pair, 2 * pair + 2)
                V.tensor_tensor(xt_lo[:, k2, :], o_t[:, k2, :], xt_hi[:, k2, :].bitcast(f32), ALU.subtract).then_inc(xt_lo_done, 1)

            for half in range(2):
                project(half)
                n0 = nu * half
                soft(n0)
                for n in range(n0, n0 + nu):
                    if n + 1 < n0 + nu:
                        soft(n + 1)
                    normalise(n)
                    if (n - n0) in (5, 10, 15):
                        split_to(S_KVQ + 18 * (half + 1) + (n - n0) // 5)
                    if half and (n - n0) in (3, 7, 13):
                        o_lo((3, 7, 13).index(n - n0))
            o_lo(3)
            split_to(S_END)
            residual((S_WO + 1, S_WO + 3))

            dve.wait_ge(res_done, 7)
            norm_scale(3)
            dve.wait_ge(tables_in, 48 + 64)
            for b in range(NB):
                ins = V.scalar_tensor_tensor(h_tok[:, b, :], x[:, b, :], rr[:, b:b + 1], gain_row[:, :], ALU.mult, ALU.mult)
            ins.then_inc(z_done, 1)
            V.memset(ones[:, :], 1.0)
            V.memset(share[:, :, NE:], 0.0)
            step(V.memset(rank[:, :, NE:], 1000.0))
            for q in range(2):
                split_slot(*FIRST_JOB.gate_up(q, 0))
            dve.wait_ge(rt_mm, 1)
            step(V.tensor_copy(logits[:, :, :], acc[:, 0:2, 0:NE]))
            settle()
            for b in range(NB):
                step(V.max(top[:, b, :], logits[:, b, :]))
            settle()
            for b in range(NB):
                step(V.max_index(top_i[:, b, :], top[:, b, :], logits[:, b, :]))
            settle()
            step(V.tensor_copy(top_f[:, :, :], top_i[:, :, :]))
            V.tensor_tensor(gate2[:, :, 0], top[:, :, 1], top[:, :, 0], ALU.subtract).then_inc(rt_v, 1)
            settle()
            for b in range(NB):
                V.tensor_scalar(hot1[:, b, :], iota[:, 0:NE], top_f[:, b, 0:1], None, ALU.is_equal)
                step(V.tensor_scalar(hot2[:, b, :], iota[:, 0:NE], top_f[:, b, 1:2], None, ALU.is_equal))
            settle()
            V.tensor_tensor(chosen[:, :, :], hot1[:, :, :], hot2[:, :, :], ALU.add).then_inc(rt_rank_in, 1)
            dve.wait_ge(rt_e, 1)
            step(V.tensor_scalar(gate2[:, :, 2], gate2[:, :, 1], 1.0, None, ALU.add))
            settle()
            step(V.reciprocal(gate2[:, :, 3], gate2[:, :, 2]))
            settle()
            step(V.tensor_tensor(gate2[:, :, 4], gate2[:, :, 3], gate2[:, :, 1], ALU.mult))
            settle()
            for b in range(NB):
                step(V.tensor_scalar(hot1[:, b, :], hot1[:, b, :], gate2[:, b, 3:4], None, ALU.mult))
            settle()
            for b in range(NB):
                step(V.scalar_tensor_tensor(share[:, b, 0:NE], hot2[:, b, :], gate2[:, b, 4:5], hot1[:, b, :], ALU.mult, ALU.add))
            dve.wait_ge(rt_rank, 1)
            settle()
            step(V.tensor_scalar(hot2[:, :, :], chosen[:, :, :], -1000.0, 1000.0, ALU.mult, ALU.add))
            settle()
            step(V.tensor_tensor(rank[:, :, 0:NE], acc[:, 2, 0:2 * NE].rearrange("p (b e) -> p b e", b=NB), hot2[:, :, :], ALU.add))
            V.tensor_copy(over[:, 7, :], acc[:, 3, 0:NE]).then_inc(rt_counts, 1)
            settle()

            def pick_of(job, value):
                V.tensor_copy(rk_now[:, :].unsqueeze(2), rank[:, :, bass.ds(job, 1)]).then_inc(rk_sem, 1)
                dve.wait_ge(rk_sem, value + 1)
                for b in range(NB):
                    ins = V.tensor_scalar(pick[:, b, :], iota[:, :], rk_now[:, b:b + 1], None, ALU.is_equal)
                ins.then_inc(pick_done, 1)

            def gather_out(job):
                dve.wait_ge(xs_hi_done, job + 1)
                V.tensor_tensor(xs_lo[:, :, :], tb[:, 0:2, :].rearrange("p i (k t) -> p (i k) t", t=P), xs_hi[:, :, :].bitcast(f32), ALU.subtract).then_inc(xs_lo_done, 1)

            pick_of(0, 0)
            gather_out(0)

            def e_mult(job, c):
                jc = job.j * FE_CHUNKS + c + 1
                wait_multiplied(dve, job.gate_up(3, c))
                dve.wait_ge(e_silu, jc + 1)
                dve.wait_ge(et_tr, jc)
                V.tensor_tensor(act_e[:, :], acc[:, 1, :], silu_e[:, :], ALU.mult).then_inc(e_act, 1)

            def act_out(jc, kc):
                dve.wait_ge(et_hi, jc)
                V.tensor_tensor(aet_lo[:, kc, :], tb[:, 2, :].rearrange("p (k t) -> p k t", k=4), aet_hi[:, kc, :].bitcast(f32), ALU.subtract).then_inc(et_lo, 1)

            def take_y(job):
                for s in (1, 3):
                    dve.wait_ge(slab_used[s], job.use[s])
                V.tensor_copy(y_e[:, :], acc[:, 2:4, :].rearrange("p i n -> p (i n)")).then_inc(y_done, 1)

            def add_sum(j):
                dve.wait_ge(sc_mm, j + 1)
                V.tensor_tensor(x[:, :, :].rearrange("p b d -> p (b d)"), x[:, :, :].rearrange("p b d -> p (b d)"),
                                tb[:, :, :].rearrange("p i n -> p (i n)"), ALU.add).then_inc(sum_done, 1)

            def job_rest(job, further=False):
                j = job.j

                def chunk(c, first):
                    jc = j * FE_CHUNKS + c
                    if not first:
                        for q in range(2):
                            split_slot(*job.gate_up(q, c))
                        e_mult(job, c - 1)
                    for q in range(2, 4):
                        split_slot(*job.gate_up(q, c))
                    if first:
                        add_sum(j)
                    else:
                        act_out(jc, bass.ds(c * 4 - 4, 4))

                chunk(0, True)
                with dve.Fori(1, FE_CHUNKS) as c:
                    chunk(c, False)
                V.tensor_copy(sh_now[:, :].unsqueeze(2), share[:, :, bass.ds(j, 1)]).then_inc(sh_sem, 1)
                dve.wait_ge(sh_sem, j + 1)
                dve.wait_ge(pick_done, j + 1)
                for b in range(NB):
                    ins = V.tensor_scalar(put[:, b, :], pick[:, b, :], sh_now[:, b:b + 1], None, ALU.mult)
                ins.then_inc(put_done, 1)
                dve.wait_ge(put_done, j + 1)
                dve.wait_ge(rt_done, 1)
                pick_of(j + 1, j + 1)
                for d in range(FE_KC // 2):
                    split_slot(*job.down(d))
                    if d == 1:
                        e_mult(job, FE_CHUNKS - 1)
                    if d == 3:
                        act_out((j + 1) * FE_CHUNKS, slice(24, 28))
                        gather_out(j + 1)
                after = job.next() if not further else Job(j + 1, 0, job.next().use)
                split_slot(*after.gate_up(0, 0))
                take_y(after)
                split_slot(*after.gate_up(1, 0))

            take_y(FIRST_JOB)
            end = job_loops(dve, job_rest)
            for b in range(NB):
                dve.wait_ge(sc_mm, end.j + (1 + b))
                V.tensor_tensor(x[:, b, :], x[:, b, :], tb[:, 2 * b:2 * b + 2, :].rearrange("p i n -> p (i n)"), ALU.add).then_inc(sum_done, 1)

        return


def kernel(**inputs):
    import concourse.bacc as bacc
    from concourse.bass_utils import run_bass_kernel_spmd

    nc = bacc.Bacc("TRN2", target_bir_lowering=False, num_devices=1)
    arrays = {k: np.ascontiguousarray(v) for k, v in inputs.items()}
    arrays.update(host_constants())
    feed, args = {}, {}
    for name, v in arrays.items():
        feed["in_" + name] = v
        args[name] = nc.dram_tensor("in_" + name, v.shape, mybir.dt.from_np(v.dtype), kind="ExternalInput").ap()
    out = nc.dram_tensor("out_0", (1, SEQ, D), mybir.dt.float32, kind="ExternalOutput").ap()
    build(nc, args, out)
    r = run_bass_kernel_spmd(nc, [feed], core_ids=[0])
    return r.results[0]["out_0"]
```
